# Optimizing a Trainium2 kernel written in Bass

```python
import math
import jax, jax.numpy as jnp
from jax import lax
import numpy as np

D_MODEL = 1024
BATCH = 1
SEQ = 256
DEPTH = 2

GRID_W = 64
CTX_LEN = 256
HEAD_DIM = 64
GROUP_HEADS = 4
GROUP_WIDTH = GROUP_HEADS * HEAD_DIM
N_MIXERS = 4
MIX_WIDTH = N_MIXERS * GROUP_WIDTH
SWA_KV_HEADS = 2
SWA_WINDOW = 128
SWA_BLOCK = 128
MLA_Q_RANK = 256
MLA_KV_RANK = 128
MLA_NOPE = 64
MLA_ROPE = 32
MLA_V = 64
DIFF_QK = 32
DIFF_V = 64
NA_KH = 8
NA_KW = 16
N_GROUPS = 4
EXPERTS_PER_GROUP = 8
N_EXPERTS = N_GROUPS * EXPERTS_PER_GROUP
EXPERT_HIDDEN = 256
TOP_K_IN_GROUP = 2
Q_BLOCK = 128
ROPE_BASE = 10000.0
NORM_EPS = 1e-5
NEG_INF = -1e30
DN_ALPHA = (2 * DEPTH) ** 0.25
DN_BETA = (8 * DEPTH) ** -0.25
SWA_SCALE = HEAD_DIM ** -0.5
MLA_SCALE = (MLA_NOPE + MLA_ROPE) ** -0.5
DIFF_SCALE = DIFF_QK ** -0.5
NA_SCALE = HEAD_DIM ** -0.5
IN_SPLITS = (GROUP_WIDTH, SWA_KV_HEADS * HEAD_DIM, SWA_KV_HEADS * HEAD_DIM,
             MLA_Q_RANK, MLA_KV_RANK, MLA_ROPE,
             GROUP_HEADS * 2 * DIFF_QK, GROUP_HEADS * 2 * DIFF_QK, GROUP_HEADS * DIFF_V,
             GROUP_WIDTH, GROUP_WIDTH, GROUP_WIDTH)
D_IN = sum(IN_SPLITS)
IN_CUTS = tuple(int(v) for v in np.cumsum(IN_SPLITS)[:-1])

kernel_name = 'hymba_style_hybrid_dit_block'

def layer_norm(x, g, b):
    xf = x.astype(jnp.float32)
    mu = jnp.mean(xf, -1, keepdims=True)
    var = jnp.mean(jnp.square(xf - mu), -1, keepdims=True)
    return ((xf - mu) * lax.rsqrt(var + NORM_EPS)).astype(x.dtype) * g + b

def rms_norm(x, g):
    xf = x.astype(jnp.float32)
    return (xf * lax.rsqrt(jnp.mean(xf * xf, -1, keepdims=True) + NORM_EPS)).astype(x.dtype) * g

def rope_1d(x, pos):
    half = x.shape[-1] // 2
    inv = ROPE_BASE ** (-jnp.arange(half, dtype=jnp.float32) / half)
    ang = pos.astype(jnp.float32)[:, None] * inv[None, :]
    bshape = (ang.shape[0],) + (1,) * (x.ndim - 3) + (half,)
    cos = jnp.cos(ang).reshape(bshape).astype(x.dtype)
    sin = jnp.sin(ang).reshape(bshape).astype(x.dtype)
    x1, x2 = x[..., :half], x[..., half:]
    return jnp.concatenate([x1 * cos - x2 * sin, x1 * sin + x2 * cos], -1)

def rope_2d(x, rows, cols):
    r = x.shape[-1] // 2
    return jnp.concatenate([rope_1d(x[..., :r], rows), rope_1d(x[..., r:], cols)], -1)

def attend(q, k, v, scale):
    s = jnp.einsum('bqhd,bkhd->bhqk', q, k).astype(jnp.float32) * scale
    p = jax.nn.softmax(s, axis=-1).astype(v.dtype)
    return jnp.einsum('bhqk,bkhd->bqhd', p, v)

def diff_attend(q1, q2, k1, k2, v, lam, scale):
    a1 = jax.nn.softmax(jnp.einsum('bqhd,bkhd->bhqk', q1, k1).astype(jnp.float32) * scale, axis=-1)
    a2 = jax.nn.softmax(jnp.einsum('bqhd,bkhd->bhqk', q2, k2).astype(jnp.float32) * scale, axis=-1)
    p = (a1 - lam * a2).astype(v.dtype)
    return jnp.einsum('bhqk,bkhd->bqhd', p, v)

def sweep_query_blocks(fn, qs):
    B, L = qs[0].shape[:2]
    nb = L // Q_BLOCK
    blocks = tuple(jnp.moveaxis(q.reshape((B, nb, Q_BLOCK) + q.shape[2:]), 1, 0) for q in qs)
    out = lax.map(lambda a: fn(*a), blocks)
    out = jnp.moveaxis(out, 0, 1)
    return out.reshape((B, L) + out.shape[3:])

def swa_sink_latent(q, k, v, kc, vc, sink):
    B, L, HQ, d = q.shape
    HKV = k.shape[2]
    G = HQ // HKV
    C = kc.shape[1]
    nb = L // SWA_BLOCK
    span = 3 * SWA_BLOCK

    def band(z):
        zp = jnp.pad(z, ((0, 0), (SWA_BLOCK, SWA_BLOCK), (0, 0), (0, 0)))
        zp = zp.reshape(B, nb + 2, SWA_BLOCK, HKV, z.shape[-1])
        return jnp.concatenate([zp[:, :-2], zp[:, 1:-1], zp[:, 2:]], axis=2)

    kb, vb = band(k), band(v)
    qb = q.reshape(B, nb, SWA_BLOCK, HKV, G, d)
    s_band = jnp.einsum('bnqhgd,bnkhd->bnhgqk', qb, kb).astype(jnp.float32) * SWA_SCALE
    s_ctx = jnp.einsum('bnqhgd,bchd->bnhgqc', qb, kc).astype(jnp.float32) * SWA_SCALE
    rel_q = jnp.arange(SWA_BLOCK)[:, None]
    rel_k = jnp.arange(span)[None, :] - SWA_BLOCK
    in_window = jnp.abs(rel_k - rel_q) <= SWA_WINDOW
    k_abs = (jnp.arange(nb) * SWA_BLOCK)[:, None] + rel_k
    in_range = (k_abs >= 0) & (k_abs < L)
    mask = in_window[None] & in_range[:, None, :]
    s_band = jnp.where(mask[None, :, None, None], s_band, NEG_INF)
    sink_logit = jnp.broadcast_to(sink.reshape(HKV, G)[None, None, :, :, None, None].astype(jnp.float32),
                                  s_band.shape[:-1] + (1,))
    p = jax.nn.softmax(jnp.concatenate([s_band, s_ctx, sink_logit], -1), axis=-1)
    p_band = p[..., :span].astype(v.dtype)
    p_ctx = p[..., span:span + C].astype(v.dtype)
    out = (jnp.einsum('bnhgqk,bnkhd->bnqhgd', p_band, vb)
           + jnp.einsum('bnhgqc,bchd->bnqhgd', p_ctx, vc))
    return out.reshape(B, L, HQ * d)

def swa_sink_context(qc, kc, vc, sink):
    B, C, HQ, d = qc.shape
    HKV = kc.shape[2]
    G = HQ // HKV
    qg = qc.reshape(B, C, HKV, G, d)
    s = jnp.einsum('bqhgd,bkhd->bhgqk', qg, kc).astype(jnp.float32) * SWA_SCALE
    sink_logit = jnp.broadcast_to(sink.reshape(HKV, G)[None, :, :, None, None].astype(jnp.float32),
                                  s.shape[:-1] + (1,))
    p = jax.nn.softmax(jnp.concatenate([s, sink_logit], -1), axis=-1)[..., :C].astype(vc.dtype)
    return jnp.einsum('bhgqk,bkhd->bqhgd', p, vc).reshape(B, C, HQ * d)

def neighborhood_latent(q, k, v, kc, vc, rpb):
    B, L, H, d = q.shape
    rows = L // GRID_W
    kh = min(NA_KH, rows)
    qg = q.reshape(B, rows, GRID_W, H, d)
    kg = k.reshape(B, rows, GRID_W, H, d)
    vg = v.reshape(B, rows, GRID_W, H, d)
    col = jnp.arange(GRID_W)
    col_start = jnp.clip(col - NA_KW // 2, 0, GRID_W - NA_KW)
    col_idx = col_start[:, None] + jnp.arange(NA_KW)[None, :]
    col_off = col_idx - col[:, None] + (NA_KW - 1)
    n_win = kh * NA_KW

    def one_row(args):
        r, q_r = args
        r_start = jnp.clip(r - kh // 2, 0, rows - kh)
        k_rows = lax.dynamic_slice_in_dim(kg, r_start, kh, axis=1)
        v_rows = lax.dynamic_slice_in_dim(vg, r_start, kh, axis=1)
        k_win = k_rows[:, :, col_idx]
        v_win = v_rows[:, :, col_idx]
        row_off = r_start + jnp.arange(kh) - r + (NA_KH - 1)
        bias = rpb[:, row_off[None, :, None], col_off[:, None, :]]
        s_win = (jnp.einsum('bqhd,bkqwhd->bhqkw', q_r, k_win).astype(jnp.float32) * NA_SCALE
                 + bias[None].astype(jnp.float32))
        s_ctx = jnp.einsum('bqhd,bchd->bhqc', q_r, kc).astype(jnp.float32) * NA_SCALE
        p = jax.nn.softmax(jnp.concatenate([s_win.reshape(B, H, GRID_W, n_win), s_ctx], -1), axis=-1)
        p_win = p[..., :n_win].reshape(B, H, GRID_W, kh, NA_KW).astype(v.dtype)
        p_ctx = p[..., n_win:].astype(v.dtype)
        return (jnp.einsum('bhqkw,bkqwhd->bqhd', p_win, v_win)
                + jnp.einsum('bhqc,bchd->bqhd', p_ctx, vc))

    out = lax.map(one_row, (jnp.arange(rows, dtype=jnp.int32), jnp.moveaxis(qg, 1, 0)))
    return jnp.moveaxis(out, 0, 1).reshape(B, L, H * d)

def mixing_sublayer(h, hc, w_in, sink, q_norm_g, w_uq, kv_norm_g, w_ukv, lam, lam_init, subln_g,
                    rpb, w_out, need_ctx):
    B, L, _ = h.shape
    C = hc.shape[1]
    t = jnp.arange(L, dtype=jnp.int32)
    rows_pos = t // GRID_W
    cols_pos = t % GRID_W

    def heads(z):
        Bz, N = z.shape[:2]
        p = jnp.split(z @ w_in, IN_CUTS, axis=-1)
        qa = p[0].reshape(Bz, N, GROUP_HEADS, HEAD_DIM)
        ka = p[1].reshape(Bz, N, SWA_KV_HEADS, HEAD_DIM)
        va = p[2].reshape(Bz, N, SWA_KV_HEADS, HEAD_DIM)
        mq = (rms_norm(p[3], q_norm_g) @ w_uq).reshape(Bz, N, GROUP_HEADS, MLA_NOPE + MLA_ROPE)
        mkv = (rms_norm(p[4], kv_norm_g) @ w_ukv).reshape(Bz, N, GROUP_HEADS, MLA_NOPE + MLA_V)
        mkr = p[5].reshape(Bz, N, 1, MLA_ROPE)
        dq = p[6].reshape(Bz, N, GROUP_HEADS, 2, DIFF_QK)
        dk = p[7].reshape(Bz, N, GROUP_HEADS, 2, DIFF_QK)
        dv = p[8].reshape(Bz, N, GROUP_HEADS, DIFF_V)
        nq = p[9].reshape(Bz, N, GROUP_HEADS, HEAD_DIM)
        nk = p[10].reshape(Bz, N, GROUP_HEADS, HEAD_DIM)
        nv = p[11].reshape(Bz, N, GROUP_HEADS, HEAD_DIM)
        return qa, ka, va, mq, mkv, mkr, dq, dk, dv, nq, nk, nv

    def rot(z):
        return rope_2d(z, rows_pos, cols_pos)

    qa, ka, va, mq, mkv, mkr, dq, dk, dv, nq, nk, nv = heads(h)
    qa, ka = rot(qa), rot(ka)
    mq = jnp.concatenate([mq[..., :MLA_NOPE], rot(mq[..., MLA_NOPE:])], -1)
    mk = jnp.concatenate([mkv[..., :MLA_NOPE],
                          jnp.broadcast_to(rot(mkr), (B, L, GROUP_HEADS, MLA_ROPE))], -1)
    mv = mkv[..., MLA_NOPE:]
    dq, dk = rot(dq), rot(dk)

    qa_c, ka_c, va_c, mq_c, mkv_c, mkr_c, dq_c, dk_c, dv_c, nq_c, nk_c, nv_c = heads(hc)
    mk_c = jnp.concatenate([mkv_c[..., :MLA_NOPE],
                            jnp.broadcast_to(mkr_c, (B, C, GROUP_HEADS, MLA_ROPE))], -1)
    mv_c = mkv_c[..., MLA_NOPE:]

    out_a = swa_sink_latent(qa, ka, va, ka_c, va_c, sink)
    mk_all = jnp.concatenate([mk_c, mk], 1)
    mv_all = jnp.concatenate([mv_c, mv], 1)
    out_b = sweep_query_blocks(lambda qb: attend(qb, mk_all, mv_all, MLA_SCALE), (mq,)).reshape(B, L, -1)
    k1_all = jnp.concatenate([dk_c[..., 0, :], dk[..., 0, :]], 1)
    k2_all = jnp.concatenate([dk_c[..., 1, :], dk[..., 1, :]], 1)
    dv_all = jnp.concatenate([dv_c, dv], 1)
    out_c = sweep_query_blocks(
        lambda q1, q2: diff_attend(q1, q2, k1_all, k2_all, dv_all, lam, DIFF_SCALE),
        (dq[..., 0, :], dq[..., 1, :]))
    out_c = (rms_norm(out_c, subln_g) * (1.0 - lam_init)).reshape(B, L, -1)
    out_d = neighborhood_latent(nq, nk, nv, nk_c, nv_c, rpb)
    y = jnp.concatenate([out_a, out_b, out_c, out_d], -1) @ w_out
    if not need_ctx:
        return y, None

    yc_a = swa_sink_context(qa_c, ka_c, va_c, sink)
    yc_b = attend(mq_c, mk_c, mv_c, MLA_SCALE).reshape(B, C, -1)
    yc_c = diff_attend(dq_c[..., 0, :], dq_c[..., 1, :], dk_c[..., 0, :], dk_c[..., 1, :], dv_c, lam, DIFF_SCALE)
    yc_c = (rms_norm(yc_c, subln_g) * (1.0 - lam_init)).reshape(B, C, -1)
    yc_d = attend(nq_c, nk_c, nv_c, NA_SCALE).reshape(B, C, -1)
    yc = jnp.concatenate([yc_a, yc_b, yc_c, yc_d], -1) @ w_out
    return y, yc

def hier_moe(h, w_grp, b_grp, w_rt, b_rt, w_gate, w_up, w_down):
    T = h.shape[0]
    p_grp = jax.nn.softmax((h @ w_grp + b_grp).astype(jnp.float32), axis=-1)
    g_val, g_idx = lax.top_k(p_grp, 1)
    e_logits = (h @ w_rt + b_rt).astype(jnp.float32).reshape(T, N_GROUPS, EXPERTS_PER_GROUP)
    e_sel = jnp.take_along_axis(e_logits, g_idx[:, :, None], axis=1)[:, 0]
    p_exp = jax.nn.softmax(e_sel, axis=-1)
    e_val, e_idx = lax.top_k(p_exp, TOP_K_IN_GROUP)
    e_val = e_val / jnp.sum(e_val, -1, keepdims=True)
    w_exp = jnp.sum(jax.nn.one_hot(e_idx, EXPERTS_PER_GROUP, dtype=jnp.float32) * e_val[..., None], axis=1)
    gates = (jax.nn.one_hot(g_idx[:, 0], N_GROUPS, dtype=jnp.float32)[:, :, None]
             * (g_val * w_exp)[:, None, :]).astype(h.dtype)
    y = jnp.zeros_like(h)
    for g in range(N_GROUPS):
        hid = (jax.nn.silu(jnp.einsum('td,edf->tef', h, w_gate[g]))
               * jnp.einsum('td,edf->tef', h, w_up[g]))
        y = y + jnp.einsum('tef,efd->td', hid * gates[:, g, :, None], w_down[g])
    return y

def setup_inputs(seed: int = 0) -> dict:
    key = jax.random.key(seed)
    ks = jax.random.split(key, 30)

    def nrm(i, shape, scale):
        return jax.random.normal(ks[i], shape, jnp.float32) * scale

    D = D_MODEL
    return {
        'x': nrm(0, (BATCH, SEQ, D), 1.0),
        'c': nrm(1, (BATCH, D), 1.0),
        'ctx': nrm(2, (BATCH, CTX_LEN, D), 1.0),
        'c_ctx': nrm(3, (D,), 1.0),
        'w_mod': nrm(4, (DEPTH, D, 6 * D), 0.5 * D ** -0.5),
        'b_mod': nrm(5, (DEPTH, 6 * D), 0.02),
        'w_in': nrm(6, (DEPTH, D, D_IN), D ** -0.5),
        'attn_sink': nrm(7, (DEPTH, GROUP_HEADS), 0.5),
        'mla_q_norm': 1.0 + nrm(8, (DEPTH, MLA_Q_RANK), 0.02),
        'w_uq': nrm(9, (DEPTH, MLA_Q_RANK, GROUP_HEADS * (MLA_NOPE + MLA_ROPE)), MLA_Q_RANK ** -0.5),
        'mla_kv_norm': 1.0 + nrm(10, (DEPTH, MLA_KV_RANK), 0.02),
        'w_ukv': nrm(11, (DEPTH, MLA_KV_RANK, GROUP_HEADS * (MLA_NOPE + MLA_V)), MLA_KV_RANK ** -0.5),
        'lam_q1': nrm(12, (DEPTH, DIFF_QK), 0.1),
        'lam_k1': nrm(13, (DEPTH, DIFF_QK), 0.1),
        'lam_q2': nrm(14, (DEPTH, DIFF_QK), 0.1),
        'lam_k2': nrm(15, (DEPTH, DIFF_QK), 0.1),
        'diff_subln': 1.0 + nrm(16, (DEPTH, DIFF_V), 0.02),
        'na_rpb': nrm(17, (DEPTH, GROUP_HEADS, 2 * NA_KH - 1, 2 * NA_KW - 1), 0.02),
        'w_out': nrm(18, (DEPTH, MIX_WIDTH, D), MIX_WIDTH ** -0.5 * DN_BETA),
        'ln1_g': 1.0 + nrm(19, (DEPTH, D), 0.02),
        'ln1_b': nrm(20, (DEPTH, D), 0.02),
        'w_group': nrm(21, (DEPTH, D, N_GROUPS), D ** -0.5),
        'b_group': nrm(22, (DEPTH, N_GROUPS), 0.01),
        'w_router': nrm(23, (DEPTH, D, N_EXPERTS), D ** -0.5),
        'b_router': nrm(24, (DEPTH, N_EXPERTS), 0.01),
        'w_gate': nrm(25, (DEPTH, N_GROUPS, EXPERTS_PER_GROUP, D, EXPERT_HIDDEN), D ** -0.5),
        'w_up': nrm(26, (DEPTH, N_GROUPS, EXPERTS_PER_GROUP, D, EXPERT_HIDDEN), D ** -0.5),
        'w_down': nrm(27, (DEPTH, N_GROUPS, EXPERTS_PER_GROUP, EXPERT_HIDDEN, D), EXPERT_HIDDEN ** -0.5 * DN_BETA),
        'ln2_g': 1.0 + nrm(28, (DEPTH, D), 0.02),
        'ln2_b': nrm(29, (DEPTH, D), 0.02),
    }

def reference(x, c, ctx, c_ctx, w_mod, b_mod, w_in, attn_sink, mla_q_norm, w_uq, mla_kv_norm, w_ukv,
              lam_q1, lam_k1, lam_q2, lam_k2, diff_subln, na_rpb, w_out, ln1_g, ln1_b,
              w_group, b_group, w_router, b_router, w_gate, w_up, w_down, ln2_g, ln2_b):
    B, L, D = x.shape
    C = ctx.shape[1]
    xc = ctx
    c_act = jax.nn.silu(c)
    cc_act = jax.nn.silu(c_ctx)
    for l in range(DEPTH):
        need_ctx = l < DEPTH - 1
        mod = c_act @ w_mod[l] + b_mod[l]
        modc = cc_act @ w_mod[l] + b_mod[l]
        sh1, sc1, g1, sh2, sc2, g2 = jnp.split(mod[:, None, :], 6, axis=-1)
        sh1c, sc1c, g1c, sh2c, sc2c, g2c = jnp.split(modc, 6, axis=-1)
        lam_init = 0.8 - 0.6 * math.exp(-0.3 * l)
        lam = (jnp.exp(jnp.sum(lam_q1[l] * lam_k1[l]).astype(jnp.float32))
               - jnp.exp(jnp.sum(lam_q2[l] * lam_k2[l]).astype(jnp.float32)) + lam_init)

        h = x * (1.0 + sc1) + sh1
        hc = xc * (1.0 + sc1c) + sh1c
        y, yc = mixing_sublayer(h, hc, w_in[l], attn_sink[l], mla_q_norm[l], w_uq[l], mla_kv_norm[l],
                                w_ukv[l], lam, lam_init, diff_subln[l], na_rpb[l], w_out[l], need_ctx)
        x = layer_norm(DN_ALPHA * x + g1 * y, ln1_g[l], ln1_b[l])
        h = x * (1.0 + sc2) + sh2

        if need_ctx:
            xc = layer_norm(DN_ALPHA * xc + g1c * yc, ln1_g[l], ln1_b[l])
            hc = xc * (1.0 + sc2c) + sh2c
            tokens = jnp.concatenate([h.reshape(-1, D), hc.reshape(-1, D)], 0)
            f = hier_moe(tokens, w_group[l], b_group[l], w_router[l], b_router[l],
                         w_gate[l], w_up[l], w_down[l])
            f_lat = f[:B * L].reshape(B, L, D)
            f_ctx = f[B * L:].reshape(B, C, D)
            xc = layer_norm(DN_ALPHA * xc + g2c * f_ctx, ln2_g[l], ln2_b[l])
        else:
            f_lat = hier_moe(h.reshape(-1, D), w_group[l], b_group[l], w_router[l], b_router[l],
                             w_gate[l], w_up[l], w_down[l]).reshape(B, L, D)
        x = layer_norm(DN_ALPHA * x + g2 * f_lat, ln2_g[l], ln2_b[l])
    return x


_drawn_inputs = setup_inputs


def setup_inputs(seed=0):
    import zlib

    import numpy as np

    out = dict(_drawn_inputs(seed))
    spreads = {}
    factors = {'b_mod': 5.835,
     'attn_sink': 64.0,
     'mla_q_norm': 8.0,
     'w_uq': 6.65,
     'mla_kv_norm': 8.0,
     'w_ukv': 3.053,
     'lam_q1': 8.0,
     'lam_k1': 8.0,
     'lam_q2': 8.0,
     'lam_k2': 8.0,
     'diff_subln': 8.0,
     'na_rpb': 47.219,
     'b_group': 8.0,
     'b_router': 8.0}
    for name, (base, spread) in spreads.items():
        noise = np.random.default_rng([zlib.crc32(name.encode()), seed]).standard_normal(out[name].shape)
        drawn = base * np.exp(spread * noise) if base else spread * noise
        out[name] = __import__('jax').numpy.asarray(drawn.astype(out[name].dtype))
    for name, factor in factors.items():
        out[name] = (out[name] * factor).astype(out[name].dtype)
    return out
```

```python
import math
from contextlib import ExitStack

import concourse.bass as bass
from concourse import mybir

P = 128
D = 1024
KD = D // P
SEQ = 256
CTX = 256
TOK = SEQ + CTX
DEPTH = 2
D_IN = 2464
GRID_W = 64
NE = 32
FH = 256
ALPHA = (2 * DEPTH) ** 0.25
EPS = 1e-5
NEG = -1e30

F32 = mybir.dt.float32
ALU = mybir.AluOpType
ACT = mybir.ActivationFunctionType
AX = mybir.AxisListType.X

C_ID, C_P16, C_P8, C_BLK = 0, 128, 256, 384
C_COS64, C_SIN64, C_COS32, C_SIN32 = 512, 768, 1024, 1280
C_SWA, C_NA = 1536, 2048
C_IOTA = 2560
C_ALL = C_IOTA + 16

V_MOD, V_LN1G, V_LN1B, V_LN2G, V_LN2B, V_QN, V_KVN, V_SUB, V_C, V_CC = 0, 48, 56, 64, 72, 80, 82, 83, 84, 92
R_SINK, R_LAM, R_RB = 0, 4, 132
R_ALL = 168
SH1, SC1, G1, SH2, SC2, G2 = 0, 8, 16, 24, 32, 40

MOD_COLS = 768
MOD_J = MOD_COLS // P
IN_PARTS = [(0, 512), (512, 416), (928, 768), (1696, 768)]
SLOT = 6144
SLOTS = 3


def load_plan():
    plan = [("mod", 0, c) for c in range(3)] + [("in", 0, c) for c in range(4)]
    plan += [("mod", 0, c) for c in range(3, 8)] + [("mod", 1, c) for c in range(8)]
    plan += [("out", 0, c) for c in range(2)] + [("exp", 0, e) for e in range(NE)]
    plan += [("in", 1, c) for c in range(4)] + [("out", 1, c) for c in range(2)] + [("exp", 1, e) for e in range(NE)]
    return plan


PLAN = load_plan()
INDEX = {w: i for i, w in enumerate(PLAN)}
DMAS = {"mod": 1, "in": 1, "out": 1, "exp": 3}


def arrival(i):
    return i % SLOTS, 16 * sum(DMAS[PLAN[j][0]] for j in range(i % SLOTS, i + 1, SLOTS))


def attention_units(l):
    out = []
    for mixer in "cabd":
        for h in range(4):
            for qt in range(4 if l == 0 else 2):
                out.append((mixer, h, qt, 0 if qt < 2 else 2))
    return out


GROUPS = [
    ("qa", 0), ("qa", 1), ("ka", 0), ("va", 0),
    ("pq", 0), ("pq", 1), ("pkv", 0), ("kr", 0),
    ("qd", 0), ("qd", 1), ("kd", 0), ("kd", 1), ("vd", 0), ("vd", 1),
    ("ssq", 0), ("sskv", 0),
    ("qn", 0), ("qn", 1), ("kn", 0), ("kn", 1), ("vn", 0), ("vn", 1),
    ("mk", 0), ("mk", 1), ("mk", 2), ("mk", 3), ("mv", 0), ("mv", 1),
    ("mq", 0), ("mq", 1), ("mq", 2), ("mq", 3),
]
ROPED = ("qa", "ka", "kr", "qd", "kd", "mq")
BY_ACT = ROPED + ("ssq", "sskv", "qn")
LAST_OF_PART = {("va", 0): 0, ("kr", 0): 1, ("vd", 1): 2, ("vn", 1): 3}
PART_OF = {"qa": 0, "ka": 0, "va": 0, "pq": 1, "pkv": 1, "kr": 1, "qd": 2, "kd": 2, "vd": 2, "qn": 3, "kn": 3, "vn": 3}
NACT = [sum(n in BY_ACT for n, _ in GROUPS[:g + 1]) for g in range(len(GROUPS))]
NDVE = [sum(n not in BY_ACT for n, _ in GROUPS[:g + 1]) for g in range(len(GROUPS))]
ROPES = [g for g, (n, _) in enumerate(GROUPS) if n in ROPED]
GI = {g: i for i, g in enumerate(GROUPS)}
SCALE = {"qa": 64 ** -0.5, "ka": 1.0, "kr": 1.0, "qd": 32 ** -0.5, "kd": 1.0, "mq": 96 ** -0.5, "qn": 64 ** -0.5}
PROJ_BANKS = 4


def build(nc, x, ctx_in, w_mod, w_in, w_uq, w_ukv, w_out, w_route, w_gate, w_up, w_down, vecs, rows, bias_na, consts, out):
    with ExitStack() as st:
        def sb(name, shape):
            return st.enter_context(nc.sbuf_tensor(name, shape, F32))

        def sem(name):
            return st.enter_context(nc.semaphore(name))

        def per_layer(name):
            return [sem(f"{name}_{l}") for l in range(DEPTH)]

        xT = sb("xT", [P, KD, TOK])
        hT = sb("hT", [P, KD, TOK])
        attnT = hT
        zbuf = sb("zbuf", [P, KD * TOK])
        zT = zbuf[:, :].rearrange("p (k t) -> p k t", k=KD)
        xin = zbuf[:, :].rearrange("p (a d) -> p a d", a=4)
        slots = sb("slots", [P, SLOTS, SLOT])
        QA = sb("QA", [P, 2, TOK])
        KA = sb("KA", [P, TOK])
        QM = sb("QM", [P, 4, TOK])
        KM = sb("KM", [P, 4, TOK])
        QDf = sb("QDf", [P, 2, TOK])
        KDf = sb("KDf", [P, 2, TOK])
        QN = sb("QN", [P, 2, TOK])
        KN = sb("KN", [P, 2, TOK])
        V = sb("V", [P, 4, 896])
        VOFF = {"a": 0, "c": 128, "d": 384, "b": 640}
        cst = sb("cst", [P, C_ALL])
        biasm = sb("biasm", [P, 4, 2, SEQ])
        ropet = sb("ropet", [P, 2, SEQ])
        wuq = sb("wuq", [P, 2, 384])
        wukv = sb("wukv", [P, 512])
        wr = sb("wr", [P, DEPTH, KD, 36])
        colv = sb("colv", [P, DEPTH, P])
        rowv = sb("rowv", [P, DEPTH, R_ALL])
        cT = sb("cT", [P, 2, KD])
        modT = sb("modT", [P, DEPTH, 48, 2])
        modT1 = sb("modT1", [P, DEPTH, 48, 2])
        onesD = sb("onesD", [P, P])
        ones = sb("ones", [P, P])
        epst = sb("epst", [P, 1])
        nlam = sb("nlam", [P, DEPTH])
        nsink = sb("nsink", [P, DEPTH, 4])
        lamt = sb("lamt", [P, 2, 32])
        lams = sb("lams", [P, 4])
        subg = sb("subg", [P, DEPTH])
        nmx = sb("nmx", [P, 80])
        rsum = sb("rsum", [P, 80])
        rinv = sb("rinv", [P, 80])
        esk = sb("esk", [P, 80])
        vrow = QA[:, 0, 0:DEPTH * P].rearrange("p (l n) -> p l n", l=DEPTH)
        sqr = QDf
        rstd = KA
        sg, hid = QM[:, 0:2, :], QM[:, 2:4, :]
        gT, gbc = QA[0:NE, 0, :], QA[:, 1, :]
        rt = KM[:, 0:2, :].rearrange("p a (b n) -> p (a b) n", b=2)
        lg = KM[:, 2, 0:144].rearrange("p (t n) -> p t n", t=4)
        gates = KM[:, 3, 0:128].rearrange("p (t n) -> p t n", t=4)
        praw = zT[:, 0:3, :]
        psq = zT[:, 3:6, :]
        prstd = zT[:, 6:8, :]
        Pr = zT[:, 0:4, :]
        PTs = zT[:, 4:6, :]
        diag = zT[:, 6, :].rearrange("p (a b) -> p a b", a=4)
        yT = zT
        ident = cst[:, C_ID:C_ID + P]

        bank = [st.enter_context(nc.psum_tensor(f"bank{i}", [P, 512], F32)) for i in range(8)]

        w_here = [sem(f"w_here{i}") for i in range(SLOTS)]
        s_small = sem("s_small")
        s_xin = sem("s_xin")
        s_wqkv = per_layer("s_wqkv")
        s_bias = per_layer("s_bias")
        s_biasm = per_layer("s_biasm")
        s_ones = sem("s_ones")
        s_vt = sem("s_vt")
        s_colv = sem("s_colv")
        s_cT = sem("s_cT")
        s_lamp = sem("s_lamp")
        s_lame = sem("s_lame")
        s_tp = sem("s_tp")
        s_xT = sem("s_xT")
        s_mod = sem("s_mod")
        s_modT = sem("s_modT")
        s_h1a = per_layer("s_h1a")
        s_h1d = per_layer("s_h1d")
        s_grp = per_layer("s_grp")
        s_eva = per_layer("s_eva")
        s_evd = per_layer("s_evd")
        s_perm = per_layer("s_perm")
        s_rope = per_layer("s_rope")
        s_psq = per_layer("s_psq")
        s_prstd = per_layer("s_prstd")
        s_pn = per_layer("s_pn")
        s_S = per_layer("s_S")
        s_nm = per_layer("s_nm")
        s_exp = per_layer("s_exp")
        s_dg = per_layer("s_dg")
        s_T = per_layer("s_T")
        s_PT = per_layer("s_PT")
        s_O = per_layer("s_O")
        s_att = per_layer("s_att")
        s_csq = per_layer("s_csq")
        s_css = per_layer("s_css")
        s_cstd = per_layer("s_cstd")
        s_cn = per_layer("s_cn")
        s_y = per_layer("s_y")
        s_yg = per_layer("s_yg")
        LN = [[{n: sem(f"ln{l}{w}_{n}") for n in ("z", "mean", "cent", "sq", "sqs", "std", "zn", "x")} for w in range(2)] for l in range(DEPTH)]
        s_h2d = per_layer("s_h2d")
        s_h2p = per_layer("s_h2p")
        s_lg = per_layer("s_lg")
        s_rexp = per_layer("s_rexp")
        s_rexpd = per_layer("s_rexpd")
        s_gates = per_layer("s_gates")
        s_gT = per_layer("s_gT")
        s_gTs = per_layer("s_gTs")
        s_bc = per_layer("s_bc")
        s_bcs = per_layer("s_bcs")
        s_hg = per_layer("s_hg")
        s_sg = per_layer("s_sg")
        s_hid = per_layer("s_hid")
        s_dn = per_layer("s_dn")
        s_ya = per_layer("s_ya")
        s_ot = sem("s_ot")
        s_oe = sem("s_oe")
        s_out = sem("s_out")
        s_dch = sem("s_dch")
        s_ach = sem("s_ach")

        block = st.enter_context(nc.Block())

        units = [attention_units(l) for l in range(DEPTH)]
        first = []
        for l in range(DEPTH):
            f = [0]
            for u in units[l]:
                f.append(f[-1] + (2 if u[0] == "c" else 1))
            first.append(f)
        TQ = [TOK, SEQ]

        def dest(name, i):
            return {"qa": lambda: QA[:, i, :], "ka": lambda: KA[:, :], "qd": lambda: QDf[:, i, :], "kd": lambda: KDf[:, i, :],
                    "qn": lambda: QN[:, i, :], "kn": lambda: KN[:, i, :], "mq": lambda: QM[:, i, :],
                    "kr": lambda: KM[:, 0, :]}[name]()

        def width(l, name):
            return TQ[l] if name in ("qa", "qd", "qn", "mq", "ssq") or name == "pq" else TOK

        def released(i):
            kind, l, c = PLAN[i]
            if kind == "mod":
                return s_mod, 8 * l + c + 1
            if kind == "in":
                return s_grp[l], GI[[g for g, p in LAST_OF_PART.items() if p == c][0]] + 1
            if kind == "out":
                return s_y[l], 4 * (c + 1)
            return s_dn[l], KD * (c + 1)

        def mod_bank(i):
            return bank[6 + i % 2] if i < 3 else bank[7]

        @block.sync
        def _(sp):
            sp.dma_start(xin[:, 0:2, :], x.rearrange("o (a p) d -> p (o a) d", p=P)).then_inc(s_xin, 16)
            sp.dma_start(xin[:, 2:4, :], ctx_in.rearrange("o (a p) d -> p (o a) d", p=P)).then_inc(s_xin, 16)
            for i, (kind, l, c) in enumerate(PLAN):
                slot = slots[:, i % SLOTS, :]
                here = w_here[i % SLOTS]
                if i >= SLOTS:
                    sp.wait_ge(*released(i - SLOTS))
                if kind == "mod":
                    sp.dma_start(slot.rearrange("p (k n) -> p k n", k=KD),
                                 w_mod[l].rearrange("(k p) n -> p k n", p=P)[:, :, c * MOD_COLS:(c + 1) * MOD_COLS]).then_inc(here, 16)
                elif kind == "in":
                    o, n = IN_PARTS[c]
                    sp.dma_start(slot[:, 0:KD * n].rearrange("p (k n) -> p k n", k=KD),
                                 w_in[l].rearrange("(k p) n -> p k n", p=P)[:, :, o:o + n]).then_inc(here, 16)
                elif kind == "out":
                    sp.dma_start(slot[:, 0:KD * 512].rearrange("p (k n) -> p k n", k=KD),
                                 w_out[l].rearrange("(k p) n -> p k n", p=P)[:, :, c * 512:(c + 1) * 512]).then_inc(here, 16)
                else:
                    for j, w in enumerate((w_gate, w_up)):
                        sp.dma_start(slot[:, j * 2048:(j + 1) * 2048].rearrange("p (k f) -> p k f", k=KD),
                                     w[l, c // 8, c % 8].rearrange("(k p) f -> p k f", p=P)).then_inc(here, 16)
                    sp.dma_start(slot[:, 4096:6144].rearrange("p (k d) -> p k d", k=2),
                                 w_down[l, c // 8, c % 8].rearrange("(k p) d -> p k d", p=P)).then_inc(here, 16)
            for t in range(2):
                sp.wait_ge(s_oe, 4 * (t + 1))
                sp.dma_start(out[0, t * P:(t + 1) * P, :], xin[:, t, :]).then_inc(s_out, 16)
            sp.wait_ge(s_out, 32)

        @block.gpsimd
        def _(pool):
            nc.gpsimd.memset(onesD[:, :], 1.0 / D)
            nc.gpsimd.memset(epst[:, :], EPS)
            nc.gpsimd.memset(ones[:, :], 1.0).then_inc(s_ones, 1)
            pool.wait_ge(s_small, 16 * 4)
            for l in range(DEPTH):
                if l >= 1:
                    pool.wait_ge(s_S[l - 1], first[l - 1][-1])
                pool.wait_ge(s_bias[l], 16)
                for h in range(4):
                    nc.gpsimd.tensor_tensor(biasm[:, h, :, :], biasm[:, h, :, :],
                                            cst[:, C_NA:C_NA + 512].rearrange("p (a k) -> p a k", a=2), ALU.add).then_inc(s_biasm[l], 1)
                if TQ[l] > SEQ:
                    for m in range(KD):
                        pool.wait_ge(LN[l][0]["x"], m + 1)
                        nc.gpsimd.tensor_scalar(hT[:, m, SEQ:TOK], xT[:, m, SEQ:TOK], modT1[:, l, SC2 + m, 1:2],
                                                modT[:, l, SH2 + m, 1:2], ALU.mult, ALU.add).then_inc(s_h2p[l], 1)

        @block.scalar
        def _(act):
            chain = [0]

            def link(ins):
                chain[0] += 1
                ins.then_inc(s_ach, 1)
                act.wait_ge(s_ach, chain[0])

            act.dma_start(cst[:, :], consts[:, :]).then_inc(s_small, 16)
            act.dma_start(vrow[:, :, :], vecs.rearrange("l p n -> p l n")).then_inc(s_small, 16)
            act.dma_start(rowv[:, :, :], rows.rearrange("l p n -> p l n")).then_inc(s_small, 16)
            act.dma_start(wr[:, :, :, :].rearrange("p l k n -> p (l k) n"),
                          w_route.rearrange("l (k p) n -> p (l k) n", p=P)).then_inc(s_small, 16)

            def small_weights(l):
                act.dma_start(wuq[:, :, :], w_uq[l].rearrange("(k p) n -> p k n", p=P)).then_inc(s_wqkv[l], 16)
                act.dma_start(wukv[:, :], w_ukv[l]).then_inc(s_wqkv[l], 16)

            def small_bias(l):
                act.dma_start(biasm[:, :, :, :].rearrange("p h a k -> p (h a) k"),
                              bias_na[l].rearrange("h (a p) k -> p (h a) k", p=P)).then_inc(s_bias[l], 16)

            small_weights(0)
            small_bias(0)
            act.wait_ge(s_colv, 1)
            act.activation(cT[:, :, :].rearrange("p a k -> p (a k)"), colv[:, 0, V_C:V_C + 16], ACT.Silu).then_inc(s_cT, 1)
            act.wait_ge(s_lamp, 2)
            act.activation(lams[:, 0:4], lams[:, 0:4], ACT.Exp).then_inc(s_lame, 1)

            def layer_norm_act(l, w):
                s = LN[l][w]
                n = TQ[l]
                for m in range(KD):
                    act.wait_ge(s["cent"], m + 1)
                    if m >= 2:
                        act.wait_ge(s["sqs"], m - 1)
                    act.activation(sqr[:, m % 2, 0:n], zT[:, m, 0:n], ACT.Square).then_inc(s["sq"], 1)
                act.wait_ge(s["sqs"], KD)
                act.activation(rstd[:, 0:n], bank[5][:, 0:n], ACT.Sqrt, bias=epst[:, 0:1], scale=1.0 / D).then_inc(s["std"], 1)
                g, b = (V_LN1G, V_LN1B) if w == 0 else (V_LN2G, V_LN2B)
                for m in range(KD):
                    act.wait_ge(s["zn"], m + 1)
                    act.activation(xT[:, m, 0:n], zT[:, m, 0:n], ACT.Identity, bias=colv[:, l, b + m:b + m + 1],
                                   scale=colv[:, l, g + m:g + m + 1]).then_inc(s["x"], 1)

            def gated(l, m, src, chunk):
                ins = act.activation(zT[:, m, 0:SEQ], src[:, 0:SEQ], ACT.Copy, scale=modT[:, l, chunk + m, 0:1])
                if TQ[l] > SEQ:
                    ins = act.activation(zT[:, m, SEQ:TOK], src[:, SEQ:TOK], ACT.Copy, scale=modT[:, l, chunk + m, 1:2])
                return ins

            for l in range(DEPTH):
                n = TQ[l]
                act.wait_ge(s_modT, 3 if l == 0 else 16)
                if l == 0:
                    act.wait_ge(s_xT, KD)
                    act.wait_ge(s_ones, 1)
                else:
                    act.wait_ge(LN[l - 1][1]["x"], KD)
                for m in range(KD):
                    act.activation(hT[:, m, SEQ:TOK], xT[:, m, SEQ:TOK], ACT.Identity, bias=modT[:, l, SH1 + m, 1:2],
                                   scale=modT1[:, l, SC1 + m, 1:2]).then_inc(s_h1a[l], 1)
                for g, (name, i) in enumerate(GROUPS):
                    if (name, i) == ("vd", 0):
                        for j in range(3):
                            act.wait_ge(s_evd[l], NDVE[GI[("pkv", 0)] if j == 2 else GI[("pq", j)]])
                            nn = width(l, "pq") if j < 2 else TOK
                            act.activation(psq[:, j, 0:nn], praw[:, j, 0:nn], ACT.Square).then_inc(s_psq[l], 1)
                    if name not in BY_ACT:
                        continue
                    act.wait_ge(s_grp[l], g + 1)
                    w = width(l, name)
                    src = bank[g % PROJ_BANKS]
                    if name == "ssq":
                        act.activation(prstd[:, 0, 0:w], src[:, 0:w], ACT.Sqrt, bias=epst[:, 0:1], scale=1.0 / 256).then_inc(s_eva[l], 1)
                    elif name == "sskv":
                        act.activation(prstd[:, 1, 0:w], src[:, 0:w], ACT.Sqrt, bias=epst[:, 0:1], scale=1.0 / 128).then_inc(s_eva[l], 1)
                    else:
                        lo, hi = (64, 96) if name == "kr" else (0, 96) if name == "mq" else (0, 128)
                        act.activation(dest(name, i)[lo:hi, 0:w], src[lo:hi, 0:w], ACT.Copy, scale=SCALE[name]).then_inc(s_eva[l], 1)
                uf = first[l]
                vof = [v for v in range(len(units[l])) for _ in range(uf[v + 1] - uf[v])]
                act.wait_ge(s_grp[l], len(GROUPS))
                for v in range(len(units[l]) + 2):
                    if v < len(units[l]):
                        mixer, h, qt, k0 = units[l][v]
                        for u in range(uf[v], uf[v + 1]):
                            act.wait_ge(s_nm[l], u + 1)
                            if u >= 4:
                                act.wait_ge(s_T[l], vof[u - 4] + 1)
                            if mixer == "a":
                                act.activation(esk[:, u:u + 1], rowv[:, l, R_SINK + h:R_SINK + h + 1], ACT.Exp, bias=nmx[:, u:u + 1])
                            act.activation(Pr[:, u % 4, k0 * P:TOK], bank[u % 3][:, k0 * P:TOK], ACT.Exp, bias=nmx[:, u:u + 1],
                                           accum_out=rsum[:, u:u + 1]).then_inc(s_exp[l], 1)
                    if v >= 2:
                        t = v - 2
                        k0 = units[l][t][3]
                        act.wait_ge(s_T[l], t + 1)
                        if t >= 2:
                            act.wait_ge(s_O[l], t - 1)
                        act.activation(PTs[:, t % 2, k0 * P:TOK], bank[3 + t % 2][:, k0 * P:TOK], ACT.Copy).then_inc(s_PT[l], 1)
                if l + 1 < DEPTH:
                    small_weights(l + 1)
                    act.wait_ge(s_S[l], uf[-1])
                    small_bias(l + 1)
                act.wait_ge(s_att[l], len(units[l]))
                for j in range(2):
                    act.activation(sqr[:, j, 0:n], attnT[:, 4 + j, 0:n], ACT.Square).then_inc(s_csq[l], 1)
                for j in range(2):
                    act.wait_ge(s_css[l], j + 1)
                    act.activation(sqr[:, j, 0:n], bank[j][:, 0:n], ACT.Sqrt, bias=epst[:, 0:1]).then_inc(s_cstd[l], 1)
                act.wait_ge(s_modT, 16)
                for m in range(KD):
                    act.wait_ge(s_y[l], m + 1)
                    gated(l, m, bank[m % 4], G1).then_inc(s_yg[l], 1)
                layer_norm_act(l, 0)
                for j in range(2):
                    act.wait_ge(s_rexp[l], j + 1)
                    nn = n // P
                    if j == 0:
                        act.activation(rt[:, 0:nn, 0:4], rt[:, 0:nn, 0:4], ACT.Exp).then_inc(s_rexpd[l], 1)
                    else:
                        act.activation(rt[:, 0:nn, 100:101], rt[:, 0:nn, 100:101], ACT.Exp).then_inc(s_rexpd[l], 1)
                for e in range(NE):
                    act.wait_ge(s_bc[l], e + 1)
                    if e >= 1:
                        act.wait_ge(s_hid[l], 2 * e)
                    act.activation(gbc[:, 0:n], bank[4][:, 0:n], ACT.Copy).then_inc(s_bcs[l], 1)
                    for f in range(2):
                        act.wait_ge(s_hg[l], 2 * e + f + 1)
                        act.activation(sg[:, f, 0:n], bank[f][:, 0:n], ACT.Silu).then_inc(s_sg[l], 1)
                act.wait_ge(s_ya[l], NE * KD)
                for m in range(KD):
                    gated(l, m, zT[:, m, :], G2).then_inc(s_yg[l], 1)
                layer_norm_act(l, 1)

        @block.vector
        def _(dve):
            chain = [0]

            def link(ins):
                chain[0] += 1
                ins.then_inc(s_dch, 1)
                dve.wait_ge(s_dch, chain[0])

            vec = nc.vector
            for l in range(DEPTH):
                dve.wait_ge(s_vt, l + 1)
                vec.tensor_copy(colv[:, l, :], bank[l][:, 0:P]).then_inc(s_colv, 1)
            dve.wait_ge(s_small, 64)
            for l in range(DEPTH):
                lam = rowv[:, l, R_LAM:R_LAM + 128].rearrange("p (a b n) -> p a b n", a=2, b=2)
                link(vec.tensor_tensor(lamt[:, :, :], lam[:, :, 0, :], lam[:, :, 1, :], ALU.mult))
                vec.tensor_reduce(lams[:, 2 * l:2 * l + 2], lamt[:, :, :], AX, ALU.add).then_inc(s_lamp, 1)
                dve.wait_ge(s_lamp, l + 1)
                vec.tensor_scalar(nsink[:, l, :], rowv[:, l, R_SINK:R_SINK + 4], -1.0, None, ALU.mult)
            dve.wait_ge(s_lame, 1)
            dve.wait_ge(s_colv, 2)
            for l in range(DEPTH):
                lam_init = 0.8 - 0.6 * math.exp(-0.3 * l)
                link(vec.tensor_tensor(nlam[:, l:l + 1], lams[:, 2 * l + 1:2 * l + 2], lams[:, 2 * l:2 * l + 1], ALU.subtract))
                link(vec.tensor_scalar(nlam[:, l:l + 1], nlam[:, l:l + 1], -lam_init, None, ALU.add))
                link(vec.tensor_scalar(subg[:, l:l + 1], colv[:, l, V_SUB:V_SUB + 1], 1.0 - lam_init, None, ALU.mult))
            for k in range(KD):
                dve.wait_ge(s_tp, k + 1)
                vec.tensor_copy(xT[:, k, :], bank[2 + k % 2][:, :]).then_inc(s_xT, 1)

            def mod_columns(l, c):
                dve.wait_ge(s_mod, 8 * l + c + 1)
                src = mod_bank(8 * l + c)[:, 0:2 * MOD_J].rearrange("p (j a) -> p j a", a=2)
                cols = slice(c * MOD_J, (c + 1) * MOD_J)
                for a in range(2):
                    vec.tensor_tensor(modT[:, l, cols, a], src[:, :, a], colv[:, l, cols], ALU.add)
                    ins = vec.scalar_tensor_tensor(modT1[:, l, cols, a], src[:, :, a], 1.0, colv[:, l, cols], ALU.add, ALU.add)
                ins.then_inc(s_modT, 1)

            for c in range(3):
                mod_columns(0, c)

            def layer_norm_dve(l, w):
                s = LN[l][w]
                n = TQ[l]
                for m in range(KD):
                    dve.wait_ge(s_yg[l], KD * w + m + 1)
                    vec.scalar_tensor_tensor(zT[:, m, 0:n], xT[:, m, 0:n], ALPHA, zT[:, m, 0:n], ALU.mult, ALU.add).then_inc(s["z"], 1)
                dve.wait_ge(s["mean"], 1)
                for m in range(KD):
                    dve.wait_ge(s["z"], m + 1)
                    vec.tensor_tensor(zT[:, m, 0:n], zT[:, m, 0:n], bank[4][:, 0:n], ALU.subtract).then_inc(s["cent"], 1)
                dve.wait_ge(s["std"], 1)
                link(vec.reciprocal(rstd[:, 0:n], rstd[:, 0:n]))
                for m in range(KD):
                    vec.tensor_tensor(zT[:, m, 0:n], zT[:, m, 0:n], rstd[:, 0:n], ALU.mult).then_inc(s["zn"], 1)

            for l in range(DEPTH):
                n = TQ[l]
                nt = n // P
                if l == 0:
                    dve.wait_ge(s_xT, KD)
                    dve.wait_ge(s_modT, 3)
                else:
                    dve.wait_ge(LN[l - 1][1]["x"], KD)
                for m in range(KD):
                    vec.tensor_scalar(hT[:, m, 0:SEQ], xT[:, m, 0:SEQ], modT1[:, l, SC1 + m, 0:1],
                                      modT[:, l, SH1 + m, 0:1], ALU.mult, ALU.add).then_inc(s_h1d[l], 1)

                def rope(r):
                    g = ROPES[r]
                    name, i = GROUPS[g]
                    lo, hi = (64, 96) if name in ("kr", "mq") else (0, 128)
                    cos, sin = (C_COS64, C_SIN64) if name in ("qa", "ka") else (C_COS32, C_SIN32)
                    d = dest(name, i)[lo:hi, 0:SEQ]
                    dve.wait_ge(s_perm[l], r + 1)
                    vec.tensor_tensor(ropet[lo:hi, r % 2, :], bank[4 + r % 2][lo:hi, 0:SEQ], cst[lo:hi, sin:sin + SEQ], ALU.mult)
                    link(vec.tensor_tensor(d, d, cst[lo:hi, cos:cos + SEQ], ALU.mult))
                    vec.tensor_tensor(d, d, ropet[lo:hi, r % 2, :], ALU.add).then_inc(s_rope[l], 1)
                    if name == "kr":
                        dve.wait_ge(s_rope[l], r + 1)
                        for h in range(1, 4):
                            vec.tensor_copy(KM[64:96, h, :], KM[64:96, 0, :])

                done = 0
                for g, (name, i) in enumerate(GROUPS):
                    if (name, i) == ("mk", 0):
                        for j in range(2):
                            w = TOK if j else n
                            dve.wait_ge(s_eva[l], NACT[GI[("sskv" if j else "ssq", 0)]])
                            link(vec.reciprocal(prstd[:, j, 0:w], prstd[:, j, 0:w]))
                        for j in range(3):
                            w = TOK if j == 2 else n
                            col = V_KVN if j == 2 else V_QN + j
                            vec.scalar_tensor_tensor(praw[:, j, 0:w], praw[:, j, 0:w], colv[:, l, col:col + 1],
                                                     prstd[:, 1 if j == 2 else 0, 0:w], ALU.mult, ALU.mult).then_inc(s_pn[l], 1)
                    if name not in BY_ACT:
                        dve.wait_ge(s_grp[l], g + 1)
                        src = bank[g % PROJ_BANKS]
                        if name == "va":
                            ins = vec.tensor_copy(V[:, :, 0:P], src[:, :].rearrange("p (t c) -> p t c", t=4))
                        elif name in ("vd", "vn", "mv"):
                            o = VOFF[{"vd": "c", "vn": "d", "mv": "b"}[name]]
                            ins = vec.tensor_copy(V[:, 2 * i:2 * i + 2, o:o + 256], src[:, :].rearrange("p (t c) -> p t c", t=2))
                        elif name in ("pq", "pkv"):
                            w = width(l, name)
                            ins = vec.tensor_copy(praw[:, i if name == "pq" else 2, 0:w], src[:, 0:w])
                        elif name == "mk":
                            ins = vec.tensor_copy(KM[0:64, i, :], src[0:64, :])
                        else:
                            ins = vec.tensor_copy(dest(name, i), src[:, :])
                        ins.then_inc(s_evd[l], 1)
                    while done < len(ROPES) and ROPES[done] + 2 <= g:
                        rope(done)
                        done += 1
                while done < len(ROPES):
                    rope(done)
                    done += 1

                uf = first[l]
                vof = [v for v in range(len(units[l])) for _ in range(uf[v + 1] - uf[v])]
                mods = [(0, c) for c in range(3, 8)] + [(1, c) for c in range(8)] if l == 0 else []
                for v in range(len(units[l]) + 3):
                    if v < len(units[l]):
                        mixer, h, qt, k0 = units[l][v]
                        for u in range(uf[v], uf[v + 1]):
                            dve.wait_ge(s_S[l], u + 1)
                            ins = vec.tensor_reduce(nmx[:, u:u + 1], bank[u % 3][:, k0 * P:TOK], AX, ALU.max, negate=True)
                            if mixer == "a":
                                link(ins)
                                ins = vec.tensor_tensor(nmx[:, u:u + 1], nmx[:, u:u + 1], nsink[:, l, h:h + 1], ALU.min)
                            ins.then_inc(s_nm[l], 1)
                    if 1 <= v <= len(units[l]):
                        mixer, h, qt, k0 = units[l][v - 1]
                        for u in range(uf[v - 1], uf[v]):
                            dve.wait_ge(s_exp[l], u + 1)
                            if mixer == "a":
                                link(vec.tensor_tensor(rsum[:, u:u + 1], rsum[:, u:u + 1], esk[:, u:u + 1], ALU.add))
                            link(vec.reciprocal(rinv[:, u:u + 1], rsum[:, u:u + 1]))
                            if u >= 4:
                                dve.wait_ge(s_T[l], vof[u - 4] + 1)
                            if mixer == "c" and u == uf[v] - 1:
                                ins = vec.tensor_scalar(diag[:, u % 4, :], ident, rinv[:, u:u + 1], nlam[:, l:l + 1], ALU.mult, ALU.mult)
                            else:
                                ins = vec.tensor_scalar(diag[:, u % 4, :], ident, rinv[:, u:u + 1], None, ALU.mult)
                            ins.then_inc(s_dg[l], 1)
                    if v >= 3:
                        t = v - 3
                        mixer, h, qt, k0 = units[l][t]
                        dve.wait_ge(s_O[l], t + 1)
                        lo = 64 * (h % 2)
                        ch = 2 * "abcd".index(mixer) + h // 2
                        vec.tensor_copy(attnT[lo:lo + 64, ch, qt * P:(qt + 1) * P], bank[5 + t % 2][lo:lo + 64, 0:P]).then_inc(s_att[l], 1)
                    if mods and v % 4 == 3:
                        mod_columns(*mods.pop(0))
                assert not mods

                for j in range(2):
                    dve.wait_ge(s_cstd[l], j + 1)
                    link(vec.reciprocal(sqr[:, j, 0:n], sqr[:, j, 0:n]))
                    vec.scalar_tensor_tensor(attnT[:, 4 + j, 0:n], attnT[:, 4 + j, 0:n], subg[:, l:l + 1], sqr[:, j, 0:n],
                                             ALU.mult, ALU.mult).then_inc(s_cn[l], 1)
                layer_norm_dve(l, 0)
                for m in range(KD):
                    dve.wait_ge(LN[l][0]["x"], m + 1)
                    vec.tensor_scalar(hT[:, m, 0:SEQ], xT[:, m, 0:SEQ], modT1[:, l, SC2 + m, 0:1],
                                      modT[:, l, SH2 + m, 0:1], ALU.mult, ALU.add).then_inc(s_h2d[l], 1)

                dve.wait_ge(s_lg[l], 1)
                for t in range(nt):
                    vec.tensor_tensor(lg[:, t, :], bank[6][:, 36 * t:36 * (t + 1)], rowv[:, l, R_RB:R_RB + 36], ALU.add).then_inc(s_dch, 1)
                    chain[0] += 1
                dve.wait_ge(s_dch, chain[0])

                def col(i):
                    return rt[:, 0:nt, i:i + 1]

                def bc(i, k):
                    return rt[:, 0:nt, i:i + 1].to_broadcast([P, nt, k])

                def first_max(src, k, m, one):
                    iota = cst[:, C_IOTA:C_IOTA + k]
                    link(vec.tensor_reduce(col(m), src, AX, ALU.max))
                    link(vec.tensor_tensor(rt[:, 0:nt, one:one + k], src, bc(m, k), ALU.is_equal))
                    for t in range(nt):
                        link(vec.tensor_tensor(rt[:, t, one:one + k], rt[:, t, one:one + k], iota, ALU.mult))
                    link(vec.tensor_reduce(col(99), rt[:, 0:nt, one:one + k], AX, ALU.max))
                    link(vec.tensor_tensor(rt[:, 0:nt, one:one + k], rt[:, 0:nt, one:one + k], bc(99, k), ALU.is_equal))

                first_max(lg[:, 0:nt, 0:4], 4, 96, 8)
                vec.tensor_tensor(rt[:, 0:nt, 0:4], lg[:, 0:nt, 0:4], bc(96, 4), ALU.subtract).then_inc(s_rexp[l], 1)
                for t in range(nt):
                    prod = rt[:, t, 64:96].rearrange("p (g e) -> p g e", g=4)
                    one = rt[:, t, 8:12].unsqueeze(2).to_broadcast([P, 4, 8])
                    link(vec.tensor_tensor(prod, lg[:, t, 4:36].rearrange("p (g e) -> p g e", g=4), one, ALU.mult))
                    link(vec.tensor_reduce(rt[:, t, 24:32], rt[:, t, 64:96].rearrange("p (g e) -> p e g", g=4), AX, ALU.add))
                first_max(rt[:, 0:nt, 24:32], 8, 97, 40)
                link(vec.scalar_tensor_tensor(rt[:, 0:nt, 32:40], rt[:, 0:nt, 40:48], NEG, rt[:, 0:nt, 24:32], ALU.mult, ALU.add))
                first_max(rt[:, 0:nt, 32:40], 8, 98, 48)
                vec.tensor_tensor(col(100), col(98), col(97), ALU.subtract).then_inc(s_rexp[l], 1)
                dve.wait_ge(s_rexpd[l], 2)
                link(vec.tensor_reduce(col(101), rt[:, 0:nt, 0:4], AX, ALU.add))
                link(vec.reciprocal(col(101), col(101)))
                link(vec.tensor_scalar(col(102), col(100), 1.0, None, ALU.add))
                link(vec.reciprocal(col(102), col(102)))
                link(vec.tensor_tensor(col(102), col(102), col(101), ALU.mult))
                link(vec.tensor_tensor(col(103), col(102), col(100), ALU.mult))
                link(vec.tensor_tensor(rt[:, 0:nt, 56:64], rt[:, 0:nt, 40:48], bc(102, 8), ALU.mult))
                link(vec.tensor_tensor(rt[:, 0:nt, 48:56], rt[:, 0:nt, 48:56], bc(103, 8), ALU.mult))
                link(vec.tensor_tensor(rt[:, 0:nt, 56:64], rt[:, 0:nt, 56:64], rt[:, 0:nt, 48:56], ALU.add))
                for t in range(nt):
                    for g in range(4):
                        ins = vec.tensor_scalar(gates[:, t, 8 * g:8 * g + 8], rt[:, t, 56:64], rt[:, t, 8 + g:9 + g], None, ALU.mult)
                ins.then_inc(s_gates[l], 1)
                dve.wait_ge(s_gT[l], 1)
                vec.tensor_copy(gT[:, 0:n], bank[5][0:NE, 0:n]).then_inc(s_gTs[l], 1)

                for e in range(NE):
                    dve.wait_ge(s_bcs[l], e + 1)
                    for f in range(2):
                        dve.wait_ge(s_sg[l], 2 * e + f + 1)
                        if e >= 1:
                            dve.wait_ge(s_dn[l], KD * e)
                        link(vec.tensor_tensor(hid[:, f, 0:n], sg[:, f, 0:n], bank[2 + f][:, 0:n], ALU.mult))
                        vec.tensor_tensor(hid[:, f, 0:n], hid[:, f, 0:n], gbc[:, 0:n], ALU.mult).then_inc(s_hid[l], 1)
                    for m in range(KD):
                        dve.wait_ge(s_dn[l], KD * e + m + 1)
                        if e == 0:
                            vec.tensor_copy(yT[:, m, 0:n], bank[5 + m % 2][:, 0:n]).then_inc(s_ya[l], 1)
                        else:
                            dve.wait_ge(s_ya[l], KD * (e - 1) + m + 1)
                            vec.tensor_tensor(yT[:, m, 0:n], yT[:, m, 0:n], bank[5 + m % 2][:, 0:n], ALU.add).then_inc(s_ya[l], 1)
                layer_norm_dve(l, 1)

            for t in range(2):
                for j in range(4):
                    q = 4 * t + j
                    dve.wait_ge(s_ot, q + 1)
                    vec.tensor_copy(xin[:, t, 256 * j:256 * (j + 1)], bank[q % 2][:, 0:256]).then_inc(s_oe, 1)

        @block.tensor
        def _(pe):
            mm = nc.tensor.matmul
            pe.wait_ge(s_small, 64)
            for l in range(DEPTH):
                nc.tensor.transpose(bank[l][:, 0:P], vrow[:, l, :], ident).then_inc(s_vt, 1)
            pe.wait_ge(s_xin, 32)
            for k in range(KD):
                if k >= 2:
                    pe.wait_ge(s_xT, k - 1)
                for t in range(4):
                    ins = nc.tensor.transpose(bank[2 + k % 2][:, t * P:(t + 1) * P], xin[:, t, k * P:(k + 1) * P], ident)
                ins.then_inc(s_tp, 1)

            def arrived(i):
                s, n = arrival(i)
                pe.wait_ge(w_here[s], n)
                return slots[:, s, :]

            def modulation(l, c):
                w = arrived(INDEX["mod", l, c]).rearrange("p (k n) -> p k n", k=KD)
                if 8 * l + c >= 3:
                    pe.wait_ge(s_modT, 8 * l + c)
                elif c == 2:
                    pe.wait_ge(s_modT, 1)
                for j in range(MOD_J):
                    for k in range(KD):
                        ins = mm(mod_bank(8 * l + c)[:, 2 * j:2 * j + 2], w[:, k, j * P:(j + 1) * P], cT[:, :, k], start=(k == 0), stop=(k == KD - 1))
                ins.then_inc(s_mod, 1)

            def layer_norm_pe(l, w):
                s = LN[l][w]
                n = TQ[l]
                for m in range(KD):
                    pe.wait_ge(s["z"], m + 1)
                    ins = mm(bank[4][:, 0:n], onesD[:, :], zT[:, m, 0:n], start=(m == 0), stop=(m == KD - 1))
                ins.then_inc(s["mean"], 1)
                for m in range(KD):
                    pe.wait_ge(s["sq"], m + 1)
                    mm(bank[5][:, 0:n], ones[:, :], sqr[:, m % 2, 0:n], start=(m == 0), stop=(m == KD - 1)).then_inc(s["sqs"], 1)

            def projection(l, g, w):
                name, i = GROUPS[g]
                o = bank[g % PROJ_BANKS]
                n = width(l, name)

                def features(lhs, out, rhs_n):
                    for k in range(KD):
                        ins = mm(out, lhs(k), hT[:, k, 0:rhs_n], start=(k == 0), stop=(k == KD - 1))
                    return ins

                def tokens(c0, nc_, tiles):
                    for a, t in enumerate(tiles):
                        for k in range(KD):
                            ins = mm(o[:, a * nc_:(a + 1) * nc_], hT[:, k, t * P:(t + 1) * P], w[:, k, c0:c0 + nc_],
                                     start=(k == 0), stop=(k == KD - 1))
                    return ins

                if name == "qa":
                    return features(lambda k: w[:, k, 128 * i:128 * (i + 1)], o[:, 0:n], n)
                if name == "ka":
                    return features(lambda k: w[:, k, 256:384], o[:, :], n)
                if name == "va":
                    return tokens(384, P, range(4))
                if name in ("pq", "pkv"):
                    c0 = 128 * i if name == "pq" else 256
                    return features(lambda k: w[:, k, c0:c0 + 128], o[:, 0:n], n)
                if name == "kr":
                    return features(lambda k: w[:, k, 384:416], o[64:96, 0:n], n)
                if name in ("qd", "kd", "qn", "kn"):
                    c0 = (0 if name[0] == "q" else 256) + 128 * i
                    return features(lambda k: w[:, k, c0:c0 + 128], o[:, 0:n], n)
                if name in ("vd", "vn"):
                    return tokens(512, 256, (2 * i, 2 * i + 1))
                if name == "ssq":
                    mm(o[:, 0:n], ones[:, :], psq[:, 0, 0:n], start=True, stop=False)
                    return mm(o[:, 0:n], ones[:, :], psq[:, 1, 0:n], start=False, stop=True)
                if name == "sskv":
                    return mm(o[:, :], ones[:, :], psq[:, 2, :], start=True, stop=True)
                if name == "mk":
                    return mm(o[0:64, :], wukv[:, i * P:i * P + 64], praw[:, 2, :], start=True, stop=True)
                if name == "mv":
                    for a in range(2):
                        t = 2 * i + a
                        ins = mm(o[:, a * 256:(a + 1) * 256], praw[:, 2, t * P:(t + 1) * P],
                                 wukv[:, :].rearrange("p (h a c) -> p h a c", h=4, a=2)[:, :, 1, :], start=True, stop=True)
                    return ins
                mm(o[0:96, 0:n], wuq[:, 0, 96 * i:96 * (i + 1)], praw[:, 0, 0:n], start=True, stop=False)
                return mm(o[0:96, 0:n], wuq[:, 1, 96 * i:96 * (i + 1)], praw[:, 1, 0:n], start=False, stop=True)

            def permute(l, r):
                g = ROPES[r]
                name, i = GROUPS[g]
                lo, hi = (64, 96) if name in ("kr", "mq") else (0, 128)
                c = C_P16 if name in ("qa", "ka") else C_P8
                pe.wait_ge(s_eva[l], NACT[g])
                if r >= 2:
                    pe.wait_ge(s_rope[l], r - 1)
                mm(bank[4 + r % 2][lo:hi, 0:SEQ], cst[lo:hi, c + lo:c + hi], dest(name, i)[lo:hi, 0:SEQ],
                   start=True, stop=True).then_inc(s_perm[l], 1)

            pe.wait_ge(s_cT, 1)
            pe.wait_ge(s_ones, 1)
            for c in range(3):
                modulation(0, c)

            for l in range(DEPTH):
                n = TQ[l]
                nt = n // P
                pe.wait_ge(s_h1a[l], KD)
                pe.wait_ge(s_h1d[l], KD)
                part = None
                done = 0
                for g, (name, i) in enumerate(GROUPS):
                    if PART_OF.get(name) is not None and PART_OF[name] != part:
                        part = PART_OF[name]
                        w = arrived(INDEX["in", l, part])[:, 0:KD * IN_PARTS[part][1]].rearrange("p (k n) -> p k n", k=KD)
                    if g >= PROJ_BANKS:
                        old = g - PROJ_BANKS
                        if GROUPS[old][0] in BY_ACT:
                            pe.wait_ge(s_eva[l], NACT[old])
                        else:
                            pe.wait_ge(s_evd[l], NDVE[old])
                    if name == "ssq":
                        pe.wait_ge(s_psq[l], 3)
                    if (name, i) == ("mk", 0):
                        pe.wait_ge(s_wqkv[l], 32)
                        pe.wait_ge(s_pn[l], 3)
                    projection(l, g, w).then_inc(s_grp[l], 1)
                    while done < len(ROPES) and ROPES[done] + 2 <= g:
                        permute(l, done)
                        done += 1
                while done < len(ROPES):
                    permute(l, done)
                    done += 1

                uf = first[l]
                mods = [(0, c) for c in range(3, 8)] + [(1, c) for c in range(8)] if l == 0 else []
                pe.wait_ge(s_rope[l], len(ROPES))
                pe.wait_ge(s_eva[l], NACT[-1])
                pe.wait_ge(s_evd[l], NDVE[-1])
                for v in range(len(units[l]) + 3):
                    if v < len(units[l]):
                        mixer, h, qt, k0 = units[l][v]
                        q = slice(qt * P, (qt + 1) * P)
                        for u in range(uf[v], uf[v + 1]):
                            if u >= 3:
                                pe.wait_ge(s_exp[l], u - 2)
                            if mixer == "a":
                                lo, k = 64 * (h // 2), 64
                                qs, ks = QA[lo:lo + k, h % 2, q], KA[lo:lo + k, k0 * P:TOK]
                            elif mixer == "b":
                                qs, ks = QM[0:96, h, q], KM[0:96, h, k0 * P:TOK]
                            elif mixer == "c":
                                lo, k = 64 * (h % 2) + 32 * (u - uf[v]), 32
                                qs, ks = QDf[lo:lo + k, h // 2, q], KDf[lo:lo + k, h // 2, k0 * P:TOK]
                            else:
                                lo, k = 64 * (h % 2), 64
                                qs, ks = QN[lo:lo + k, h // 2, q], KN[lo:lo + k, h // 2, k0 * P:TOK]
                            more = mixer in "ad" and k0 == 0
                            ins = mm(bank[u % 3][:, k0 * P:TOK], qs, ks, start=True, stop=not more)
                            if more:
                                if mixer == "a":
                                    extra = cst[:, C_SWA + SEQ * qt:C_SWA + SEQ * (qt + 1)]
                                else:
                                    pe.wait_ge(s_biasm[l], 4)
                                    extra = biasm[:, h, qt, :]
                                ins = mm(bank[u % 3][:, 0:SEQ], ident, extra, start=False, stop=True)
                            ins.then_inc(s_S[l], 1)
                    if 2 <= v < len(units[l]) + 2:
                        t = v - 2
                        k0 = units[l][t][3]
                        pe.wait_ge(s_dg[l], uf[t + 1])
                        if t >= 2:
                            pe.wait_ge(s_PT[l], t - 1)
                        for kt in range(k0, 4):
                            for u in range(uf[t], uf[t + 1]):
                                ins = mm(bank[3 + t % 2][:, kt * P:(kt + 1) * P], Pr[:, u % 4, kt * P:(kt + 1) * P], diag[:, u % 4, :],
                                         start=(u == uf[t]), stop=(u == uf[t + 1] - 1))
                        ins.then_inc(s_T[l], 1)
                    if v >= 3:
                        t = v - 3
                        mixer, h, qt, k0 = units[l][t]
                        pe.wait_ge(s_PT[l], t + 1)
                        if t >= 2:
                            pe.wait_ge(s_att[l], t - 1)
                        lo = 64 * (h % 2)
                        c0 = VOFF[mixer] + 64 * (h // 2 if mixer == "a" else h)
                        for kt in range(k0, 4):
                            ins = mm(bank[5 + t % 2][lo:lo + 64, 0:P], V[:, kt, c0:c0 + 64], PTs[:, t % 2, kt * P:(kt + 1) * P],
                                     start=(kt == k0), stop=(kt == 3))
                        ins.then_inc(s_O[l], 1)
                    if mods and v % 4 == 3:
                        modulation(*mods.pop(0))
                for j in range(2):
                    pe.wait_ge(s_csq[l], j + 1)
                    mm(bank[j][:, 0:n], cst[:, C_BLK:C_BLK + P], sqr[:, j, 0:n], start=True, stop=True).then_inc(s_css[l], 1)
                pe.wait_ge(s_att[l], len(units[l]))
                pe.wait_ge(s_cn[l], 2)
                for m in range(KD):
                    w = arrived(INDEX["out", l, m // 4])[:, 0:KD * 512].rearrange("p (k n) -> p k n", k=KD)
                    if m >= 4:
                        pe.wait_ge(s_yg[l], m - 3)
                    for k in range(KD):
                        ins = mm(bank[m % 4][:, 0:n], w[:, k, (m % 4) * P:(m % 4 + 1) * P], attnT[:, k, 0:n],
                                 start=(k == 0), stop=(k == KD - 1))
                    ins.then_inc(s_y[l], 1)
                layer_norm_pe(l, 0)
                pe.wait_ge(s_h2d[l], KD)
                if n > SEQ:
                    pe.wait_ge(s_h2p[l], KD)
                for t in range(nt):
                    for k in range(KD):
                        ins = mm(bank[6][:, 36 * t:36 * (t + 1)], hT[:, k, t * P:(t + 1) * P], wr[:, l, k, :],
                                 start=(k == 0), stop=(k == KD - 1))
                ins.then_inc(s_lg[l], 1)
                pe.wait_ge(s_gates[l], 1)
                for t in range(nt):
                    ins = nc.tensor.transpose(bank[5][0:NE, t * P:(t + 1) * P], gates[:, t, :], ident)
                ins.then_inc(s_gT[l], 1)
                pe.wait_ge(s_gTs[l], 1)
                for e in range(NE):
                    if e >= 1:
                        pe.wait_ge(s_bcs[l], e)
                    mm(bank[4][:, 0:n], ident[0:NE, e:e + 1].to_broadcast([NE, P]), gT[:, 0:n], start=True, stop=True).then_inc(s_bc[l], 1)
                    w = arrived(INDEX["exp", l, e])
                    for f in range(2):
                        if e >= 1:
                            pe.wait_ge(s_sg[l], 2 * e - 1 + f)
                            pe.wait_ge(s_hid[l], 2 * e - 1 + f)
                        for j in range(2):
                            wj = w[:, 2048 * j:2048 * (j + 1)].rearrange("p (k f) -> p k f", k=KD)
                            for k in range(KD):
                                ins = mm(bank[2 * j + f][:, 0:n], wj[:, k, f * P:(f + 1) * P], hT[:, k, 0:n],
                                         start=(k == 0), stop=(k == KD - 1))
                        ins.then_inc(s_hg[l], 1)
                    wd = w[:, 4096:6144].rearrange("p (k d) -> p k d", k=2)
                    pe.wait_ge(s_hid[l], 2 * (e + 1))
                    for m in range(KD):
                        if KD * e + m >= 2:
                            pe.wait_ge(s_ya[l], KD * e + m - 1)
                        for f in range(2):
                            ins = mm(bank[5 + m % 2][:, 0:n], wd[:, f, m * P:(m + 1) * P], hid[:, f, 0:n], start=(f == 0), stop=(f == 1))
                        ins.then_inc(s_dn[l], 1)
                layer_norm_pe(l, 1)
            pe.wait_ge(LN[1][1]["x"], KD)
            for q in range(8):
                if q >= 2:
                    pe.wait_ge(s_oe, q - 1)
                t, j = q // 4, q % 4
                for a in range(2):
                    ins = nc.tensor.transpose(bank[q % 2][:, a * P:(a + 1) * P], xT[:, 2 * j + a, t * P:(t + 1) * P], ident)
                ins.then_inc(s_ot, 1)


def shape_constants():
    import numpy as np
    c = np.zeros((P, C_ALL), np.float32)
    p = np.arange(P)
    c[p, C_ID + p] = 1
    c[p, C_P16 + (p ^ 16)] = 1
    c[p, C_P8 + (p ^ 8)] = 1
    c[:, C_BLK:C_BLK + P] = (p[:, None] // 64 == p[None] // 64) / 64.0
    t = np.arange(SEQ)
    for width, o_cos, o_sin in ((64, C_COS64, C_SIN64), (32, C_COS32, C_SIN32)):
        r, half = width // 2, width // 4
        inv = (np.float32(10000.0) ** (-np.arange(half, dtype=np.float32) / np.float32(half))).astype(np.float32)
        d = p % width
        pos = np.where((d < r)[:, None], (t // GRID_W)[None], (t % GRID_W)[None]).astype(np.float32)
        ang = pos * inv[d % half][:, None]
        c[:, o_cos:o_cos + SEQ] = np.cos(ang)
        c[:, o_sin:o_sin + SEQ] = np.sin(ang) * np.where(d % r < half, -1.0, 1.0)[:, None]
    q = np.arange(SEQ).reshape(2, P).T[:, :, None]
    k = t[None, None, :]
    c[:, C_SWA:C_SWA + 512] = np.where(np.abs(k - q) <= 128, 0, NEG).reshape(P, 512)
    start = np.clip(q % GRID_W - 8, 0, GRID_W - 16)
    c[:, C_NA:C_NA + 512] = np.where((k % GRID_W >= start) & (k % GRID_W < start + 16), 0, NEG).reshape(P, 512)
    c[:, C_IOTA:C_IOTA + 16] = 16 - np.arange(16)
    return c


def kernel(**inputs):
    import numpy as np
    import concourse.bacc as bacc
    from concourse.bass_utils import run_bass_kernel_spmd

    a = {k: np.asarray(v) for k, v in inputs.items()}
    def r128(v):
        return v.reshape(DEPTH, -1, P)
    both = np.stack([np.concatenate([a["c"].reshape(KD, P), a["c_ctx"].reshape(KD, P)])] * DEPTH)
    sub = np.concatenate([a["diff_subln"], a["diff_subln"]], -1).reshape(DEPTH, 1, P)
    vecs = np.concatenate([r128(a["b_mod"]), r128(a["ln1_g"]), r128(a["ln1_b"]), r128(a["ln2_g"]), r128(a["ln2_b"]),
                           r128(a["mla_q_norm"]), r128(a["mla_kv_norm"]), sub, both, np.zeros((DEPTH, P - 100, P), np.float32)], 1)
    rows = np.concatenate([a["attn_sink"], a["lam_q1"], a["lam_k1"], a["lam_q2"], a["lam_k2"], a["b_group"], a["b_router"]], -1)
    rows = np.ascontiguousarray(np.broadcast_to(rows[:, None, :], (DEPTH, P, R_ALL)))
    w = a["w_in"]
    w_in = np.concatenate([w[:, :, 0:64], w[:, :, 128:192], w[:, :, 64:128], w[:, :, 192:]], -1)
    t = np.arange(SEQ)
    row_off = (t[None] // GRID_W) - (t[:, None] // GRID_W) + 7
    col_off = np.clip((t[None] % GRID_W) - (t[:, None] % GRID_W) + 15, 0, 30)
    bias = a["na_rpb"][:, :, row_off, col_off]
    ins = {
        "x": a["x"], "ctx": a["ctx"], "w_mod": a["w_mod"], "w_in": w_in, "w_uq": a["w_uq"], "w_ukv": a["w_ukv"],
        "w_out": a["w_out"], "w_route": np.concatenate([a["w_group"], a["w_router"]], -1),
        "w_gate": a["w_gate"], "w_up": a["w_up"], "w_down": a["w_down"],
        "vecs": vecs, "rows": rows, "bias_na": bias, "consts": shape_constants(),
    }
    nc = bacc.Bacc("TRN2", target_bir_lowering=False, num_devices=1)
    arrays, args = {}, []
    for name, v in ins.items():
        v = np.ascontiguousarray(v)
        arrays[f"in_{name}"] = v
        args.append(nc.dram_tensor(f"in_{name}", v.shape, mybir.dt.from_np(v.dtype), kind="ExternalInput").ap())
    args.append(nc.dram_tensor("out_0", (1, SEQ, D), F32, kind="ExternalOutput").ap())
    build(nc, *args)
    r = run_bass_kernel_spmd(nc, [arrays], core_ids=[0])
    return r.results[0]["out_0"]
```

```python
import math
from contextlib import ExitStack

import concourse.bass as bass
from concourse import mybir

P = 128
D = 1024
KD = D // P
SEQ = 256
CTX = 256
TOK = SEQ + CTX
DEPTH = 2
D_IN = 2464
GRID_W = 64
NE = 32
FH = 256
ALPHA = (2 * DEPTH) ** 0.25
EPS = 1e-5
NEG = -1e30

F32 = mybir.dt.float32
ALU = mybir.AluOpType
ACT = mybir.ActivationFunctionType
AX = mybir.AxisListType.X

CH = 64

C_ID, C_P16, C_P8, C_BLK = 0, 128, 256, 384
C_COS64, C_SIN64, C_COS32, C_SIN32 = 512, 768, 1024, 1280
C_SWA, C_NA = 1536, 2048
C_IOTA = 2560
C_UP = C_IOTA + 16
C_UPX = C_UP + P
C_UP64 = C_UPX + 65
C_THR = C_UP64 + 32
C_SLOT = C_THR + 8
C_ALL = C_SLOT + CH

V_MOD, V_LN1G, V_LN1B, V_LN2G, V_LN2B, V_QN, V_KVN, V_SUB, V_C, V_CC = 0, 48, 56, 64, 72, 80, 82, 83, 84, 92
R_SINK, R_LAM, R_RB = 0, 4, 132
R_ALL = 168
SH1, SC1, G1, SH2, SC2, G2 = 0, 8, 16, 24, 32, 40

MOD_COLS = 768
MOD_J = MOD_COLS // P
MOD_N = 64
IN_PARTS = [(0, 512), (512, 416), (928, 768), (1696, 768)]
SLOT = 6144
SLOTS = 3

CHUNKS = [NE + 2 * TOK // CH, NE + 2 * SEQ // CH]
T_FIRST, T_ALL, T_N = 0, NE, NE + 1


def load_plan():
    plan = [("mod", 0, c) for c in range(3)] + [("in", 0, c) for c in range(4)]
    plan += [("mod", 0, c) for c in range(3, 8)] + [("mod", 1, c) for c in range(8)]
    plan += [("out", 0, c) for c in range(2)] + [("exp", 0, e) for e in range(NE)]
    plan += [("in", 1, c) for c in range(4)] + [("out", 1, c) for c in range(2)] + [("exp", 1, e) for e in range(NE)]
    return plan


PLAN = load_plan()
INDEX = {w: i for i, w in enumerate(PLAN)}
DMAS = {"mod": 1, "in": 1, "out": 1, "exp": 2}


def arrival(i):
    return i % SLOTS, 16 * sum(DMAS[PLAN[j][0]] for j in range(i % SLOTS, i + 1, SLOTS))


def gate_arrival(i):
    return 16 * sum(PLAN[j][0] == "exp" for j in range(i % SLOTS, i + 1, SLOTS))


def attention_units(l):
    out = []
    for mixer in "cabd":
        for h in range(4):
            for qt in range(4 if l == 0 else 2):
                out.append((mixer, h, qt, 0 if qt < 2 else 2))
    return out


GROUPS = [
    ("qa", 0), ("qa", 1), ("ka", 0), ("va", 0),
    ("pq", 0), ("pq", 1), ("pkv", 0), ("kr", 0),
    ("qd", 0), ("qd", 1), ("kd", 0), ("kd", 1), ("vd", 0), ("vd", 1),
    ("ssq", 0), ("sskv", 0),
    ("qn", 0), ("qn", 1), ("kn", 0), ("kn", 1), ("vn", 0), ("vn", 1),
    ("mk", 0), ("mk", 1), ("mk", 2), ("mk", 3), ("mv", 0), ("mv", 1),
    ("mq", 0), ("mq", 1), ("mq", 2), ("mq", 3),
]
ROPED = ("qa", "ka", "kr", "qd", "kd", "mq")
BY_ACT = ROPED + ("ssq", "sskv", "qn")
LAST_OF_PART = {("va", 0): 0, ("kr", 0): 1, ("vd", 1): 2, ("vn", 1): 3}
PART_OF = {"qa": 0, "ka": 0, "va": 0, "pq": 1, "pkv": 1, "kr": 1, "qd": 2, "kd": 2, "vd": 2, "qn": 3, "kn": 3, "vn": 3}
NACT = [sum(n in BY_ACT for n, _ in GROUPS[:g + 1]) for g in range(len(GROUPS))]
NDVE = [sum(n not in BY_ACT for n, _ in GROUPS[:g + 1]) for g in range(len(GROUPS))]
ROPES = [g for g, (n, _) in enumerate(GROUPS) if n in ROPED]
GI = {g: i for i, g in enumerate(GROUPS)}
SCALE = {"qa": 64 ** -0.5, "ka": 1.0, "kr": 1.0, "qd": 32 ** -0.5, "kd": 1.0, "mq": 96 ** -0.5, "qn": 64 ** -0.5}
PROJ_BANKS = 4


def build(nc, x, ctx_in, w_mod, w_in, w_uq, w_ukv, w_out, w_route, w_gate, w_up, w_down, vecs, rows, bias_na, consts, out):
    with ExitStack() as st:
        def sb(name, shape):
            return st.enter_context(nc.sbuf_tensor(name, shape, F32))

        def sem(name):
            return st.enter_context(nc.semaphore(name))

        def per_layer(name):
            return [sem(f"{name}_{l}") for l in range(DEPTH)]

        xT = sb("xT", [P, KD, TOK])
        hT = sb("hT", [P, KD, TOK])
        attnT = hT
        zbuf = sb("zbuf", [P, KD * TOK])
        zT = zbuf[:, :].rearrange("p (k t) -> p k t", k=KD)
        xin = zbuf[:, :].rearrange("p (a d) -> p a d", a=4)
        slots = sb("slots", [P, SLOTS, SLOT])
        region = sb("region", [P, 13312])

        def part(o, *dims):
            n = math.prod(dims)
            v = region[:, o:o + n]
            if len(dims) == 1:
                return v
            return v.rearrange("p (a b) -> p a b", a=dims[0])

        QM = part(0, 4, TOK)
        KM = part(2048, 4, TOK)
        QA = part(4096, 2, TOK)
        KA = part(5120, TOK)
        QDf = part(5632, 2, TOK)
        KDf = part(6656, 2, TOK)
        QN = part(7680, 2, TOK)
        KN = part(8704, 2, TOK)
        V = part(9728, 4, 896)
        VOFF = {"a": 0, "c": 128, "d": 384, "b": 640}
        cst = sb("cst", [P, C_ALL])
        biasm = sb("biasm", [P, 4, 2, SEQ])
        ropet = sb("ropet", [P, 2, SEQ])
        wuq = sb("wuq", [P, 2, 384])
        wukv = sb("wukv", [P, 512])
        tab = st.enter_context(nc.sbuf_tensor("tab", [P, DEPTH, 65], mybir.dt.int32))
        pos = st.enter_context(nc.sbuf_tensor("pos", [P, DEPTH, 8], mybir.dt.int32))
        gate = sb("gate", [P, DEPTH, 8])
        wr = sb("wr", [P, DEPTH, KD, 36])
        colv = sb("colv", [P, DEPTH, P])
        rowv = sb("rowv", [P, DEPTH, R_ALL])
        cT = sb("cT", [P, 2, KD])
        modT = sb("modT", [P, DEPTH, 48, 2])
        modT1 = sb("modT1", [P, DEPTH, 48, 2])
        onesD = sb("onesD", [P, P])
        ones = sb("ones", [P, P])
        epst = sb("epst", [P, 1])
        nlam = sb("nlam", [P, DEPTH])
        nsink = sb("nsink", [P, DEPTH, 4])
        lamt = sb("lamt", [P, 2, 32])
        lams = sb("lams", [P, 4])
        subg = sb("subg", [P, DEPTH])
        nmx = sb("nmx", [P, 80])
        rsum = sb("rsum", [P, 80])
        rinv = sb("rinv", [P, 80])
        esk = sb("esk", [P, 80])
        vrow = part(4096, DEPTH, P)
        sqr = part(0, 2, TOK)
        rstd = part(1024, TOK)
        rt = part(1536, 4, 104)
        lg = part(1952, 4, 36)
        oh = [part(2096 + 128 * i, 4, NE) for i in range(3)]
        posp = part(2480, 4, NE)
        nch = part(2608, 8)
        nrep = part(2616, P)
        prel = part(2744, 8)
        pick = part(2752, 4, CH)
        pick2 = part(3008, 4, CH)
        xcols = part(3264, KD, CH)
        hid = part(3776, 2, CH)
        sg = part(3904, 2, CH)
        yrows = part(4032, D)
        htok = part(9216, 4, D)
        y2 = htok
        y1 = hT[:, :, :].rearrange("p (a b) t -> p a (b t)", a=4)
        praw = zT[:, 0:3, :]
        psq = zT[:, 3:6, :]
        prstd = zT[:, 6:8, :]
        Pr = zT[:, 0:4, :]
        PTs = zT[:, 4:6, :]
        diag = zT[:, 6, :].rearrange("p (a b) -> p a b", a=4)
        ident = cst[:, C_ID:C_ID + P]

        bank = [st.enter_context(nc.psum_tensor(f"bank{i}", [P, 512], F32)) for i in range(8)]

        w_here = [sem(f"w_here{i}") for i in range(SLOTS)]
        g_here = [sem(f"g_here{i}") for i in range(SLOTS)]
        s_small = sem("s_small")
        s_xin = sem("s_xin")
        s_wqkv = per_layer("s_wqkv")
        s_bias = per_layer("s_bias")
        s_biasm = per_layer("s_biasm")
        s_ones = sem("s_ones")
        s_vt = sem("s_vt")
        s_colv = sem("s_colv")
        s_cT = sem("s_cT")
        s_lamp = sem("s_lamp")
        s_lame = sem("s_lame")
        s_tp = sem("s_tp")
        s_xT = sem("s_xT")
        s_mod = sem("s_mod")
        s_modT = sem("s_modT")
        s_h1a = per_layer("s_h1a")
        s_h1d = per_layer("s_h1d")
        s_grp = per_layer("s_grp")
        s_eva = per_layer("s_eva")
        s_evd = per_layer("s_evd")
        s_perm = per_layer("s_perm")
        s_rope = per_layer("s_rope")
        s_psq = per_layer("s_psq")
        s_prstd = per_layer("s_prstd")
        s_pn = per_layer("s_pn")
        s_S = per_layer("s_S")
        s_nm = per_layer("s_nm")
        s_exp = per_layer("s_exp")
        s_dg = per_layer("s_dg")
        s_T = per_layer("s_T")
        s_PT = per_layer("s_PT")
        s_O = per_layer("s_O")
        s_att = per_layer("s_att")
        s_csq = per_layer("s_csq")
        s_css = per_layer("s_css")
        s_cstd = per_layer("s_cstd")
        s_cn = per_layer("s_cn")
        s_y = per_layer("s_y")
        s_yg = per_layer("s_yg")
        ln = {n: sem(f"ln_{n}") for n in ("z", "mean", "cent", "sq", "sqs", "std", "zn", "x")}
        s_h2d = per_layer("s_h2d")
        s_h2p = per_layer("s_h2p")
        s_lg = per_layer("s_lg")
        s_rexp = per_layer("s_rexp")
        s_rexpd = per_layer("s_rexpd")
        s_mask = per_layer("s_mask")
        s_cnt = per_layer("s_cnt")
        s_nch = per_layer("s_nch")
        s_pos = per_layer("s_pos")
        s_tab = per_layer("s_tab")
        s_tok = per_layer("s_tok")
        s_prel = per_layer("s_prel")
        s_pick = per_layer("s_pick")
        s_toke = per_layer("s_toke")
        s_xt = per_layer("s_xt")
        s_xc = per_layer("s_xc")
        s_hg = per_layer("s_hg")
        s_sg = per_layer("s_sg")
        s_hid = per_layer("s_hid")
        s_dn = per_layer("s_dn")
        s_yev = per_layer("s_yev")
        s_yfree = per_layer("s_yfree")
        s_yw = per_layer("s_yw")
        s_cmb = per_layer("s_cmb")
        s_yt = per_layer("s_yt")
        s_yh = per_layer("s_yh")
        s_gat = [sem(f"s_gat{t}") for t in range(4)]
        s_fill = sem("s_fill")
        s_ot = sem("s_ot")
        s_oe = sem("s_oe")
        s_out = sem("s_out")
        s_dch = sem("s_dch")
        s_ach = sem("s_ach")

        slot_outs = nc.dram_tensor("slot_outs", (CHUNKS[0] * CH, D), F32, kind="Internal").ap()
        chunk_outs = slot_outs.rearrange("(g p) d -> g p d", p=CH)

        block = st.enter_context(nc.Block())

        units = [attention_units(l) for l in range(DEPTH)]
        first = []
        for l in range(DEPTH):
            f = [0]
            for u in units[l]:
                f.append(f[-1] + (2 if u[0] == "c" else 1))
            first.append(f)
        TQ = [TOK, SEQ]

        def dest(name, i):
            return {"qa": lambda: QA[:, i, :], "ka": lambda: KA[:, :], "qd": lambda: QDf[:, i, :], "kd": lambda: KDf[:, i, :],
                    "qn": lambda: QN[:, i, :], "kn": lambda: KN[:, i, :], "mq": lambda: QM[:, i, :],
                    "kr": lambda: KM[:, 0, :]}[name]()

        def width(l, name):
            return TQ[l] if name in ("qa", "qd", "qn", "mq", "ssq") or name == "pq" else TOK

        def released(i):
            kind, l, c = PLAN[i]
            if kind == "mod":
                return s_mod, 8 * l + c + 1
            if kind == "in":
                return s_grp[l], GI[[g for g, p in LAST_OF_PART.items() if p == c][0]] + 1
            if kind == "out":
                return s_y[l], 4 * (c + 1)
            raise ValueError(kind)

        def mod_bank(i):
            return bank[6 + i % 2] if i < 3 else bank[7]

        @block.sync
        def _(sp):
            sp.dma_start(xin[:, 0:2, :], x.rearrange("o (a p) d -> p (o a) d", p=P)).then_inc(s_xin, 16)
            sp.dma_start(xin[:, 2:4, :], ctx_in.rearrange("o (a p) d -> p (o a) d", p=P)).then_inc(s_xin, 16)
            def load(kind, l, c, slot_n, gate_here):
                here = w_here[slot_n]
                slot = slots[:, slot_n, :]
                if kind == "mod":
                    sp.dma_start(slot.rearrange("p (k n) -> p k n", k=KD),
                                 w_mod[l].rearrange("(k p) n -> p k n", p=P)[:, :, c * MOD_COLS:(c + 1) * MOD_COLS]).then_inc(here, 16)
                elif kind == "in":
                    o, n = IN_PARTS[c]
                    sp.dma_start(slot[:, 0:KD * n].rearrange("p (k n) -> p k n", k=KD),
                                 w_in[l].rearrange("(k p) n -> p k n", p=P)[:, :, o:o + n]).then_inc(here, 16)
                elif kind == "out":
                    sp.dma_start(slot[:, 0:KD * 512].rearrange("p (k n) -> p k n", k=KD),
                                 w_out[l].rearrange("(k p) n -> p k n", p=P)[:, :, c * 512:(c + 1) * 512]).then_inc(here, 16)
                else:
                    for j, w in enumerate((w_gate, w_up)):
                        sp.dma_start(slot[:, j * 2048:(j + 1) * 2048].rearrange("p (k f) -> p k f", k=KD),
                                     w[l].rearrange("g e (k p) f -> (g e) p k f", p=P)[c]).then_inc(here if j else g_here[slot_n], 16)
                    sp.wait_ge(g_here[slot_n], gate_here)
                    sp.dma_start(slot[:, 4096:6144].rearrange("p (k d) -> p k d", k=2),
                                 w_down[l].rearrange("g e (k p) d -> (g e) p k d", p=P)[c]).then_inc(here, 16)

            i = 0
            while i < len(PLAN):
                kind, l, c = PLAN[i]
                if kind == "exp" and c == SLOTS:
                    sp.wait_ge(s_tab[l], 1)

                    def next_expert(e, slot, gate_here):
                        done = sp.value_load(tab[0:1, l, bass.ds(e - (SLOTS - 1), 1)], min_val=1, max_val=CHUNKS[l])
                        sp.wait_ge(s_dn[l], done)
                        load("exp", l, e, slot, gate_here)

                    rounds = (NE - SLOTS) // SLOTS
                    with sp.Fori(1, rounds + 1) as r0:
                        e0 = r0 * SLOTS
                        for a in range(SLOTS):
                            next_expert(e0 + a, (i + a) % SLOTS, r0 * 16 + (gate_arrival(i + a) - 16))
                    for e in range(SLOTS + SLOTS * rounds, NE):
                        n = INDEX["exp", l, e]
                        next_expert(e, n % SLOTS, gate_arrival(n))
                    i += NE - SLOTS
                    continue
                if i >= SLOTS:
                    okind, ol, oc = PLAN[i - SLOTS]
                    if okind == "exp":
                        done = sp.value_load(tab[0:1, ol, oc + 1:oc + 2], min_val=1, max_val=CHUNKS[ol])
                        sp.wait_ge(s_dn[ol], done)
                    else:
                        sp.wait_ge(*released(i - SLOTS))
                load(kind, l, c, i % SLOTS, gate_arrival(i))
                i += 1
            for t in range(2):
                sp.wait_ge(s_oe, 4 * (t + 1))
                sp.dma_start(out[0, t * P:(t + 1) * P, :], xin[:, t, :]).then_inc(s_out, 16)
            sp.wait_ge(s_out, 32)

        @block.gpsimd
        def _(pool):
            nc.gpsimd.memset(onesD[:, :], 1.0 / D)
            nc.gpsimd.memset(epst[:, :], EPS)
            nc.gpsimd.memset(ones[:, :], 1.0).then_inc(s_ones, 1)
            pool.wait_ge(s_small, 16 * 4)
            for l in range(DEPTH):
                if l >= 1:
                    pool.wait_ge(s_S[l - 1], first[l - 1][-1])
                pool.wait_ge(s_bias[l], 16)
                for h in range(4):
                    nc.gpsimd.tensor_tensor(biasm[:, h, :, :], biasm[:, h, :, :],
                                            cst[:, C_NA:C_NA + 512].rearrange("p (a k) -> p a k", a=2), ALU.add).then_inc(s_biasm[l], 1)
                if TQ[l] > SEQ:
                    for m in range(KD):
                        pool.wait_ge(ln["x"], KD * 2 * l + m + 1)
                        nc.gpsimd.tensor_scalar(hT[:, m, SEQ:TOK], xT[:, m, SEQ:TOK], modT1[:, l, SC2 + m, 1:2],
                                                modT[:, l, SH2 + m, 1:2], ALU.mult, ALU.add).then_inc(s_h2p[l], 1)
                nt = TQ[l] // P
                pool.wait_ge(s_tab[l], 1)
                if l == 0:
                    pool.wait_ge(s_fill, 16)
                pool.sem_inc(s_yfree[l], 1)
                total = pool.value_load(tab[0:1, l, T_ALL:T_ALL + 1], min_val=NE, max_val=CHUNKS[l])
                with pool.Fori(0, total) as g:
                    pool.wait_ge(s_yev[l], g * 2 + 2)
                    pool.dma_start(chunk_outs[g], yrows[0:CH, :]).then_inc(s_yw[l], 16)
                    pool.wait_ge(s_yw[l], g * 16 + 16)
                    pool.sem_inc(s_yfree[l], 1)
                for t in range(nt):
                    for a, y in ((0, y1), (1, y2)):
                        pool.indirect_dma_start(out=y[:, t, :], out_offset=None, in_=slot_outs[:, :],
                                                in_offset=bass.IndirectOffsetOnAxis(ap=pos[:, l, 4 * a + t:4 * a + t + 1], axis=0)).then_inc(s_gat[t], 16)

        @block.scalar
        def _(act):
            chain = [0]

            def link(ins):
                chain[0] += 1
                ins.then_inc(s_ach, 1)
                act.wait_ge(s_ach, chain[0])

            act.dma_start(cst[:, :], consts[:, :]).then_inc(s_small, 16)
            act.dma_start(vrow[:, :, :], vecs.rearrange("l p n -> p l n")).then_inc(s_small, 16)
            act.dma_start(rowv[:, :, :], rows.rearrange("l p n -> p l n")).then_inc(s_small, 16)
            act.dma_start(wr[:, :, :, :].rearrange("p l k n -> p (l k) n"),
                          w_route.rearrange("l (k p) n -> p (l k) n", p=P)).then_inc(s_small, 16)

            def small_weights(l):
                act.dma_start(wuq[:, :, :], w_uq[l].rearrange("(k p) n -> p k n", p=P)).then_inc(s_wqkv[l], 16)
                act.dma_start(wukv[:, :], w_ukv[l]).then_inc(s_wqkv[l], 16)

            def small_bias(l):
                act.dma_start(biasm[:, :, :, :].rearrange("p h a k -> p (h a) k"),
                              bias_na[l].rearrange("h (a p) k -> p (h a) k", p=P)).then_inc(s_bias[l], 16)

            small_weights(0)
            small_bias(0)
            act.wait_ge(s_colv, 1)
            act.activation(cT[:, :, :].rearrange("p a k -> p (a k)"), colv[:, 0, V_C:V_C + 16], ACT.Silu).then_inc(s_cT, 1)
            act.wait_ge(s_lamp, 2)
            act.activation(lams[:, 0:4], lams[:, 0:4], ACT.Exp).then_inc(s_lame, 1)

            def layer_norm_act(l, w):
                i0 = 2 * l + w
                n = TQ[l]
                for m in range(KD):
                    act.wait_ge(ln["cent"], KD * i0 + m + 1)
                    if m >= 2:
                        act.wait_ge(ln["sqs"], KD * i0 + m - 1)
                    act.activation(sqr[:, m % 2, 0:n], zT[:, m, 0:n], ACT.Square).then_inc(ln["sq"], 1)
                act.wait_ge(ln["sqs"], KD * i0 + KD)
                act.activation(rstd[:, 0:n], bank[5][:, 0:n], ACT.Sqrt, bias=epst[:, 0:1], scale=1.0 / D).then_inc(ln["std"], 1)
                g, b = (V_LN1G, V_LN1B) if w == 0 else (V_LN2G, V_LN2B)
                for m in range(KD):
                    act.wait_ge(ln["zn"], KD * i0 + m + 1)
                    act.activation(xT[:, m, 0:n], zT[:, m, 0:n], ACT.Identity, bias=colv[:, l, b + m:b + m + 1],
                                   scale=colv[:, l, g + m:g + m + 1]).then_inc(ln["x"], 1)

            def gated(l, m, src, chunk):
                ins = act.activation(zT[:, m, 0:SEQ], src[:, 0:SEQ], ACT.Copy, scale=modT[:, l, chunk + m, 0:1])
                if TQ[l] > SEQ:
                    ins = act.activation(zT[:, m, SEQ:TOK], src[:, SEQ:TOK], ACT.Copy, scale=modT[:, l, chunk + m, 1:2])
                return ins

            for l in range(DEPTH):
                n = TQ[l]
                act.wait_ge(s_modT, 3 if l == 0 else 16)
                if l == 0:
                    act.wait_ge(s_xT, KD)
                    act.wait_ge(s_ones, 1)
                else:
                    act.wait_ge(ln["x"], KD * 2 * l)
                for m in range(KD):
                    act.activation(hT[:, m, SEQ:TOK], xT[:, m, SEQ:TOK], ACT.Identity, bias=modT[:, l, SH1 + m, 1:2],
                                   scale=modT1[:, l, SC1 + m, 1:2]).then_inc(s_h1a[l], 1)
                for g, (name, i) in enumerate(GROUPS):
                    if (name, i) == ("vd", 0):
                        for j in range(3):
                            act.wait_ge(s_evd[l], NDVE[GI[("pkv", 0)] if j == 2 else GI[("pq", j)]])
                            nn = width(l, "pq") if j < 2 else TOK
                            act.activation(psq[:, j, 0:nn], praw[:, j, 0:nn], ACT.Square).then_inc(s_psq[l], 1)
                    if name not in BY_ACT:
                        continue
                    act.wait_ge(s_grp[l], g + 1)
                    w = width(l, name)
                    src = bank[g % PROJ_BANKS]
                    if name == "ssq":
                        act.activation(prstd[:, 0, 0:w], src[:, 0:w], ACT.Sqrt, bias=epst[:, 0:1], scale=1.0 / 256).then_inc(s_eva[l], 1)
                    elif name == "sskv":
                        act.activation(prstd[:, 1, 0:w], src[:, 0:w], ACT.Sqrt, bias=epst[:, 0:1], scale=1.0 / 128).then_inc(s_eva[l], 1)
                    else:
                        lo, hi = (64, 96) if name == "kr" else (0, 96) if name == "mq" else (0, 128)
                        act.activation(dest(name, i)[lo:hi, 0:w], src[lo:hi, 0:w], ACT.Copy, scale=SCALE[name]).then_inc(s_eva[l], 1)
                uf = first[l]
                vof = [v for v in range(len(units[l])) for _ in range(uf[v + 1] - uf[v])]
                if l == 0:
                    act.dma_start(slot_outs.rearrange("(p a) (c n) -> p (a c) n", p=P, n=P),
                                  onesD[:, :].unsqueeze(1).to_broadcast([P, CHUNKS[0] * CH // P * KD, P])).then_inc(s_fill, 16)
                act.wait_ge(s_grp[l], len(GROUPS))
                for v in range(len(units[l]) + 2):
                    if v < len(units[l]):
                        mixer, h, qt, k0 = units[l][v]
                        for u in range(uf[v], uf[v + 1]):
                            act.wait_ge(s_nm[l], u + 1)
                            if u >= 4:
                                act.wait_ge(s_T[l], vof[u - 4] + 1)
                            if mixer == "a":
                                act.activation(esk[:, u:u + 1], rowv[:, l, R_SINK + h:R_SINK + h + 1], ACT.Exp, bias=nmx[:, u:u + 1])
                            act.activation(Pr[:, u % 4, k0 * P:TOK], bank[u % 3][:, k0 * P:TOK], ACT.Exp, bias=nmx[:, u:u + 1],
                                           accum_out=rsum[:, u:u + 1]).then_inc(s_exp[l], 1)
                    if v >= 2:
                        t = v - 2
                        k0 = units[l][t][3]
                        act.wait_ge(s_T[l], t + 1)
                        if t >= 2:
                            act.wait_ge(s_O[l], t - 1)
                        act.activation(PTs[:, t % 2, k0 * P:TOK], bank[3 + t % 2][:, k0 * P:TOK], ACT.Copy).then_inc(s_PT[l], 1)
                if l + 1 < DEPTH:
                    small_weights(l + 1)
                    act.wait_ge(s_S[l], uf[-1])
                    small_bias(l + 1)
                act.wait_ge(s_att[l], len(units[l]))
                for j in range(2):
                    act.activation(sqr[:, j, 0:n], attnT[:, 4 + j, 0:n], ACT.Square).then_inc(s_csq[l], 1)
                for j in range(2):
                    act.wait_ge(s_css[l], j + 1)
                    act.activation(sqr[:, j, 0:n], bank[j][:, 0:n], ACT.Sqrt, bias=epst[:, 0:1]).then_inc(s_cstd[l], 1)
                act.wait_ge(s_modT, 16)
                for m in range(KD):
                    act.wait_ge(s_y[l], m + 1)
                    gated(l, m, bank[m % 4], G1).then_inc(s_yg[l], 1)
                layer_norm_act(l, 0)
                for j in range(2):
                    act.wait_ge(s_rexp[l], j + 1)
                    nn = n // P
                    if j == 0:
                        act.activation(rt[:, 0:nn, 0:4], rt[:, 0:nn, 0:4], ACT.Exp).then_inc(s_rexpd[l], 1)
                    else:
                        act.activation(rt[:, 0:nn, 100:101], rt[:, 0:nn, 100:101], ACT.Exp).then_inc(s_rexpd[l], 1)
                for q in range(2 * nn):
                    act.wait_ge(s_tok[l], q + 1)
                    act.activation(htok[:, q // 2, (q % 2) * 512:(q % 2 + 1) * 512], bank[q % 4][:, :], ACT.Copy).then_inc(s_toke[l], 1)
                act.wait_ge(s_tab[l], 1)
                total = act.value_load(tab[0:1, l, T_ALL:T_ALL + 1], min_val=NE, max_val=CHUNKS[l])
                with act.Fori(0, total) as g:
                    for f in range(2):
                        act.wait_ge(s_hg[l], g * 2 + (f + 1))
                        act.activation(sg[:, f, :], bank[1 + f][:, 0:CH], ACT.Silu).then_inc(s_sg[l], 1)
                    act.wait_ge(s_dn[l], g + 1)
                    act.wait_ge(s_yfree[l], g + 1)
                    for j in range(2):
                        act.activation(yrows[0:CH, j * 512:(j + 1) * 512], bank[3 + j][0:CH, :], ACT.Copy).then_inc(s_yev[l], 1)
                for h in range(n // SEQ):
                    for m in range(KD):
                        q = KD * h + m
                        act.wait_ge(s_yt[l], q + 1)
                        act.activation(zT[:, m, h * SEQ:(h + 1) * SEQ], bank[q % 4][:, 0:SEQ], ACT.Copy,
                                       scale=modT[:, l, G2 + m, h:h + 1]).then_inc(s_yh[l], 1)
                layer_norm_act(l, 1)

        @block.vector
        def _(dve):
            chain = [0]

            def link(ins):
                chain[0] += 1
                ins.then_inc(s_dch, 1)
                dve.wait_ge(s_dch, chain[0])

            vec = nc.vector
            for l in range(DEPTH):
                dve.wait_ge(s_vt, l + 1)
                vec.tensor_copy(colv[:, l, :], bank[l][:, 0:P]).then_inc(s_colv, 1)
            dve.wait_ge(s_small, 64)
            for l in range(DEPTH):
                lam = rowv[:, l, R_LAM:R_LAM + 128].rearrange("p (a b n) -> p a b n", a=2, b=2)
                link(vec.tensor_tensor(lamt[:, :, :], lam[:, :, 0, :], lam[:, :, 1, :], ALU.mult))
                vec.tensor_reduce(lams[:, 2 * l:2 * l + 2], lamt[:, :, :], AX, ALU.add).then_inc(s_lamp, 1)
                dve.wait_ge(s_lamp, l + 1)
                vec.tensor_scalar(nsink[:, l, :], rowv[:, l, R_SINK:R_SINK + 4], -1.0, None, ALU.mult)
            dve.wait_ge(s_lame, 1)
            dve.wait_ge(s_colv, 2)
            for l in range(DEPTH):
                lam_init = 0.8 - 0.6 * math.exp(-0.3 * l)
                link(vec.tensor_tensor(nlam[:, l:l + 1], lams[:, 2 * l + 1:2 * l + 2], lams[:, 2 * l:2 * l + 1], ALU.subtract))
                link(vec.tensor_scalar(nlam[:, l:l + 1], nlam[:, l:l + 1], -lam_init, None, ALU.add))
                link(vec.tensor_scalar(subg[:, l:l + 1], colv[:, l, V_SUB:V_SUB + 1], 1.0 - lam_init, None, ALU.mult))
            for k in range(KD):
                dve.wait_ge(s_tp, k + 1)
                vec.tensor_copy(xT[:, k, :], bank[2 + k % 2][:, :]).then_inc(s_xT, 1)

            def mod_columns(l, c):
                dve.wait_ge(s_mod, 8 * l + c + 1)
                src = mod_bank(8 * l + c)[:, 0:MOD_N * MOD_J].rearrange("p (j a n) -> p j a n", a=2, n=MOD_N // 2)[:, :, :, 0]
                cols = slice(c * MOD_J, (c + 1) * MOD_J)
                for a in range(2):
                    vec.tensor_tensor(modT[:, l, cols, a], src[:, :, a], colv[:, l, cols], ALU.add)
                    ins = vec.scalar_tensor_tensor(modT1[:, l, cols, a], src[:, :, a], 1.0, colv[:, l, cols], ALU.add, ALU.add)
                ins.then_inc(s_modT, 1)

            for c in range(3):
                mod_columns(0, c)

            def layer_norm_dve(l, w):
                i0 = 2 * l + w
                n = TQ[l]
                for m in range(KD):
                    if w == 0:
                        dve.wait_ge(s_yg[l], m + 1)
                    else:
                        dve.wait_ge(s_yh[l], KD * (n // SEQ - 1) + m + 1)
                    vec.scalar_tensor_tensor(zT[:, m, 0:n], xT[:, m, 0:n], ALPHA, zT[:, m, 0:n], ALU.mult, ALU.add).then_inc(ln["z"], 1)
                dve.wait_ge(ln["mean"], i0 + 1)
                for m in range(KD):
                    dve.wait_ge(ln["z"], KD * i0 + m + 1)
                    vec.tensor_tensor(zT[:, m, 0:n], zT[:, m, 0:n], bank[4][:, 0:n], ALU.subtract).then_inc(ln["cent"], 1)
                dve.wait_ge(ln["std"], i0 + 1)
                link(vec.reciprocal(rstd[:, 0:n], rstd[:, 0:n]))
                for m in range(KD):
                    vec.tensor_tensor(zT[:, m, 0:n], zT[:, m, 0:n], rstd[:, 0:n], ALU.mult).then_inc(ln["zn"], 1)

            for l in range(DEPTH):
                n = TQ[l]
                nt = n // P
                if l == 0:
                    dve.wait_ge(s_xT, KD)
                    dve.wait_ge(s_modT, 3)
                else:
                    dve.wait_ge(ln["x"], KD * 2 * l)
                for m in range(KD):
                    vec.tensor_scalar(hT[:, m, 0:SEQ], xT[:, m, 0:SEQ], modT1[:, l, SC1 + m, 0:1],
                                      modT[:, l, SH1 + m, 0:1], ALU.mult, ALU.add).then_inc(s_h1d[l], 1)

                def rope(r):
                    g = ROPES[r]
                    name, i = GROUPS[g]
                    lo, hi = (64, 96) if name in ("kr", "mq") else (0, 128)
                    cos, sin = (C_COS64, C_SIN64) if name in ("qa", "ka") else (C_COS32, C_SIN32)
                    d = dest(name, i)[lo:hi, 0:SEQ]
                    dve.wait_ge(s_perm[l], r + 1)
                    vec.tensor_tensor(ropet[lo:hi, r % 2, :], bank[4 + r % 2][lo:hi, 0:SEQ], cst[lo:hi, sin:sin + SEQ], ALU.mult)
                    link(vec.tensor_tensor(d, d, cst[lo:hi, cos:cos + SEQ], ALU.mult))
                    vec.tensor_tensor(d, d, ropet[lo:hi, r % 2, :], ALU.add).then_inc(s_rope[l], 1)
                    if name == "kr":
                        dve.wait_ge(s_rope[l], r + 1)
                        for h in range(1, 4):
                            vec.tensor_copy(KM[64:96, h, :], KM[64:96, 0, :])

                done = 0
                for g, (name, i) in enumerate(GROUPS):
                    if (name, i) == ("mk", 0):
                        for j in range(2):
                            w = TOK if j else n
                            dve.wait_ge(s_eva[l], NACT[GI[("sskv" if j else "ssq", 0)]])
                            link(vec.reciprocal(prstd[:, j, 0:w], prstd[:, j, 0:w]))
                        for j in range(3):
                            w = TOK if j == 2 else n
                            col = V_KVN if j == 2 else V_QN + j
                            vec.scalar_tensor_tensor(praw[:, j, 0:w], praw[:, j, 0:w], colv[:, l, col:col + 1],
                                                     prstd[:, 1 if j == 2 else 0, 0:w], ALU.mult, ALU.mult).then_inc(s_pn[l], 1)
                    if name not in BY_ACT:
                        dve.wait_ge(s_grp[l], g + 1)
                        src = bank[g % PROJ_BANKS]
                        if name == "va":
                            ins = vec.tensor_copy(V[:, :, 0:P], src[:, :].rearrange("p (t c) -> p t c", t=4))
                        elif name in ("vd", "vn", "mv"):
                            o = VOFF[{"vd": "c", "vn": "d", "mv": "b"}[name]]
                            ins = vec.tensor_copy(V[:, 2 * i:2 * i + 2, o:o + 256], src[:, :].rearrange("p (t c) -> p t c", t=2))
                        elif name in ("pq", "pkv"):
                            w = width(l, name)
                            ins = vec.tensor_copy(praw[:, i if name == "pq" else 2, 0:w], src[:, 0:w])
                        elif name == "mk":
                            ins = vec.tensor_copy(KM[0:64, i, :], src[0:64, :])
                        else:
                            ins = vec.tensor_copy(dest(name, i), src[:, :])
                        ins.then_inc(s_evd[l], 1)
                    while done < len(ROPES) and ROPES[done] + 2 <= g:
                        rope(done)
                        done += 1
                while done < len(ROPES):
                    rope(done)
                    done += 1

                uf = first[l]
                vof = [v for v in range(len(units[l])) for _ in range(uf[v + 1] - uf[v])]
                mods = [(0, c) for c in range(3, 8)] + [(1, c) for c in range(8)] if l == 0 else []
                for v in range(len(units[l]) + 3):
                    if v < len(units[l]):
                        mixer, h, qt, k0 = units[l][v]
                        for u in range(uf[v], uf[v + 1]):
                            dve.wait_ge(s_S[l], u + 1)
                            ins = vec.tensor_reduce(nmx[:, u:u + 1], bank[u % 3][:, k0 * P:TOK], AX, ALU.max, negate=True)
                            if mixer == "a":
                                link(ins)
                                ins = vec.tensor_tensor(nmx[:, u:u + 1], nmx[:, u:u + 1], nsink[:, l, h:h + 1], ALU.min)
                            ins.then_inc(s_nm[l], 1)
                    if 1 <= v <= len(units[l]):
                        mixer, h, qt, k0 = units[l][v - 1]
                        for u in range(uf[v - 1], uf[v]):
                            dve.wait_ge(s_exp[l], u + 1)
                            if mixer == "a":
                                link(vec.tensor_tensor(rsum[:, u:u + 1], rsum[:, u:u + 1], esk[:, u:u + 1], ALU.add))
                            link(vec.reciprocal(rinv[:, u:u + 1], rsum[:, u:u + 1]))
                            if u >= 4:
                                dve.wait_ge(s_T[l], vof[u - 4] + 1)
                            if mixer == "c" and u == uf[v] - 1:
                                ins = vec.tensor_scalar(diag[:, u % 4, :], ident, rinv[:, u:u + 1], nlam[:, l:l + 1], ALU.mult, ALU.mult)
                            else:
                                ins = vec.tensor_scalar(diag[:, u % 4, :], ident, rinv[:, u:u + 1], None, ALU.mult)
                            ins.then_inc(s_dg[l], 1)
                    if v >= 3:
                        t = v - 3
                        mixer, h, qt, k0 = units[l][t]
                        dve.wait_ge(s_O[l], t + 1)
                        lo = 64 * (h % 2)
                        ch = 2 * "abcd".index(mixer) + h // 2
                        vec.tensor_copy(attnT[lo:lo + 64, ch, qt * P:(qt + 1) * P], bank[5 + t % 2][lo:lo + 64, 0:P]).then_inc(s_att[l], 1)
                    if mods and v % 4 == 3:
                        mod_columns(*mods.pop(0))
                assert not mods

                for j in range(2):
                    dve.wait_ge(s_cstd[l], j + 1)
                    link(vec.reciprocal(sqr[:, j, 0:n], sqr[:, j, 0:n]))
                    vec.scalar_tensor_tensor(attnT[:, 4 + j, 0:n], attnT[:, 4 + j, 0:n], subg[:, l:l + 1], sqr[:, j, 0:n],
                                             ALU.mult, ALU.mult).then_inc(s_cn[l], 1)
                layer_norm_dve(l, 0)
                for m in range(KD):
                    dve.wait_ge(ln["x"], KD * 2 * l + m + 1)
                    vec.tensor_scalar(hT[:, m, 0:SEQ], xT[:, m, 0:SEQ], modT1[:, l, SC2 + m, 0:1],
                                      modT[:, l, SH2 + m, 0:1], ALU.mult, ALU.add).then_inc(s_h2d[l], 1)

                dve.wait_ge(s_lg[l], 1)
                for t in range(nt):
                    vec.tensor_tensor(lg[:, t, :], bank[6][:, 36 * t:36 * (t + 1)], rowv[:, l, R_RB:R_RB + 36], ALU.add).then_inc(s_dch, 1)
                    chain[0] += 1
                dve.wait_ge(s_dch, chain[0])

                def col(i):
                    return rt[:, 0:nt, i:i + 1]

                def bc(i, k):
                    return rt[:, 0:nt, i:i + 1].to_broadcast([P, nt, k])

                def first_max(src, k, m, one):
                    iota = cst[:, C_IOTA:C_IOTA + k]
                    link(vec.tensor_reduce(col(m), src, AX, ALU.max))
                    link(vec.tensor_tensor(rt[:, 0:nt, one:one + k], src, bc(m, k), ALU.is_equal))
                    for t in range(nt):
                        link(vec.tensor_tensor(rt[:, t, one:one + k], rt[:, t, one:one + k], iota, ALU.mult))
                    link(vec.tensor_reduce(col(99), rt[:, 0:nt, one:one + k], AX, ALU.max))
                    link(vec.tensor_tensor(rt[:, 0:nt, one:one + k], rt[:, 0:nt, one:one + k], bc(99, k), ALU.is_equal))

                first_max(lg[:, 0:nt, 0:4], 4, 96, 8)
                vec.tensor_tensor(rt[:, 0:nt, 0:4], lg[:, 0:nt, 0:4], bc(96, 4), ALU.subtract).then_inc(s_rexp[l], 1)
                for t in range(nt):
                    prod = rt[:, t, 64:96].rearrange("p (g e) -> p g e", g=4)
                    one = rt[:, t, 8:12].unsqueeze(2).to_broadcast([P, 4, 8])
                    link(vec.tensor_tensor(prod, lg[:, t, 4:36].rearrange("p (g e) -> p g e", g=4), one, ALU.mult))
                    link(vec.tensor_reduce(rt[:, t, 24:32], rt[:, t, 64:96].rearrange("p (g e) -> p e g", g=4), AX, ALU.add))
                first_max(rt[:, 0:nt, 24:32], 8, 97, 40)
                link(vec.scalar_tensor_tensor(rt[:, 0:nt, 32:40], rt[:, 0:nt, 40:48], NEG, rt[:, 0:nt, 24:32], ALU.mult, ALU.add))
                first_max(rt[:, 0:nt, 32:40], 8, 98, 48)
                vec.tensor_tensor(col(100), col(98), col(97), ALU.subtract).then_inc(s_rexp[l], 1)
                dve.wait_ge(s_rexpd[l], 2)
                link(vec.tensor_reduce(col(101), rt[:, 0:nt, 0:4], AX, ALU.add))
                link(vec.reciprocal(col(101), col(101)))
                link(vec.tensor_scalar(col(102), col(100), 1.0, None, ALU.add))
                link(vec.reciprocal(col(102), col(102)))
                link(vec.tensor_tensor(col(102), col(102), col(101), ALU.mult))
                link(vec.tensor_tensor(col(103), col(102), col(100), ALU.mult))
                for a in range(2):
                    vec.tensor_copy(gate[:, l, 4 * a:4 * a + nt], rt[:, 0:nt, 102 + a])
                for a in range(2):
                    for t in range(nt):
                        ins = vec.tensor_tensor(oh[a][:, t, :].rearrange("p (g e) -> p g e", g=4),
                                                rt[:, t, 8:12].unsqueeze(2).to_broadcast([P, 4, 8]),
                                                rt[:, t, 40 + 8 * a:48 + 8 * a].unsqueeze(1).to_broadcast([P, 4, 8]), ALU.mult)
                link(ins)
                vec.tensor_tensor(oh[2][:, 0:nt, :], oh[0][:, 0:nt, :], oh[1][:, 0:nt, :], ALU.add).then_inc(s_mask[l], 1)
                dve.wait_ge(s_cnt[l], 1)
                link(vec.tensor_copy(nch[0:NE, 0:1], bank[5][0:NE, 0:1]))
                link(vec.tensor_tensor(rt[0:NE, 0, 56:64], cst[0:NE, C_THR:C_THR + 8], nch[0:NE, 0:1].to_broadcast([NE, 8]), ALU.is_lt))
                link(vec.tensor_reduce(nch[0:NE, 1:2], rt[0:NE, 0, 56:64], AX, ALU.add))
                vec.tensor_scalar(nrep[0:NE, :], ones[0:NE, :], nch[0:NE, 1:2], None, ALU.mult).then_inc(s_nch[l], 1)
                dve.wait_ge(s_pos[l], 1)
                src = bank[6][:, 0:NE * nt].rearrange("p (t e) -> p t e", t=nt)
                for a in range(2):
                    link(vec.tensor_tensor(oh[a][:, 0:nt, :], oh[a][:, 0:nt, :], src, ALU.mult))
                    link(vec.tensor_reduce(posp[:, 0:nt, a:a + 1], oh[a][:, 0:nt, :], AX, ALU.add))
                    link(vec.tensor_copy(pos[:, l, 4 * a:4 * a + nt], posp[:, 0:nt, a]))
                vec.tensor_copy(tab[:, l, :], bank[7][:, 0:65]).then_inc(s_tab[l], 1)

                dve.wait_ge(s_tab[l], 1)
                total = dve.value_load(tab[0:1, l, T_ALL:T_ALL + 1], min_val=NE, max_val=CHUNKS[l])

                def picks(chunk_done):
                    for t in range(nt):
                        ins = vec.tensor_scalar(pick2[:, t, :], cst[:, C_SLOT:C_SLOT + CH], prel[:, 4 + t:5 + t], None, ALU.is_equal)
                    ins.then_inc(s_prel[l], 1)
                    dve.wait_ge(s_prel[l], chunk_done * 2 + 1)
                    for t in range(nt):
                        ins = vec.scalar_tensor_tensor(pick[:, t, :], cst[:, C_SLOT:C_SLOT + CH], prel[:, t:t + 1], pick2[:, t, :],
                                                       ALU.is_equal, ALU.add)
                    ins.then_inc(s_pick[l], 1)
                    dve.wait_ge(s_pick[l], chunk_done + 1)
                    vec.tensor_scalar(prel[:, :], prel[:, :], float(-CH), None, ALU.add).then_inc(s_prel[l], 1)
                    dve.wait_ge(s_prel[l], chunk_done * 2 + 2)

                for a in range(2):
                    ins = vec.tensor_copy(prel[:, 4 * a:4 * a + nt], posp[:, 0:nt, a])
                    if nt < 4:
                        vec.memset(prel[:, 4 * a + nt:4 * a + 4], 0.0)
                link(ins)
                picks(0)
                dve.wait_ge(s_xt[l], 1)
                vec.tensor_copy(xcols[:, :, :].rearrange("p k c -> p (k c)"), bank[0][:, :]).then_inc(s_xc[l], 1)
                picks(1)
                with dve.Fori(0, total) as g:
                    for f in range(2):
                        dve.wait_ge(s_sg[l], g * 2 + (f + 1))
                        vec.tensor_tensor(hid[:, f, :], sg[:, f, :], bank[1 + f][:, CH:2 * CH], ALU.mult).then_inc(s_hid[l], 1)
                    dve.wait_ge(s_xt[l], g + 2)
                    vec.tensor_copy(xcols[:, :, :].rearrange("p k c -> p (k c)"), bank[0][:, :]).then_inc(s_xc[l], 1)
                    picks(g + 2)
                for t in range(nt):
                    dve.wait_ge(s_gat[t], 32 * (l + 1))
                    link(vec.tensor_scalar(y1[:, t, :], y1[:, t, :], gate[:, l, t:t + 1], None, ALU.mult))
                    vec.scalar_tensor_tensor(y1[:, t, :], y2[:, t, :], gate[:, l, 4 + t:5 + t], y1[:, t, :], ALU.mult, ALU.add).then_inc(s_cmb[l], 1)
                layer_norm_dve(l, 1)

            for t in range(2):
                for j in range(4):
                    q = 4 * t + j
                    dve.wait_ge(s_ot, q + 1)
                    vec.tensor_copy(xin[:, t, 256 * j:256 * (j + 1)], bank[q % 2][:, 0:256]).then_inc(s_oe, 1)

        @block.tensor
        def _(pe):
            mm = nc.tensor.matmul
            pe.wait_ge(s_small, 64)
            for l in range(DEPTH):
                nc.tensor.transpose(bank[l][:, 0:P], vrow[:, l, :], ident).then_inc(s_vt, 1)
            pe.wait_ge(s_xin, 32)
            for k in range(KD):
                if k >= 2:
                    pe.wait_ge(s_xT, k - 1)
                for t in range(4):
                    ins = nc.tensor.transpose(bank[2 + k % 2][:, t * P:(t + 1) * P], xin[:, t, k * P:(k + 1) * P], ident)
                ins.then_inc(s_tp, 1)

            def arrived(i):
                s, n = arrival(i)
                pe.wait_ge(w_here[s], n)
                return slots[:, s, :]

            def modulation(l, c):
                w = arrived(INDEX["mod", l, c]).rearrange("p (k n) -> p k n", k=KD)
                if 8 * l + c >= 3:
                    pe.wait_ge(s_modT, 8 * l + c)
                elif c == 2:
                    pe.wait_ge(s_modT, 1)
                for j in range(MOD_J):
                    for k in range(KD):
                        ins = mm(mod_bank(8 * l + c)[:, MOD_N * j:MOD_N * (j + 1)], w[:, k, j * P:(j + 1) * P],
                                 cT[:, :, k].unsqueeze(2).to_broadcast([P, 2, MOD_N // 2]), start=(k == 0), stop=(k == KD - 1))
                ins.then_inc(s_mod, 1)

            def layer_norm_pe(l, w):
                i0 = 2 * l + w
                n = TQ[l]
                for m in range(KD):
                    pe.wait_ge(ln["z"], KD * i0 + m + 1)
                    ins = mm(bank[4][:, 0:n], onesD[:, :], zT[:, m, 0:n], start=(m == 0), stop=(m == KD - 1))
                ins.then_inc(ln["mean"], 1)
                for m in range(KD):
                    pe.wait_ge(ln["sq"], KD * i0 + m + 1)
                    mm(bank[5][:, 0:n], ones[:, :], sqr[:, m % 2, 0:n], start=(m == 0), stop=(m == KD - 1)).then_inc(ln["sqs"], 1)

            def projection(l, g, w):
                name, i = GROUPS[g]
                o = bank[g % PROJ_BANKS]
                n = width(l, name)

                def features(lhs, out, rhs_n):
                    for k in range(KD):
                        ins = mm(out, lhs(k), hT[:, k, 0:rhs_n], start=(k == 0), stop=(k == KD - 1))
                    return ins

                def tokens(c0, nc_, tiles):
                    for a, t in enumerate(tiles):
                        for k in range(KD):
                            ins = mm(o[:, a * nc_:(a + 1) * nc_], hT[:, k, t * P:(t + 1) * P], w[:, k, c0:c0 + nc_],
                                     start=(k == 0), stop=(k == KD - 1))
                    return ins

                if name == "qa":
                    return features(lambda k: w[:, k, 128 * i:128 * (i + 1)], o[:, 0:n], n)
                if name == "ka":
                    return features(lambda k: w[:, k, 256:384], o[:, :], n)
                if name == "va":
                    return tokens(384, P, range(4))
                if name in ("pq", "pkv"):
                    c0 = 128 * i if name == "pq" else 256
                    return features(lambda k: w[:, k, c0:c0 + 128], o[:, 0:n], n)
                if name == "kr":
                    return features(lambda k: w[:, k, 384:416], o[64:96, 0:n], n)
                if name in ("qd", "kd", "qn", "kn"):
                    c0 = (0 if name[0] == "q" else 256) + 128 * i
                    return features(lambda k: w[:, k, c0:c0 + 128], o[:, 0:n], n)
                if name in ("vd", "vn"):
                    return tokens(512, 256, (2 * i, 2 * i + 1))
                if name == "ssq":
                    mm(o[:, 0:n], ones[:, :], psq[:, 0, 0:n], start=True, stop=False)
                    return mm(o[:, 0:n], ones[:, :], psq[:, 1, 0:n], start=False, stop=True)
                if name == "sskv":
                    return mm(o[:, :], ones[:, :], psq[:, 2, :], start=True, stop=True)
                if name == "mk":
                    return mm(o[0:64, :], wukv[:, i * P:i * P + 64], praw[:, 2, :], start=True, stop=True)
                if name == "mv":
                    for a in range(2):
                        t = 2 * i + a
                        ins = mm(o[:, a * 256:(a + 1) * 256], praw[:, 2, t * P:(t + 1) * P],
                                 wukv[:, :].rearrange("p (h a c) -> p h a c", h=4, a=2)[:, :, 1, :], start=True, stop=True)
                    return ins
                mm(o[0:96, 0:n], wuq[:, 0, 96 * i:96 * (i + 1)], praw[:, 0, 0:n], start=True, stop=False)
                return mm(o[0:96, 0:n], wuq[:, 1, 96 * i:96 * (i + 1)], praw[:, 1, 0:n], start=False, stop=True)

            def permute(l, r):
                g = ROPES[r]
                name, i = GROUPS[g]
                lo, hi = (64, 96) if name in ("kr", "mq") else (0, 128)
                c = C_P16 if name in ("qa", "ka") else C_P8
                pe.wait_ge(s_eva[l], NACT[g])
                if r >= 2:
                    pe.wait_ge(s_rope[l], r - 1)
                mm(bank[4 + r % 2][lo:hi, 0:SEQ], cst[lo:hi, c + lo:c + hi], dest(name, i)[lo:hi, 0:SEQ],
                   start=True, stop=True).then_inc(s_perm[l], 1)

            pe.wait_ge(s_cT, 1)
            pe.wait_ge(s_ones, 1)
            for c in range(3):
                modulation(0, c)

            for l in range(DEPTH):
                n = TQ[l]
                nt = n // P
                pe.wait_ge(s_h1a[l], KD)
                pe.wait_ge(s_h1d[l], KD)
                part = None
                done = 0
                for g, (name, i) in enumerate(GROUPS):
                    if PART_OF.get(name) is not None and PART_OF[name] != part:
                        part = PART_OF[name]
                        w = arrived(INDEX["in", l, part])[:, 0:KD * IN_PARTS[part][1]].rearrange("p (k n) -> p k n", k=KD)
                    if g >= PROJ_BANKS:
                        old = g - PROJ_BANKS
                        if GROUPS[old][0] in BY_ACT:
                            pe.wait_ge(s_eva[l], NACT[old])
                        else:
                            pe.wait_ge(s_evd[l], NDVE[old])
                    if name == "ssq":
                        pe.wait_ge(s_psq[l], 3)
                    if (name, i) == ("mk", 0):
                        pe.wait_ge(s_wqkv[l], 32)
                        pe.wait_ge(s_pn[l], 3)
                    projection(l, g, w).then_inc(s_grp[l], 1)
                    while done < len(ROPES) and ROPES[done] + 2 <= g:
                        permute(l, done)
                        done += 1
                while done < len(ROPES):
                    permute(l, done)
                    done += 1

                uf = first[l]
                mods = [(0, c) for c in range(3, 8)] + [(1, c) for c in range(8)] if l == 0 else []
                pe.wait_ge(s_rope[l], len(ROPES))
                pe.wait_ge(s_eva[l], NACT[-1])
                pe.wait_ge(s_evd[l], NDVE[-1])
                for v in range(len(units[l]) + 3):
                    if v < len(units[l]):
                        mixer, h, qt, k0 = units[l][v]
                        q = slice(qt * P, (qt + 1) * P)
                        for u in range(uf[v], uf[v + 1]):
                            if u >= 3:
                                pe.wait_ge(s_exp[l], u - 2)
                            if mixer == "a":
                                lo, k = 64 * (h // 2), 64
                                qs, ks = QA[lo:lo + k, h % 2, q], KA[lo:lo + k, k0 * P:TOK]
                            elif mixer == "b":
                                qs, ks = QM[0:96, h, q], KM[0:96, h, k0 * P:TOK]
                            elif mixer == "c":
                                lo, k = 64 * (h % 2) + 32 * (u - uf[v]), 32
                                qs, ks = QDf[lo:lo + k, h // 2, q], KDf[lo:lo + k, h // 2, k0 * P:TOK]
                            else:
                                lo, k = 64 * (h % 2), 64
                                qs, ks = QN[lo:lo + k, h // 2, q], KN[lo:lo + k, h // 2, k0 * P:TOK]
                            more = mixer in "ad" and k0 == 0
                            ins = mm(bank[u % 3][:, k0 * P:TOK], qs, ks, start=True, stop=not more)
                            if more:
                                if mixer == "a":
                                    extra = cst[:, C_SWA + SEQ * qt:C_SWA + SEQ * (qt + 1)]
                                else:
                                    pe.wait_ge(s_biasm[l], 4)
                                    extra = biasm[:, h, qt, :]
                                ins = mm(bank[u % 3][:, 0:SEQ], ident, extra, start=False, stop=True)
                            ins.then_inc(s_S[l], 1)
                    if 2 <= v < len(units[l]) + 2:
                        t = v - 2
                        k0 = units[l][t][3]
                        pe.wait_ge(s_dg[l], uf[t + 1])
                        if t >= 2:
                            pe.wait_ge(s_PT[l], t - 1)
                        for kt in range(k0, 4):
                            for u in range(uf[t], uf[t + 1]):
                                ins = mm(bank[3 + t % 2][:, kt * P:(kt + 1) * P], Pr[:, u % 4, kt * P:(kt + 1) * P], diag[:, u % 4, :],
                                         start=(u == uf[t]), stop=(u == uf[t + 1] - 1))
                        ins.then_inc(s_T[l], 1)
                    if v >= 3:
                        t = v - 3
                        mixer, h, qt, k0 = units[l][t]
                        pe.wait_ge(s_PT[l], t + 1)
                        if t >= 2:
                            pe.wait_ge(s_att[l], t - 1)
                        lo = 64 * (h % 2)
                        c0 = VOFF[mixer] + 64 * (h // 2 if mixer == "a" else h)
                        for kt in range(k0, 4):
                            ins = mm(bank[5 + t % 2][lo:lo + 64, 0:P], V[:, kt, c0:c0 + 64], PTs[:, t % 2, kt * P:(kt + 1) * P],
                                     start=(kt == k0), stop=(kt == 3))
                        ins.then_inc(s_O[l], 1)
                    if mods and v % 4 == 3:
                        modulation(*mods.pop(0))
                for j in range(2):
                    pe.wait_ge(s_csq[l], j + 1)
                    mm(bank[j][:, 0:n], cst[:, C_BLK:C_BLK + P], sqr[:, j, 0:n], start=True, stop=True).then_inc(s_css[l], 1)
                pe.wait_ge(s_att[l], len(units[l]))
                pe.wait_ge(s_cn[l], 2)
                for m in range(KD):
                    w = arrived(INDEX["out", l, m // 4])[:, 0:KD * 512].rearrange("p (k n) -> p k n", k=KD)
                    if m >= 4:
                        pe.wait_ge(s_yg[l], m - 3)
                    for k in range(KD):
                        ins = mm(bank[m % 4][:, 0:n], w[:, k, (m % 4) * P:(m % 4 + 1) * P], attnT[:, k, 0:n],
                                 start=(k == 0), stop=(k == KD - 1))
                    ins.then_inc(s_y[l], 1)
                layer_norm_pe(l, 0)
                pe.wait_ge(s_h2d[l], KD)
                if n > SEQ:
                    pe.wait_ge(s_h2p[l], KD)
                for t in range(nt):
                    for k in range(KD):
                        ins = mm(bank[6][:, 36 * t:36 * (t + 1)], hT[:, k, t * P:(t + 1) * P], wr[:, l, k, :],
                                 start=(k == 0), stop=(k == KD - 1))
                ins.then_inc(s_lg[l], 1)
                for q in range(2 * nt):
                    if q >= 4:
                        pe.wait_ge(s_toke[l], q - 3)
                    for a in range(4):
                        ins = nc.tensor.transpose(bank[q % 4][:, a * P:(a + 1) * P], hT[:, 4 * (q % 2) + a, (q // 2) * P:(q // 2 + 1) * P], ident)
                    ins.then_inc(s_tok[l], 1)
                pe.wait_ge(s_mask[l], 1)
                for t in range(nt):
                    ins = mm(bank[5][0:NE, 0:P], oh[2][:, t, :], ones[:, :], start=(t == 0), stop=(t == nt - 1))
                ins.then_inc(s_cnt[l], 1)
                pe.wait_ge(s_nch[l], 1)
                for t in range(nt):
                    o = bank[6][:, NE * t:NE * (t + 1)]
                    mm(o, cst[:, C_UP:C_UP + P], oh[2][:, t, :], start=True, stop=False)
                    for b in range(t):
                        mm(o, ones[:, :], oh[2][:, b, :], start=False, stop=False)
                    mm(o, nrep[0:NE, :], cst[0:NE, C_UP64:C_UP64 + NE], start=False, stop=True)
                mm(bank[7][:, 0:65], nrep[0:NE, :], cst[0:NE, C_UPX:C_UPX + 65], start=True, stop=True).then_inc(s_pos[l], 1)

                def columns(g):
                    pe.wait_ge(s_pick[l], g + 1)
                    for k in range(KD):
                        for t in range(nt):
                            ins = mm(bank[0][:, k * CH:(k + 1) * CH], htok[:, t, k * P:(k + 1) * P], pick[:, t, :],
                                     start=(t == 0), stop=(t == nt - 1))
                    ins.then_inc(s_xt[l], 1)

                def expert(e, slot, here, gate_here):
                    first_g = pe.value_load(tab[0:1, l, bass.ds(e + T_FIRST, 1)], min_val=0, max_val=CHUNKS[l])
                    count = pe.value_load(tab[0:1, l, bass.ds(e + T_N, 1)], min_val=1, max_val=1 + 2 * TOK // CH)
                    w = slots[:, slot, :]
                    wd = w[:, 4096:6144].rearrange("p (k d) -> p k d", k=2)
                    with pe.Fori(0, count) as j:
                        g = first_g + j
                        pe.wait_ge(w_here[slot], here)
                        pe.wait_ge(g_here[slot], gate_here)
                        pe.wait_ge(s_xc[l], g + 1)
                        for f in range(2):
                            for a in range(2):
                                wj = w[:, 2048 * a:2048 * (a + 1)].rearrange("p (k f) -> p k f", k=KD)
                                for k in range(KD):
                                    ins = mm(bank[1 + f][:, a * CH:(a + 1) * CH], wj[:, k, f * P:(f + 1) * P], xcols[:, k, :],
                                             start=(k == 0), stop=(k == KD - 1))
                            ins.then_inc(s_hg[l], 1)
                        columns(g + 1)
                        pe.wait_ge(s_hid[l], g * 2 + 2)
                        for c in range(2):
                            for f in range(2):
                                ins = mm(bank[3 + c][0:CH, :], hid[:, f, :], wd[:, f, c * 512:(c + 1) * 512], start=(f == 0), stop=(f == 1))
                        ins.then_inc(s_dn[l], 1)

                pe.wait_ge(s_tab[l], 1)
                pe.wait_ge(s_toke[l], 2 * nt)
                columns(0)
                base = INDEX["exp", l, 0]
                rounds = NE // SLOTS
                with pe.Fori(0, rounds) as r0:
                    for a in range(SLOTS):
                        slot, here = arrival(base + a)
                        expert(r0 * SLOTS + a, slot, r0 * (16 * DMAS["exp"]) + here, r0 * 16 + gate_arrival(base + a))
                for e in range(SLOTS * rounds, NE):
                    expert(e, *arrival(base + e), gate_arrival(base + e))
                for h in range(n // SEQ):
                    pe.wait_ge(s_cmb[l], 2 * (h + 1))
                    for m in range(KD):
                        q = KD * h + m
                        if q >= 4:
                            pe.wait_ge(s_yh[l], q - 3)
                        for a in range(2):
                            ins = nc.tensor.transpose(bank[q % 4][:, a * P:(a + 1) * P], y1[:, 2 * h + a, m * P:(m + 1) * P], ident)
                        ins.then_inc(s_yt[l], 1)
                layer_norm_pe(l, 1)
            pe.wait_ge(ln["x"], KD * 2 * DEPTH)
            for q in range(8):
                if q >= 2:
                    pe.wait_ge(s_oe, q - 1)
                t, j = q // 4, q % 4
                for a in range(2):
                    ins = nc.tensor.transpose(bank[q % 2][:, a * P:(a + 1) * P], xT[:, 2 * j + a, t * P:(t + 1) * P], ident)
                ins.then_inc(s_ot, 1)


def shape_constants():
    import numpy as np
    c = np.zeros((P, C_ALL), np.float32)
    p = np.arange(P)
    c[p, C_ID + p] = 1
    c[p, C_P16 + (p ^ 16)] = 1
    c[p, C_P8 + (p ^ 8)] = 1
    c[:, C_BLK:C_BLK + P] = (p[:, None] // 64 == p[None] // 64) / 64.0
    t = np.arange(SEQ)
    for width, o_cos, o_sin in ((64, C_COS64, C_SIN64), (32, C_COS32, C_SIN32)):
        r, half = width // 2, width // 4
        inv = (np.float32(10000.0) ** (-np.arange(half, dtype=np.float32) / np.float32(half))).astype(np.float32)
        d = p % width
        pos = np.where((d < r)[:, None], (t // GRID_W)[None], (t % GRID_W)[None]).astype(np.float32)
        ang = pos * inv[d % half][:, None]
        c[:, o_cos:o_cos + SEQ] = np.cos(ang)
        c[:, o_sin:o_sin + SEQ] = np.sin(ang) * np.where(d % r < half, -1.0, 1.0)[:, None]
    q = np.arange(SEQ).reshape(2, P).T[:, :, None]
    k = t[None, None, :]
    c[:, C_SWA:C_SWA + 512] = np.where(np.abs(k - q) <= 128, 0, NEG).reshape(P, 512)
    start = np.clip(q % GRID_W - 8, 0, GRID_W - 16)
    c[:, C_NA:C_NA + 512] = np.where((k % GRID_W >= start) & (k % GRID_W < start + 16), 0, NEG).reshape(P, 512)
    c[:, C_IOTA:C_IOTA + 16] = 16 - np.arange(16)
    c[:, C_UP:C_UP + P] = p[:, None] < p[None]
    e = np.arange(NE)
    c[0:NE, C_UPX:C_UPX + NE + 1] = e[:, None] < np.arange(NE + 1)[None]
    c[0:NE, C_UPX + T_N:C_UPX + T_N + NE] = np.eye(NE)
    c[0:NE, C_UP64:C_UP64 + NE] = CH * (e[:, None] < e[None])
    c[:, C_THR:C_THR + 8] = [-1] + [CH * a for a in range(1, 8)]
    c[:, C_SLOT:C_SLOT + CH] = np.arange(CH)
    return c


def kernel(**inputs):
    import numpy as np
    import concourse.bacc as bacc
    from concourse.bass_utils import run_bass_kernel_spmd

    a = {k: np.asarray(v) for k, v in inputs.items()}
    def r128(v):
        return v.reshape(DEPTH, -1, P)
    both = np.stack([np.concatenate([a["c"].reshape(KD, P), a["c_ctx"].reshape(KD, P)])] * DEPTH)
    sub = np.concatenate([a["diff_subln"], a["diff_subln"]], -1).reshape(DEPTH, 1, P)
    vecs = np.concatenate([r128(a["b_mod"]), r128(a["ln1_g"]), r128(a["ln1_b"]), r128(a["ln2_g"]), r128(a["ln2_b"]),
                           r128(a["mla_q_norm"]), r128(a["mla_kv_norm"]), sub, both, np.zeros((DEPTH, P - 100, P), np.float32)], 1)
    rows = np.concatenate([a["attn_sink"], a["lam_q1"], a["lam_k1"], a["lam_q2"], a["lam_k2"], a["b_group"], a["b_router"]], -1)
    rows = np.ascontiguousarray(np.broadcast_to(rows[:, None, :], (DEPTH, P, R_ALL)))
    w = a["w_in"]
    w_in = np.concatenate([w[:, :, 0:64], w[:, :, 128:192], w[:, :, 64:128], w[:, :, 192:]], -1)
    t = np.arange(SEQ)
    row_off = (t[None] // GRID_W) - (t[:, None] // GRID_W) + 7
    col_off = np.clip((t[None] % GRID_W) - (t[:, None] % GRID_W) + 15, 0, 30)
    bias = a["na_rpb"][:, :, row_off, col_off]
    ins = {
        "x": a["x"], "ctx": a["ctx"], "w_mod": a["w_mod"], "w_in": w_in, "w_uq": a["w_uq"], "w_ukv": a["w_ukv"],
        "w_out": a["w_out"], "w_route": np.concatenate([a["w_group"], a["w_router"]], -1),
        "w_gate": a["w_gate"], "w_up": a["w_up"], "w_down": a["w_down"],
        "vecs": vecs, "rows": rows, "bias_na": bias, "consts": shape_constants(),
    }
    nc = bacc.Bacc("TRN2", target_bir_lowering=False, num_devices=1)
    arrays, args = {}, []
    for name, v in ins.items():
        v = np.ascontiguousarray(v)
        arrays[f"in_{name}"] = v
        args.append(nc.dram_tensor(f"in_{name}", v.shape, mybir.dt.from_np(v.dtype), kind="ExternalInput").ap())
    args.append(nc.dram_tensor("out_0", (1, SEQ, D), F32, kind="ExternalOutput").ap())
    build(nc, *args)
    r = run_bass_kernel_spmd(nc, [arrays], core_ids=[0])
    return r.results[0]["out_0"]
```

```python
import math
from contextlib import ExitStack

import concourse.bass as bass
from concourse import mybir

P = 128
D = 1024
KD = D // P
SEQ = 256
CTX = 256
TOK = SEQ + CTX
DEPTH = 2
D_IN = 2464
GRID_W = 64
NE = 32
FH = 256
ALPHA = (2 * DEPTH) ** 0.25
EPS = 1e-5
NEG = -1e30

F32 = mybir.dt.float32
BF16 = mybir.dt.bfloat16
ALU = mybir.AluOpType
ACT = mybir.ActivationFunctionType
AX = mybir.AxisListType.X

CH = 64

C_ID, C_P16, C_P8, C_BLK = 0, 128, 256, 384
C_COS64, C_SIN64, C_COS32, C_SIN32 = 512, 768, 1024, 1280
C_SWA, C_NA = 1536, 2048
C_IOTA = 2560
C_UP = C_IOTA + 16
C_UPX = C_UP + P
C_UP64 = C_UPX + 65
C_THR = C_UP64 + 32
C_SLOT = C_THR + 8
C_ALL = C_SLOT + CH

V_MOD, V_LN1G, V_LN1B, V_LN2G, V_LN2B, V_QN, V_KVN, V_SUB, V_C, V_CC = 0, 48, 56, 64, 72, 80, 82, 83, 84, 92
R_SINK, R_LAM, R_RB = 0, 4, 132
R_ALL = 168
SH1, SC1, G1, SH2, SC2, G2 = 0, 8, 16, 24, 32, 40

MOD_COLS = 768
MOD_J = MOD_COLS // P
IN_PARTS = [(0, 512), (512, 416), (928, 768), (1696, 768)]
SLOT = 6144
SLOTS = 3
EXTRA = SLOTS

CHUNKS = [NE + 2 * TOK // CH, NE + 2 * SEQ // CH]
T_FIRST, T_ALL, T_N = 0, NE, NE + 1


def load_plan():
    plan = [("mod", 0, c) for c in range(3)] + [("in", 0, c) for c in range(4)]
    plan += [("mod", 0, c) for c in range(3, 8)] + [("mod", 1, c) for c in range(8)]
    experts = [e for e in range(NE) if e != EXTRA]
    plan += [("out", 0, c) for c in range(2)] + [("exp", 0, e) for e in experts]
    plan += [("in", 1, c) for c in range(4)] + [("out", 1, c) for c in range(2)] + [("exp", 1, e) for e in experts]
    return plan


PLAN = load_plan()
INDEX = {w: i for i, w in enumerate(PLAN)}
DMAS = {"mod": 1, "in": 1, "out": 1, "exp": 2}


def arrival(i):
    return i % SLOTS, 16 * sum(DMAS[PLAN[j][0]] for j in range(i % SLOTS, i + 1, SLOTS))


def gate_arrival(i):
    return 16 * sum(PLAN[j][0] == "exp" for j in range(i % SLOTS, i + 1, SLOTS))


def attention_units(l):
    def of(mixer):
        return [[(mixer, h, qt, 0 if qt < 2 else 2) for h in (2 * pair, 2 * pair + 1)]
                for pair in range(2) for qt in range(4 if l == 0 else 2)]

    pairs = [p for both in zip(of("a"), of("c")) for p in both] + of("b") + of("d")
    return [u for p in pairs for u in p]


GROUPS = [
    ("qa", 0), ("qa", 1), ("ka", 0), ("va", 0),
    ("pq", 0), ("pq", 1), ("pkv", 0), ("kr", 0),
    ("qd", 0), ("qd", 1), ("kd", 0), ("kd", 1), ("vd", 0), ("vd", 1),
    ("ssq", 0), ("sskv", 0),
    ("qn", 0), ("qn", 1), ("kn", 0), ("kn", 1), ("vn", 0), ("vn", 1),
    ("mq", 0), ("mq", 1), ("mq", 2), ("mq", 3),
    ("mk", 0), ("mk", 1), ("mk", 2), ("mk", 3), ("mv", 0), ("mv", 1),
]
ROPED = ("qa", "ka", "kr", "qd", "kd", "mq")
BY_ACT = ROPED + ("ssq", "sskv", "qn")
LAST_OF_PART = {("va", 0): 0, ("kr", 0): 1, ("vd", 1): 2, ("vn", 1): 3}
PART_OF = {"qa": 0, "ka": 0, "va": 0, "pq": 1, "pkv": 1, "kr": 1, "qd": 2, "kd": 2, "vd": 2, "qn": 3, "kn": 3, "vn": 3}
NACT = [sum(n in BY_ACT for n, _ in GROUPS[:g + 1]) for g in range(len(GROUPS))]
NDVE = [sum(n not in BY_ACT for n, _ in GROUPS[:g + 1]) for g in range(len(GROUPS))]
ROPES = [g for g, (n, _) in enumerate(GROUPS) if n in ROPED]
GI = {g: i for i, g in enumerate(GROUPS)}
SCALE = {"qa": 64 ** -0.5, "ka": 1.0, "kr": 1.0, "qd": 32 ** -0.5, "kd": 1.0, "mq": 96 ** -0.5, "qn": 64 ** -0.5}
PROJ_BANKS = 4
RING = 16


def build(nc, x, ctx_in, w_mod, w_in, w_uq, w_ukv, w_out, w_route, w_gate, w_up, w_down, vecs, rows, bias_na, consts, out):
    with ExitStack() as st:
        def sb(name, shape):
            return st.enter_context(nc.sbuf_tensor(name, shape, F32))

        def sem(name):
            return st.enter_context(nc.semaphore(name))

        def per_layer(name):
            return [sem(f"{name}_{l}") for l in range(DEPTH)]

        TQ = [TOK, SEQ]
        xT = sb("xT", [P, KD, TOK])
        hT = sb("hT", [P, KD, TOK])
        attnT = hT
        zbuf = sb("zbuf", [P, KD * TOK])
        zT = zbuf[:, :].rearrange("p (k t) -> p k t", k=KD)
        xin = zbuf[:, :].rearrange("p (a d) -> p a d", a=4)
        slots = sb("slots", [P, SLOTS, SLOT])
        region = sb("region", [P, 13312])

        def part(o, *dims):
            n = math.prod(dims)
            v = region[:, o:o + n]
            if len(dims) == 1:
                return v
            return v.rearrange("p (a b) -> p a b", a=dims[0])

        QM = part(0, 4, TOK)
        KM = part(2048, 4, TOK)
        QA = part(4096, 2, TOK)
        KA = part(5120, TOK)
        QDf = part(5632, 2, TOK)
        KDf = part(6656, 2, TOK)
        QN = part(7680, 2, TOK)
        KN = part(8704, 2, TOK)
        V = part(9728, 4, 896)
        VOFF = {"a": 0, "c": 128, "d": 384, "b": 640}
        cst = sb("cst", [P, C_ALL])
        biasm = sb("biasm", [P, 4, 2, SEQ])
        ropet = sb("ropet", [P, 2, SEQ])
        wuq = sb("wuq", [P, 2, 384])
        wukv = sb("wukv", [P, 512])
        tab = st.enter_context(nc.sbuf_tensor("tab", [P, DEPTH, 65], mybir.dt.int32))
        pos = st.enter_context(nc.sbuf_tensor("pos", [P, DEPTH, 8], mybir.dt.int32))
        gate = sb("gate", [P, DEPTH, 8])
        wr = sb("wr", [P, DEPTH, KD, 36])
        colv = sb("colv", [P, DEPTH, P])
        rowv = sb("rowv", [P, DEPTH, R_ALL])
        cT = sb("cT", [P, KD, 32])
        modT = sb("modT", [P, DEPTH, 48, 2])
        modT1 = sb("modT1", [P, DEPTH, 48, 2])
        onesD = sb("onesD", [P, P])
        ones = sb("ones", [P, P])
        epst = sb("epst", [P, 1])
        nlam = sb("nlam", [P, DEPTH])
        nsink = sb("nsink", [P, DEPTH, 4])
        lamt = sb("lamt", [P, 2, 32])
        lams = sb("lams", [P, 4])
        subg = sb("subg", [P, DEPTH])
        nmx = sb("nmx", [P, RING])
        rsum = sb("rsum", [P, RING])
        rinv = sb("rinv", [P, RING])
        esk = sb("esk", [P, RING])
        vrow = part(4096, DEPTH, P)
        sqr = part(0, 2, TOK)
        rstd = part(1024, TOK)
        rt = part(1536, 4, 104)
        lg = part(1952, 4, 36)
        oh = [part(2096 + 128 * i, 4, NE) for i in range(3)]
        posp = part(2480, 4, NE)
        nch = part(2608, 8)
        nrep = part(2616, P)
        prel = part(2744, 8)
        xcols = part(2752, KD, CH)
        sg = part(3264, P)
        hid = part(3392, P)
        hidT = part(3520, P)
        yrows = part(3648, 512)
        pick = part(4160, 4 * CH // 2).bitcast(BF16).rearrange("p (t c) -> p t c", t=4)
        pick2 = part(4288, 4 * CH // 2).bitcast(BF16).rearrange("p (t c) -> p t c", t=4)
        hparts = part(4608, 3 * 4 * D // 2).bitcast(BF16).rearrange("p (i t d) -> p i t d", i=3, t=4)
        stage = part(10752, 4, 512)

        def hpart(i, q):
            return hparts[:, i, q // 2, (q % 2) * 512:(q % 2 + 1) * 512]

        def first_left(l, q):
            return 4 * TQ[0] // P * l + max(1, 2 * q)

        def split_done(l, q):
            return 4 * TQ[0] // P * l + min(2 * q + 3, 4 * TQ[l] // P)

        y2 = part(9216, 4, D)
        extra_in = zbuf[:, :]
        extra_down = hT[:, 0:4, :].rearrange("p k t -> p (k t)")
        y1 = hT[:, :, :].rearrange("p (a b) t -> p a (b t)", a=4)
        praw = zT[:, 0:3, :]
        psq = zT[:, 3:6, :]
        prstd = zT[:, 6:8, :]
        Pr = zT[:, 0:4, :]
        PTs = zT[:, 4:7, :]
        mrow = ropet[0:96, 0, :]
        ident = cst[:, C_ID:C_ID + P]

        bank = [st.enter_context(nc.psum_tensor(f"bank{i}", [P, 512], F32)) for i in range(8)]

        w_here = [sem(f"w_here{i}") for i in range(SLOTS)]
        g_here = [sem(f"g_here{i}") for i in range(SLOTS)]
        x_here = sem("x_here")
        x_down = sem("x_down")
        s_small = sem("s_small")
        s_xin = sem("s_xin")
        s_wqkv = per_layer("s_wqkv")
        s_bias = per_layer("s_bias")
        s_biasm = per_layer("s_biasm")
        s_ones = sem("s_ones")
        s_vt = sem("s_vt")
        s_colv = sem("s_colv")
        s_cT = sem("s_cT")
        s_lamp = sem("s_lamp")
        s_lame = sem("s_lame")
        s_tp = sem("s_tp")
        s_xT = sem("s_xT")
        s_mod = sem("s_mod")
        s_mrow = sem("s_mrow")
        s_mtr = sem("s_mtr")
        s_modT = sem("s_modT")
        s_h1a = per_layer("s_h1a")
        s_h1d = per_layer("s_h1d")
        s_grp = per_layer("s_grp")
        s_eva = per_layer("s_eva")
        s_evd = per_layer("s_evd")
        s_perm = per_layer("s_perm")
        s_rope = per_layer("s_rope")
        s_psq = per_layer("s_psq")
        s_pn = per_layer("s_pn")
        s_S = per_layer("s_S")
        s_nm = per_layer("s_nm")
        s_exp = per_layer("s_exp")
        s_norm = per_layer("s_norm")
        s_T = per_layer("s_T")
        s_PT = per_layer("s_PT")
        s_O = per_layer("s_O")
        s_att = per_layer("s_att")
        s_csq = sem("s_csq")
        s_css = sem("s_css")
        s_cstd = sem("s_cstd")
        s_cn = sem("s_cn")
        s_y = per_layer("s_y")
        s_yg = per_layer("s_yg")
        ln = {n: sem(f"ln_{n}") for n in ("z", "mean", "cent", "sq", "sqs", "std", "zn", "x")}
        s_h2d = per_layer("s_h2d")
        s_h2p = per_layer("s_h2p")
        s_lg = per_layer("s_lg")
        s_rexp = sem("s_rexp")
        s_rexpd = sem("s_rexpd")
        s_mask = sem("s_mask")
        s_cnt = sem("s_cnt")
        s_nch = sem("s_nch")
        s_pos = sem("s_pos")
        s_tab = sem("s_tab")
        s_tok = per_layer("s_tok")
        s_prel = per_layer("s_prel")
        s_pick = per_layer("s_pick")
        s_toke = per_layer("s_toke")
        s_xt = per_layer("s_xt")
        s_xc = per_layer("s_xc")
        s_hg = per_layer("s_hg")
        s_sg = per_layer("s_sg")
        s_hid = per_layer("s_hid")
        s_ht = per_layer("s_ht")
        s_hte = per_layer("s_hte")
        s_dn = per_layer("s_dn")
        s_yev = per_layer("s_yev")
        s_yfree = per_layer("s_yfree")
        s_yw = per_layer("s_yw")
        s_cmb = per_layer("s_cmb")
        s_yt = per_layer("s_yt")
        s_yh = per_layer("s_yh")
        s_gat = [sem(f"s_gat{t}") for t in range(4)]
        s_fill = sem("s_fill")
        s_ot = sem("s_ot")
        s_oe = sem("s_oe")
        s_out = sem("s_out")
        s_dch = sem("s_dch")
        s_ach = sem("s_ach")
        s_pch = sem("s_pch")
        s_h2 = sem("s_h2")

        slot_outs = nc.dram_tensor("slot_outs", (CHUNKS[0] * CH, D), F32, kind="Internal").ap()
        chunk_outs = slot_outs.rearrange("(g p) d -> g p d", p=CH)

        block = st.enter_context(nc.Block())

        units = [attention_units(l) for l in range(DEPTH)]
        first = []
        for l in range(DEPTH):
            f = [0]
            for u in units[l]:
                f.append(f[-1] + (2 if u[0] == "c" else 1))
            first.append(f)

        def dest(name, i):
            return {"qa": lambda: QA[:, i, :], "ka": lambda: KA[:, :], "qd": lambda: QDf[:, i, :], "kd": lambda: KDf[:, i, :],
                    "qn": lambda: QN[:, i, :], "kn": lambda: KN[:, i, :], "mq": lambda: QM[:, i, :],
                    "kr": lambda: KM[:, 0, :]}[name]()

        def width(l, name):
            return TQ[l] if name in ("qa", "qd", "qn", "mq", "ssq") or name == "pq" else TOK

        def released(i):
            kind, l, c = PLAN[i]
            if kind == "mod":
                return s_mod, 8 * l + c + 1
            if kind == "in":
                return s_grp[l], GI[[g for g, p in LAST_OF_PART.items() if p == c][0]] + 1
            if kind == "out":
                return s_y[l], 4 * (c + 1)
            raise ValueError(kind)

        def mod_bank(i):
            return bank[6 + i % 2] if i < 3 else bank[7]

        @block.sync
        def _(sp):
            sp.dma_start(xin[:, 0:2, :], x.rearrange("o (a p) d -> p (o a) d", p=P)).then_inc(s_xin, 16)
            sp.dma_start(xin[:, 2:4, :], ctx_in.rearrange("o (a p) d -> p (o a) d", p=P)).then_inc(s_xin, 16)
            sp.wait_ge(s_small, 48)

            def load(kind, l, c, slot_n, gate_here):
                here = w_here[slot_n]
                slot = slots[:, slot_n, :]
                if kind == "mod":
                    sp.dma_start(slot.rearrange("p (k n) -> p k n", k=KD),
                                 w_mod[l].rearrange("(k p) n -> p k n", p=P)[:, :, c * MOD_COLS:(c + 1) * MOD_COLS]).then_inc(here, 16)
                elif kind == "in":
                    o, n = IN_PARTS[c]
                    sp.dma_start(slot[:, 0:KD * n].rearrange("p (k n) -> p k n", k=KD),
                                 w_in[l].rearrange("(k p) n -> p k n", p=P)[:, :, o:o + n]).then_inc(here, 16)
                elif kind == "out":
                    sp.dma_start(slot[:, 0:KD * 512].rearrange("p (k n) -> p k n", k=KD),
                                 w_out[l].rearrange("(k p) n -> p k n", p=P)[:, :, c * 512:(c + 1) * 512]).then_inc(here, 16)
                else:
                    for j, w in enumerate((w_gate, w_up)):
                        sp.dma_start(slot[:, j * 2048:(j + 1) * 2048].rearrange("p (k f) -> p k f", k=KD),
                                     w[l].rearrange("g e (k p) f -> (g e) p k f", p=P)[c]).then_inc(here if j else g_here[slot_n], 16)
                    sp.wait_ge(g_here[slot_n], gate_here)
                    sp.dma_start(slot[:, 4096:6144].rearrange("p (k d) -> p k d", k=2),
                                 w_down[l].rearrange("g e (k p) d -> (g e) p k d", p=P)[c]).then_inc(here, 16)

            i = 0
            while i < len(PLAN):
                kind, l, c = PLAN[i]
                if kind == "exp" and c == SLOTS + 1:
                    sp.wait_ge(ln["x"], KD * (2 * l + 1))
                    for j, w in enumerate((w_gate, w_up)):
                        sp.dma_start(extra_in[:, j * 2048:(j + 1) * 2048].rearrange("p (k f) -> p k f", k=KD),
                                     w[l].rearrange("g e (k p) f -> (g e) p k f", p=P)[EXTRA]).then_inc(x_here, 16)
                    sp.wait_ge(s_tok[l], 2 * (TQ[l] // P))
                    sp.dma_start(extra_down.rearrange("p (k d) -> p k d", k=2),
                                 w_down[l].rearrange("g e (k p) d -> (g e) p k d", p=P)[EXTRA]).then_inc(x_down, 16)
                    sp.wait_ge(s_tab, l + 1)

                    def next_expert(e, back, slot, gate_here):
                        done = sp.value_load(tab[0:1, l, bass.ds(e - (back - 1), 1)], min_val=1, max_val=CHUNKS[l])
                        sp.wait_ge(s_dn[l], done)
                        load("exp", l, e, slot, gate_here)

                    for e in range(EXTRA + 1, EXTRA + 1 + SLOTS):
                        n = INDEX["exp", l, e]
                        next_expert(e, SLOTS + 1, n % SLOTS, gate_arrival(n))
                    e1 = EXTRA + 1 + SLOTS
                    rounds = (NE - e1) // SLOTS
                    n = INDEX["exp", l, e1]
                    with sp.Fori(0, rounds) as r0:
                        for a in range(SLOTS):
                            next_expert(r0 * SLOTS + (e1 + a), SLOTS, (n + a) % SLOTS, r0 * 16 + gate_arrival(n + a))
                    for e in range(e1 + SLOTS * rounds, NE):
                        n = INDEX["exp", l, e]
                        next_expert(e, SLOTS, n % SLOTS, gate_arrival(n))
                    i += NE - SLOTS - 1
                    continue
                if i >= SLOTS:
                    okind, ol, oc = PLAN[i - SLOTS]
                    if okind == "exp":
                        done = sp.value_load(tab[0:1, ol, oc + 1:oc + 2], min_val=1, max_val=CHUNKS[ol])
                        sp.wait_ge(s_dn[ol], done)
                        if oc == NE - 1:
                            for t in range(TQ[ol] // P):
                                sp.wait_ge(s_gat[t], 32 * (ol + 1))
                    else:
                        sp.wait_ge(*released(i - SLOTS))
                load(kind, l, c, i % SLOTS, gate_arrival(i))
                i += 1
            for t in range(2):
                sp.wait_ge(s_oe, 4 * (t + 1))
                sp.dma_start(out[0, t * P:(t + 1) * P, :], xin[:, t, :]).then_inc(s_out, 16)
            sp.wait_ge(s_out, 32)

        @block.gpsimd
        def _(pool):
            nc.gpsimd.memset(cT[:, :, :], 0.0)
            nc.gpsimd.memset(onesD[:, :], 1.0 / D)
            nc.gpsimd.memset(epst[:, :], EPS)
            nc.gpsimd.memset(ones[:, :], 1.0).then_inc(s_ones, 1)
            pool.wait_ge(s_small, 48)
            for l in range(DEPTH):
                if l >= 1:
                    pool.wait_ge(s_S[l - 1], first[l - 1][-1])
                pool.wait_ge(s_bias[l], 16)
                for h in range(4):
                    nc.gpsimd.tensor_tensor(biasm[:, h, :, :], biasm[:, h, :, :],
                                            cst[:, C_NA:C_NA + 512].rearrange("p (a k) -> p a k", a=2), ALU.add).then_inc(s_biasm[l], 1)
                if TQ[l] > SEQ:
                    for m in range(KD):
                        pool.wait_ge(ln["x"], KD * 2 * l + m + 1)
                        nc.gpsimd.tensor_scalar(hT[:, m, SEQ:TOK], xT[:, m, SEQ:TOK], modT1[:, l, SC2 + m, 1:2],
                                                modT[:, l, SH2 + m, 1:2], ALU.mult, ALU.add).then_inc(s_h2p[l], 1)
                nt = TQ[l] // P
                for q in range(2 * nt + 1):
                    if q < 2 * nt:
                        pool.wait_ge(s_toke[l], q + 1)
                        nc.gpsimd.tensor_tensor(stage[:, q % 4, :], stage[:, q % 4, :], hpart(0, q), ALU.subtract).then_inc(s_pch, 1)
                    if q >= 1:
                        pool.wait_ge(s_h2, 2 * TQ[0] // P * l + q)
                        nc.gpsimd.tensor_tensor(hpart(2, q - 1), stage[:, (q - 1) % 4, :], hpart(1, q - 1), ALU.subtract).then_inc(s_pch, 1)
                pool.wait_ge(s_tab, l + 1)
                if l == 0:
                    pool.wait_ge(s_fill, 16)
                pool.sem_inc(s_yfree[l], 1)
                total = pool.value_load(tab[0:1, l, T_ALL:T_ALL + 1], min_val=NE, max_val=CHUNKS[l])
                with pool.Fori(0, total) as g:
                    pool.wait_ge(s_yev[l], g + 1)
                    for c in range(2):
                        pool.dma_start(chunk_outs[g][:, c * 512:(c + 1) * 512], yrows[c * CH:(c + 1) * CH, :]).then_inc(s_yw[l], 16)
                    pool.wait_ge(s_yw[l], g * 32 + 32)
                    pool.sem_inc(s_yfree[l], 1)
                for t in range(nt):
                    for a, y in ((0, y1), (1, y2)):
                        pool.indirect_dma_start(out=y[:, t, :], out_offset=None, in_=slot_outs[:, :],
                                                in_offset=bass.IndirectOffsetOnAxis(ap=pos[:, l, 4 * a + t:4 * a + t + 1], axis=0)).then_inc(s_gat[t], 16)

        @block.scalar
        def _(act):
            chain = [0]

            def link(ins):
                chain[0] += 1
                ins.then_inc(s_ach, 1)
                act.wait_ge(s_ach, chain[0])

            act.dma_start(cst[:, :], consts[:, :]).then_inc(s_small, 16)
            act.dma_start(vrow[:, :, :], vecs.rearrange("l p n -> p l n")).then_inc(s_small, 16)
            act.dma_start(rowv[:, :, :], rows.rearrange("l p n -> p l n")).then_inc(s_small, 16)

            def small_weights(l):
                act.dma_start(wuq[:, :, :], w_uq[l].rearrange("(k p) n -> p k n", p=P)).then_inc(s_wqkv[l], 16)
                act.dma_start(wukv[:, :], w_ukv[l]).then_inc(s_wqkv[l], 16)

            def small_bias(l):
                act.dma_start(biasm[:, :, :, :].rearrange("p h a k -> p (h a) k"),
                              bias_na[l].rearrange("h (a p) k -> p (h a) k", p=P)).then_inc(s_bias[l], 16)

            act.wait_ge(s_colv, 1)
            act.wait_ge(s_ones, 1)
            act.activation(cT[:, :, 0:2], colv[:, 0, V_C:V_C + 16].rearrange("p (a k) -> p k a", a=2), ACT.Silu).then_inc(s_cT, 1)
            act.wait_ge(s_lamp, 2)
            act.activation(lams[:, 0:4], lams[:, 0:4], ACT.Exp).then_inc(s_lame, 1)

            def layer_norm_act(l, w):
                i0 = 2 * l + w
                n = TQ[l]
                for m in range(KD):
                    act.wait_ge(ln["cent"], KD * i0 + m + 1)
                    if m >= 2:
                        act.wait_ge(ln["sqs"], KD * i0 + m - 1)
                    act.activation(sqr[:, m % 2, 0:n], zT[:, m, 0:n], ACT.Square).then_inc(ln["sq"], 1)
                act.wait_ge(ln["sqs"], KD * i0 + KD)
                act.activation(rstd[:, 0:n], bank[5][:, 0:n], ACT.Sqrt, bias=epst[:, 0:1], scale=1.0 / D).then_inc(ln["std"], 1)
                g, b = (V_LN1G, V_LN1B) if w == 0 else (V_LN2G, V_LN2B)
                for m in range(KD):
                    act.wait_ge(ln["zn"], KD * i0 + m + 1)
                    act.activation(xT[:, m, 0:n], zT[:, m, 0:n], ACT.Identity, bias=colv[:, l, b + m:b + m + 1],
                                   scale=colv[:, l, g + m:g + m + 1]).then_inc(ln["x"], 1)

            def gated(l, m, src, chunk):
                ins = act.activation(zT[:, m, 0:SEQ], src[:, 0:SEQ], ACT.Copy, scale=modT[:, l, chunk + m, 0:1])
                if TQ[l] > SEQ:
                    ins = act.activation(zT[:, m, SEQ:TOK], src[:, SEQ:TOK], ACT.Copy, scale=modT[:, l, chunk + m, 1:2])
                return ins

            for l in range(DEPTH):
                n = TQ[l]
                act.wait_ge(s_modT, 3 if l == 0 else 16)
                if l == 0:
                    act.wait_ge(s_xT, KD)
                    act.wait_ge(s_ones, 1)
                else:
                    act.wait_ge(ln["x"], KD * 2 * l)
                for m in range(KD):
                    act.activation(hT[:, m, SEQ:TOK], xT[:, m, SEQ:TOK], ACT.Identity, bias=modT[:, l, SH1 + m, 1:2],
                                   scale=modT1[:, l, SC1 + m, 1:2]).then_inc(s_h1a[l], 1)
                if l == 0:
                    small_weights(0)
                    act.dma_start(wr[:, :, :, :].rearrange("p l k n -> p (l k) n"),
                                  w_route.rearrange("l (k p) n -> p (l k) n", p=P)).then_inc(s_wqkv[0], 16)
                    small_bias(0)
                for g, (name, i) in enumerate(GROUPS):
                    if (name, i) == ("vd", 0):
                        for j in range(3):
                            act.wait_ge(s_evd[l], NDVE[GI[("pkv", 0)] if j == 2 else GI[("pq", j)]])
                            nn = width(l, "pq") if j < 2 else TOK
                            act.activation(psq[:, j, 0:nn], praw[:, j, 0:nn], ACT.Square).then_inc(s_psq[l], 1)
                    if name not in BY_ACT:
                        continue
                    act.wait_ge(s_grp[l], g + 1)
                    w = width(l, name)
                    src = bank[g % PROJ_BANKS]
                    if name == "ssq":
                        act.activation(prstd[:, 0, 0:w], src[:, 0:w], ACT.Sqrt, bias=epst[:, 0:1], scale=1.0 / 256).then_inc(s_eva[l], 1)
                    elif name == "sskv":
                        act.activation(prstd[:, 1, 0:w], src[:, 0:w], ACT.Sqrt, bias=epst[:, 0:1], scale=1.0 / 128).then_inc(s_eva[l], 1)
                    else:
                        lo, hi = (64, 96) if name == "kr" else (0, 96) if name == "mq" else (0, 128)
                        act.activation(dest(name, i)[lo:hi, 0:w], src[lo:hi, 0:w], ACT.Copy, scale=SCALE[name]).then_inc(s_eva[l], 1)
                uf = first[l]
                vof = [v for v in range(len(units[l])) for _ in range(uf[v + 1] - uf[v])]
                if l == 0:
                    act.dma_start(slot_outs.rearrange("(p a) (c n) -> p (a c) n", p=P, n=P),
                                  onesD[:, :].unsqueeze(1).to_broadcast([P, CHUNKS[0] * CH // P * KD, P])).then_inc(s_fill, 16)
                act.wait_ge(s_grp[l], len(GROUPS))
                for v in range(len(units[l]) + 2):
                    if v < len(units[l]):
                        mixer, h, qt, k0 = units[l][v]
                        for u in range(uf[v], uf[v + 1]):
                            act.wait_ge(s_nm[l], u + 1)
                            if u >= 4:
                                act.wait_ge(s_T[l], vof[u - 4] + 1)
                            if mixer == "a":
                                act.activation(esk[:, u % RING:u % RING + 1], rowv[:, l, R_SINK + h:R_SINK + h + 1], ACT.Exp, bias=nmx[:, u % RING:u % RING + 1])
                            act.activation(Pr[:, u % 4, k0 * P:TOK], bank[u % 3][:, k0 * P:TOK], ACT.Exp, bias=nmx[:, u % RING:u % RING + 1],
                                           accum_out=rsum[:, u % RING:u % RING + 1]).then_inc(s_exp[l], 1)
                    if v >= 2:
                        t = v - 2
                        k0 = units[l][t][3]
                        act.wait_ge(s_T[l], t + 1)
                        if t >= 3:
                            act.wait_ge(s_O[l], (t - 3) // 2 + 1)
                        act.activation(PTs[:, t % 3, k0 * P:TOK], bank[3 + t % 2][:, k0 * P:TOK], ACT.Copy).then_inc(s_PT[l], 1)
                    step = v - (len(units[l]) - 8)
                    if step == 0:
                        act.wait_ge(s_S[l], uf[-1 - 8])
                        act.wait_ge(s_att[l], len(units[l]) // 4)
                        for j in range(2):
                            act.activation(sqr[:, j, 0:n], attnT[:, 4 + j, 0:n], ACT.Square).then_inc(s_csq, 1)
                    if step in (2, 5):
                        j = step // 5
                        act.wait_ge(s_css, 2 * l + j + 1)
                        act.activation(sqr[:, j, 0:n], bank[7][:, 0:n], ACT.Copy).then_inc(s_cstd, 1)
                    if step == 6:
                        act.wait_ge(s_cstd, 3 * l + 2)
                        act.activation(sqr[:, :, 0:n], sqr[:, :, 0:n], ACT.Sqrt, bias=epst[:, 0:1]).then_inc(s_cstd, 1)
                if l + 1 < DEPTH:
                    small_weights(l + 1)
                    act.wait_ge(s_S[l], uf[-1])
                    small_bias(l + 1)
                act.wait_ge(s_modT, 16)
                for m in range(KD):
                    act.wait_ge(s_y[l], m + 1)
                    gated(l, m, bank[m % 4], G1).then_inc(s_yg[l], 1)
                layer_norm_act(l, 0)
                nn = n // P

                def router_exp(j):
                    act.wait_ge(s_rexp, 2 * l + j + 1)
                    c0, c1 = (0, 4) if j == 0 else (100, 101)
                    act.activation(rt[:, 0:nn, c0:c1], rt[:, 0:nn, c0:c1], ACT.Exp).then_inc(s_rexpd, 1)

                for q in range(2 * nn + 1):
                    if q in (2 * nn - 4, 2 * nn - 2):
                        router_exp((q - (2 * nn - 4)) // 2)
                    if q < 2 * nn:
                        act.wait_ge(s_tok[l], q + 1)
                        if q >= 4:
                            act.wait_ge(s_pch, split_done(l, q - 4))
                        act.activation(stage[:, q % 4, :], bank[q % 4][:, :], ACT.Copy)
                        act.activation(hpart(0, q), bank[q % 4][:, :], ACT.Copy).then_inc(s_toke[l], 1)
                    if q >= 1:
                        act.wait_ge(s_pch, first_left(l, q - 1))
                        act.activation(hpart(1, q - 1), stage[:, (q - 1) % 4, :], ACT.Copy).then_inc(s_h2, 1)
                act.wait_ge(s_tab, l + 1)
                total = act.value_load(tab[0:1, l, T_ALL:T_ALL + 1], min_val=NE, max_val=CHUNKS[l])
                with act.Fori(0, total) as g:
                    act.wait_ge(s_hg[l], g + 1)
                    act.activation(sg[:, :], bank[1][:, 0:P], ACT.Silu).then_inc(s_sg[l], 1)
                for h in range(n // SEQ):
                    for m in range(KD):
                        q = KD * h + m
                        act.wait_ge(s_yt[l], q + 1)
                        act.activation(zT[:, m, h * SEQ:(h + 1) * SEQ], bank[q % 4][:, 0:SEQ], ACT.Copy,
                                       scale=modT[:, l, G2 + m, h:h + 1]).then_inc(s_yh[l], 1)
                layer_norm_act(l, 1)

        @block.vector
        def _(dve):
            chain = [0]

            def link(ins):
                chain[0] += 1
                ins.then_inc(s_dch, 1)
                dve.wait_ge(s_dch, chain[0])

            vec = nc.vector
            for l in range(DEPTH):
                dve.wait_ge(s_vt, l + 1)
                vec.tensor_copy(colv[:, l, :], bank[l][:, 0:P]).then_inc(s_colv, 1)
            dve.wait_ge(s_small, 48)
            for l in range(DEPTH):
                lam = rowv[:, l, R_LAM:R_LAM + 128].rearrange("p (a b n) -> p a b n", a=2, b=2)
                link(vec.tensor_tensor(lamt[:, :, :], lam[:, :, 0, :], lam[:, :, 1, :], ALU.mult))
                vec.tensor_reduce(lams[:, 2 * l:2 * l + 2], lamt[:, :, :], AX, ALU.add).then_inc(s_lamp, 1)
                dve.wait_ge(s_lamp, l + 1)
                vec.tensor_scalar(nsink[:, l, :], rowv[:, l, R_SINK:R_SINK + 4], -1.0, None, ALU.mult)
            dve.wait_ge(s_lame, 1)
            dve.wait_ge(s_colv, 2)
            for l in range(DEPTH):
                lam_init = 0.8 - 0.6 * math.exp(-0.3 * l)
                link(vec.tensor_tensor(nlam[:, l:l + 1], lams[:, 2 * l + 1:2 * l + 2], lams[:, 2 * l:2 * l + 1], ALU.subtract))
                link(vec.tensor_scalar(nlam[:, l:l + 1], nlam[:, l:l + 1], -lam_init, None, ALU.add))
                link(vec.tensor_scalar(subg[:, l:l + 1], colv[:, l, V_SUB:V_SUB + 1], 1.0 - lam_init, None, ALU.mult))
            for k in range(KD):
                dve.wait_ge(s_tp, k + 1)
                vec.tensor_copy(xT[:, k, :], bank[2 + k % 2][:, :]).then_inc(s_xT, 1)

            def mod_rows(l, c):
                dve.wait_ge(s_mod, 8 * l + c + 1)
                vec.tensor_copy(mrow[:, :], mod_bank(8 * l + c)[0:96, 0:256]).then_inc(s_mrow, 1)

            def mod_columns(l, c):
                dve.wait_ge(s_mtr, 8 * l + c + 1)
                src = mod_bank(8 * l + c)[:, 256:448].rearrange("p (h j n) -> p j h n", h=2, j=3)
                cols = slice(c * MOD_J, (c + 1) * MOD_J)
                bias = colv[:, l, cols].rearrange("p (j h) -> p j h", h=2)
                for a in range(2):
                    vec.tensor_tensor(modT[:, l, cols, a].rearrange("p (j h) -> p j h", h=2), src[:, :, :, a], bias, ALU.add)
                    ins = vec.scalar_tensor_tensor(modT1[:, l, cols, a].rearrange("p (j h) -> p j h", h=2), src[:, :, :, a], 1.0, bias,
                                                   ALU.add, ALU.add)
                ins.then_inc(s_modT, 1)

            for c in range(3):
                mod_rows(0, c)
                mod_columns(0, c)

            def layer_norm_dve(l, w):
                i0 = 2 * l + w
                n = TQ[l]
                for m in range(KD):
                    if w == 0:
                        dve.wait_ge(s_yg[l], m + 1)
                    else:
                        dve.wait_ge(s_yh[l], KD * (n // SEQ - 1) + m + 1)
                    vec.scalar_tensor_tensor(zT[:, m, 0:n], xT[:, m, 0:n], ALPHA, zT[:, m, 0:n], ALU.mult, ALU.add).then_inc(ln["z"], 1)
                dve.wait_ge(ln["mean"], i0 + 1)
                for m in range(KD):
                    dve.wait_ge(ln["z"], KD * i0 + m + 1)
                    vec.tensor_tensor(zT[:, m, 0:n], zT[:, m, 0:n], bank[4][:, 0:n], ALU.subtract).then_inc(ln["cent"], 1)
                dve.wait_ge(ln["std"], i0 + 1)
                link(vec.reciprocal(rstd[:, 0:n], rstd[:, 0:n]))
                for m in range(KD):
                    vec.tensor_tensor(zT[:, m, 0:n], zT[:, m, 0:n], rstd[:, 0:n], ALU.mult).then_inc(ln["zn"], 1)

            for l in range(DEPTH):
                n = TQ[l]
                nt = n // P
                if l == 0:
                    dve.wait_ge(s_xT, KD)
                    dve.wait_ge(s_modT, 3)
                else:
                    dve.wait_ge(ln["x"], KD * 2 * l)
                for m in range(KD):
                    vec.tensor_scalar(hT[:, m, 0:SEQ], xT[:, m, 0:SEQ], modT1[:, l, SC1 + m, 0:1],
                                      modT[:, l, SH1 + m, 0:1], ALU.mult, ALU.add).then_inc(s_h1d[l], 1)

                def rope(r):
                    g = ROPES[r]
                    name, i = GROUPS[g]
                    lo, hi = (64, 96) if name in ("kr", "mq") else (0, 128)
                    cos, sin = (C_COS64, C_SIN64) if name in ("qa", "ka") else (C_COS32, C_SIN32)
                    d = dest(name, i)[lo:hi, 0:SEQ]
                    dve.wait_ge(s_perm[l], r + 1)
                    vec.tensor_tensor(ropet[lo:hi, r % 2, :], bank[4 + r % 2][lo:hi, 0:SEQ], cst[lo:hi, sin:sin + SEQ], ALU.mult)
                    link(vec.tensor_tensor(d, d, cst[lo:hi, cos:cos + SEQ], ALU.mult))
                    vec.tensor_tensor(d, d, ropet[lo:hi, r % 2, :], ALU.add).then_inc(s_rope[l], 1)
                    if name == "kr":
                        dve.wait_ge(s_rope[l], r + 1)
                        for h in range(1, 4):
                            vec.tensor_copy(KM[64:96, h, :], KM[64:96, 0, :])

                done = 0
                for g, (name, i) in enumerate(GROUPS):
                    if (name, i) == ("mq", 0):
                        for j in range(2):
                            w = TOK if j else n
                            dve.wait_ge(s_eva[l], NACT[GI[("sskv" if j else "ssq", 0)]])
                            link(vec.reciprocal(prstd[:, j, 0:w], prstd[:, j, 0:w]))
                        for j in range(3):
                            w = TOK if j == 2 else n
                            col = V_KVN if j == 2 else V_QN + j
                            vec.scalar_tensor_tensor(praw[:, j, 0:w], praw[:, j, 0:w], colv[:, l, col:col + 1],
                                                     prstd[:, 1 if j == 2 else 0, 0:w], ALU.mult, ALU.mult).then_inc(s_pn[l], 1)
                    if name not in BY_ACT:
                        dve.wait_ge(s_grp[l], g + 1)
                        src = bank[g % PROJ_BANKS]
                        if name == "va":
                            ins = vec.tensor_copy(V[:, :, 0:P], src[:, :].rearrange("p (t c) -> p t c", t=4))
                        elif name in ("vd", "vn", "mv"):
                            o = VOFF[{"vd": "c", "vn": "d", "mv": "b"}[name]]
                            ins = vec.tensor_copy(V[:, 2 * i:2 * i + 2, o:o + 256], src[:, :].rearrange("p (t c) -> p t c", t=2))
                        elif name in ("pq", "pkv"):
                            w = width(l, name)
                            ins = vec.tensor_copy(praw[:, i if name == "pq" else 2, 0:w], src[:, 0:w])
                        elif name == "mk":
                            ins = vec.tensor_copy(KM[0:64, i, :], src[0:64, :])
                        else:
                            ins = vec.tensor_copy(dest(name, i), src[:, :])
                        ins.then_inc(s_evd[l], 1)
                    while done < len(ROPES) and ROPES[done] + 2 <= g:
                        rope(done)
                        done += 1
                while done < len(ROPES):
                    rope(done)
                    done += 1

                def normalise_c(j):
                    dve.wait_ge(s_cstd, 3 * l + 3)
                    link(vec.reciprocal(sqr[:, j, 0:n], sqr[:, j, 0:n]))
                    vec.scalar_tensor_tensor(attnT[:, 4 + j, 0:n], attnT[:, 4 + j, 0:n], subg[:, l:l + 1], sqr[:, j, 0:n],
                                             ALU.mult, ALU.mult).then_inc(s_cn, 1)

                uf = first[l]
                mods = [(0, c) for c in range(3, 8)] + [(1, c) for c in range(8)] if l == 0 else []
                for v in range(len(units[l]) + 4):
                    if v < len(units[l]):
                        mixer, h, qt, k0 = units[l][v]
                        for u in range(uf[v], uf[v + 1]):
                            dve.wait_ge(s_S[l], u + 1)
                            ins = vec.tensor_reduce(nmx[:, u % RING:u % RING + 1], bank[u % 3][:, k0 * P:TOK], AX, ALU.max, negate=True)
                            if mixer == "a":
                                link(ins)
                                ins = vec.tensor_tensor(nmx[:, u % RING:u % RING + 1], nmx[:, u % RING:u % RING + 1], nsink[:, l, h:h + 1], ALU.min)
                            ins.then_inc(s_nm[l], 1)
                    if 1 <= v <= len(units[l]):
                        mixer, h, qt, k0 = units[l][v - 1]
                        for u in range(uf[v - 1], uf[v]):
                            dve.wait_ge(s_exp[l], u + 1)
                            if mixer == "a":
                                link(vec.tensor_tensor(rsum[:, u % RING:u % RING + 1], rsum[:, u % RING:u % RING + 1], esk[:, u % RING:u % RING + 1], ALU.add))
                            link(vec.reciprocal(rinv[:, u % RING:u % RING + 1], rsum[:, u % RING:u % RING + 1]))
                            r = rinv[:, u % RING:u % RING + 1]
                            own = Pr[:, u % 4, k0 * P:TOK]
                            if mixer == "c" and u == uf[v] - 1:
                                link(vec.tensor_scalar(r, r, nlam[:, l:l + 1], None, ALU.mult))
                                one = Pr[:, (u - 1) % 4, k0 * P:TOK]
                                ins = vec.scalar_tensor_tensor(one, own, r, one, ALU.mult, ALU.add)
                            else:
                                ins = vec.tensor_scalar(own, own, r, None, ALU.mult)
                            ins.then_inc(s_norm[l], 1)
                            if mixer == "c" and u < uf[v] - 1:
                                dve.wait_ge(s_norm[l], u + 1)
                    if v >= 4 and v % 2 == 0:
                        p = (v - 4) // 2
                        mixer, h, qt, k0 = units[l][2 * p]
                        dve.wait_ge(s_O[l], p + 1)
                        ch = 2 * "abcd".index(mixer) + h // 2
                        vec.tensor_copy(attnT[:, ch, qt * P:(qt + 1) * P], bank[5 + p % 2][:, 0:P]).then_inc(s_att[l], 1)
                    if mods and v % 4 == 3:
                        mod_rows(*mods[0])
                    if mods and v % 4 == 0 and v:
                        mod_columns(*mods.pop(0))
                    if v == len(units[l]) - 1:
                        normalise_c(0)
                assert not mods

                normalise_c(1)
                layer_norm_dve(l, 0)
                for m in range(KD):
                    dve.wait_ge(ln["x"], KD * 2 * l + m + 1)
                    vec.tensor_scalar(hT[:, m, 0:SEQ], xT[:, m, 0:SEQ], modT1[:, l, SC2 + m, 0:1],
                                      modT[:, l, SH2 + m, 0:1], ALU.mult, ALU.add).then_inc(s_h2d[l], 1)

                dve.wait_ge(s_lg[l], 1)
                for t in range(nt):
                    vec.tensor_tensor(lg[:, t, :], bank[4 + t][:, 0:36], rowv[:, l, R_RB:R_RB + 36], ALU.add).then_inc(s_dch, 1)
                    chain[0] += 1
                dve.wait_ge(s_dch, chain[0])

                def col(i):
                    return rt[:, 0:nt, i:i + 1]

                def bc(i, k):
                    return rt[:, 0:nt, i:i + 1].to_broadcast([P, nt, k])

                def first_max(src, k, m, one):
                    iota = cst[:, C_IOTA:C_IOTA + k]
                    link(vec.tensor_reduce(col(m), src, AX, ALU.max))
                    link(vec.tensor_tensor(rt[:, 0:nt, one:one + k], src, bc(m, k), ALU.is_equal))
                    link(vec.tensor_tensor(rt[:, 0:nt, one:one + k], rt[:, 0:nt, one:one + k],
                                           iota.unsqueeze(1).to_broadcast([P, nt, k]), ALU.mult))
                    link(vec.tensor_reduce(col(99), rt[:, 0:nt, one:one + k], AX, ALU.max))
                    link(vec.tensor_tensor(rt[:, 0:nt, one:one + k], rt[:, 0:nt, one:one + k], bc(99, k), ALU.is_equal))

                first_max(lg[:, 0:nt, 0:4], 4, 96, 8)
                vec.tensor_tensor(rt[:, 0:nt, 0:4], lg[:, 0:nt, 0:4], bc(96, 4), ALU.subtract).then_inc(s_rexp, 1)
                for t in range(nt):
                    prod = rt[:, t, 64:96].rearrange("p (g e) -> p g e", g=4)
                    one = rt[:, t, 8:12].unsqueeze(2).to_broadcast([P, 4, 8])
                    ins = vec.tensor_tensor(prod, lg[:, t, 4:36].rearrange("p (g e) -> p g e", g=4), one, ALU.mult)
                link(ins)
                for t in range(nt):
                    ins = vec.tensor_reduce(rt[:, t, 24:32], rt[:, t, 64:96].rearrange("p (g e) -> p e g", g=4), AX, ALU.add)
                link(ins)
                first_max(rt[:, 0:nt, 24:32], 8, 97, 40)
                link(vec.scalar_tensor_tensor(rt[:, 0:nt, 32:40], rt[:, 0:nt, 40:48], NEG, rt[:, 0:nt, 24:32], ALU.mult, ALU.add))
                first_max(rt[:, 0:nt, 32:40], 8, 98, 48)
                vec.tensor_tensor(col(100), col(98), col(97), ALU.subtract).then_inc(s_rexp, 1)
                for a in range(2):
                    for t in range(nt):
                        ins = vec.tensor_tensor(oh[a][:, t, :].rearrange("p (g e) -> p g e", g=4),
                                                rt[:, t, 8:12].unsqueeze(2).to_broadcast([P, 4, 8]),
                                                rt[:, t, 40 + 8 * a:48 + 8 * a].unsqueeze(1).to_broadcast([P, 4, 8]), ALU.mult)
                link(ins)
                vec.tensor_tensor(oh[2][:, 0:nt, :], oh[0][:, 0:nt, :], oh[1][:, 0:nt, :], ALU.add).then_inc(s_mask, 1)
                dve.wait_ge(s_cnt, l + 1)
                link(vec.tensor_copy(nch[0:NE, 0:1], bank[5][0:NE, 0:1]))
                link(vec.tensor_tensor(rt[0:NE, 0, 56:64], cst[0:NE, C_THR:C_THR + 8], nch[0:NE, 0:1].to_broadcast([NE, 8]), ALU.is_lt))
                link(vec.tensor_reduce(nch[0:NE, 1:2], rt[0:NE, 0, 56:64], AX, ALU.add))
                vec.tensor_scalar(nrep[0:NE, :], ones[0:NE, :], nch[0:NE, 1:2], None, ALU.mult).then_inc(s_nch, 1)
                dve.wait_ge(s_pos, l + 1)
                src = bank[6][:, 0:NE * nt].rearrange("p (t e) -> p t e", t=nt)
                for a in range(2):
                    ins = vec.tensor_tensor(oh[a][:, 0:nt, :], oh[a][:, 0:nt, :], src, ALU.mult)
                link(ins)
                for a in range(2):
                    ins = vec.tensor_reduce(posp[:, 0:nt, a:a + 1], oh[a][:, 0:nt, :], AX, ALU.add)
                link(ins)
                for a in range(2):
                    vec.tensor_copy(pos[:, l, 4 * a:4 * a + nt], posp[:, 0:nt, a])
                vec.tensor_copy(tab[:, l, :], bank[7][:, 0:65]).then_inc(s_tab, 1)

                dve.wait_ge(s_tab, l + 1)
                total = dve.value_load(tab[0:1, l, T_ALL:T_ALL + 1], min_val=NE, max_val=CHUNKS[l])

                def picks(chunk_done):
                    for t in range(nt):
                        ins = vec.tensor_scalar(pick2[:, t, :], cst[:, C_SLOT:C_SLOT + CH], prel[:, 4 + t:5 + t], None, ALU.is_equal)
                    ins.then_inc(s_prel[l], 1)
                    dve.wait_ge(s_prel[l], chunk_done * 2 + 1)
                    for t in range(nt):
                        ins = vec.scalar_tensor_tensor(pick[:, t, :], cst[:, C_SLOT:C_SLOT + CH], prel[:, t:t + 1], pick2[:, t, :],
                                                       ALU.is_equal, ALU.add)
                    ins.then_inc(s_pick[l], 1)
                    dve.wait_ge(s_pick[l], chunk_done + 1)
                    vec.tensor_scalar(prel[:, :], prel[:, :], float(-CH), None, ALU.add).then_inc(s_prel[l], 1)
                    dve.wait_ge(s_prel[l], chunk_done * 2 + 2)

                for a in range(2):
                    ins = vec.tensor_copy(prel[:, 4 * a:4 * a + nt], posp[:, 0:nt, a])
                    if nt < 4:
                        vec.memset(prel[:, 4 * a + nt:4 * a + 4], 0.0)
                link(ins)
                picks(0)
                dve.wait_ge(s_xt[l], 1)
                vec.tensor_copy(xcols[:, :, :].rearrange("p k c -> p (k c)"), bank[0][:, :]).then_inc(s_xc[l], 1)
                picks(1)
                with dve.Fori(0, total) as g:
                    dve.wait_ge(s_sg[l], g + 1)
                    vec.tensor_tensor(hid[:, :], sg[:, :], bank[1][:, P:2 * P], ALU.mult).then_inc(s_hid[l], 1)
                    dve.wait_ge(s_ht[l], g + 1)
                    vec.tensor_copy(hidT[:, :], bank[2][:, 0:P]).then_inc(s_hte[l], 1)
                    dve.wait_ge(s_xt[l], g + 2)
                    vec.tensor_copy(xcols[:, :, :].rearrange("p k c -> p (k c)"), bank[0][:, :]).then_inc(s_xc[l], 1)
                    picks(g + 2)
                    dve.wait_ge(s_dn[l], g + 1)
                    dve.wait_ge(s_yfree[l], g + 1)
                    vec.tensor_copy(yrows[:, :], bank[3][:, :]).then_inc(s_yev[l], 1)
                dve.wait_ge(s_rexpd, 2 * l + 2)
                link(vec.tensor_reduce(col(101), rt[:, 0:nt, 0:4], AX, ALU.add))
                link(vec.reciprocal(col(101), col(101)))
                link(vec.tensor_scalar(col(102), col(100), 1.0, None, ALU.add))
                link(vec.reciprocal(col(102), col(102)))
                link(vec.tensor_tensor(col(102), col(102), col(101), ALU.mult))
                link(vec.tensor_tensor(col(103), col(102), col(100), ALU.mult))
                for a in range(2):
                    ins = vec.tensor_copy(gate[:, l, 4 * a:4 * a + nt], rt[:, 0:nt, 102 + a])
                link(ins)
                for t in range(nt):
                    dve.wait_ge(s_gat[t], 32 * (l + 1))
                    link(vec.tensor_scalar(y1[:, t, :], y1[:, t, :], gate[:, l, t:t + 1], None, ALU.mult))
                    vec.scalar_tensor_tensor(y1[:, t, :], y2[:, t, :], gate[:, l, 4 + t:5 + t], y1[:, t, :], ALU.mult, ALU.add).then_inc(s_cmb[l], 1)
                layer_norm_dve(l, 1)

            for t in range(2):
                for j in range(4):
                    q = 4 * t + j
                    dve.wait_ge(s_ot, q + 1)
                    vec.tensor_copy(xin[:, t, 256 * j:256 * (j + 1)], bank[q % 2][:, 0:256]).then_inc(s_oe, 1)

        @block.tensor
        def _(pe):
            mm = nc.tensor.matmul
            pe.wait_ge(s_small, 48)
            for l in range(DEPTH):
                nc.tensor.transpose(bank[l][:, 0:P], vrow[:, l, :], ident).then_inc(s_vt, 1)
            pe.wait_ge(s_xin, 32)
            for k in range(KD):
                if k >= 2:
                    pe.wait_ge(s_xT, k - 1)
                for t in range(4):
                    ins = nc.tensor.transpose(bank[2 + k % 2][:, t * P:(t + 1) * P], xin[:, t, k * P:(k + 1) * P], ident)
                ins.then_inc(s_tp, 1)

            def arrived(i):
                s, n = arrival(i)
                pe.wait_ge(w_here[s], n)
                return slots[:, s, :]

            def modulation(l, c):
                w = arrived(INDEX["mod", l, c]).rearrange("p (k n) -> p k n", k=KD)
                if 8 * l + c >= 3:
                    pe.wait_ge(s_modT, 8 * l + c)
                elif c == 2:
                    pe.wait_ge(s_modT, 1)
                for k in range(KD):
                    for j in range(3):
                        ins = mm(mod_bank(8 * l + c)[32 * j:32 * (j + 1), 0:256], cT[:, k, :], w[:, k, 256 * j:256 * (j + 1)],
                                 start=(k == 0), stop=(k == KD - 1))
                ins.then_inc(s_mod, 1)

            def modulation_columns(l, c):
                pe.wait_ge(s_mrow, 8 * l + c + 1)
                for h in range(2):
                    ins = nc.tensor.transpose(mod_bank(8 * l + c)[:, 256 + 96 * h:256 + 96 * (h + 1)], mrow[:, h * P:(h + 1) * P],
                                              ident[0:96, 0:96])
                ins.then_inc(s_mtr, 1)

            def keep_warm(count, columns=512):
                for _ in range(count):
                    mm(bank[6][:, 0:columns], onesD[:, :], cst[:, 0:columns], start=True, stop=True)

            def mean_pe(l, w, m):
                pe.wait_ge(ln["z"], KD * (2 * l + w) + m + 1)
                return mm(bank[4][:, 0:TQ[l]], onesD[:, :], zT[:, m, 0:TQ[l]], start=(m == 0), stop=(m == KD - 1))

            def layer_norm_pe(l, w):
                i0 = 2 * l + w
                n = TQ[l]
                mean_pe(l, w, KD - 2)
                mean_pe(l, w, KD - 1).then_inc(ln["mean"], 1)
                for m in range(KD):
                    pe.wait_ge(ln["sq"], KD * i0 + m + 1)
                    mm(bank[5][:, 0:n], ones[:, :], sqr[:, m % 2, 0:n], start=(m == 0), stop=(m == KD - 1)).then_inc(ln["sqs"], 1)
                keep_warm(4 * n // TOK)
                for m in range(KD):
                    pe.wait_ge(ln["zn"], KD * i0 + m + 1)
                    keep_warm(1, n // 2)

            def projection(l, g, w):
                name, i = GROUPS[g]
                o = bank[g % PROJ_BANKS]
                n = width(l, name)

                def features(lhs, out, rhs_n):
                    for k in range(KD):
                        ins = mm(out, lhs(k), hT[:, k, 0:rhs_n], start=(k == 0), stop=(k == KD - 1))
                    return ins

                def tokens(c0, nc_, tiles):
                    for a, t in enumerate(tiles):
                        for k in range(KD):
                            ins = mm(o[:, a * nc_:(a + 1) * nc_], hT[:, k, t * P:(t + 1) * P], w[:, k, c0:c0 + nc_],
                                     start=(k == 0), stop=(k == KD - 1))
                    return ins

                if name == "qa":
                    return features(lambda k: w[:, k, 128 * i:128 * (i + 1)], o[:, 0:n], n)
                if name == "ka":
                    return features(lambda k: w[:, k, 256:384], o[:, :], n)
                if name == "va":
                    return tokens(384, P, range(4))
                if name in ("pq", "pkv"):
                    c0 = 128 * i if name == "pq" else 256
                    return features(lambda k: w[:, k, c0:c0 + 128], o[:, 0:n], n)
                if name == "kr":
                    return features(lambda k: w[:, k, 384:416], o[64:96, 0:n], n)
                if name in ("qd", "kd", "qn", "kn"):
                    c0 = (0 if name[0] == "q" else 256) + 128 * i
                    return features(lambda k: w[:, k, c0:c0 + 128], o[:, 0:n], n)
                if name in ("vd", "vn"):
                    return tokens(512, 256, (2 * i, 2 * i + 1))
                if name == "ssq":
                    mm(o[:, 0:n], ones[:, :], psq[:, 0, 0:n], start=True, stop=False)
                    return mm(o[:, 0:n], ones[:, :], psq[:, 1, 0:n], start=False, stop=True)
                if name == "sskv":
                    return mm(o[:, :], ones[:, :], psq[:, 2, :], start=True, stop=True)
                if name == "mk":
                    return mm(o[0:64, :], wukv[:, i * P:i * P + 64], praw[:, 2, :], start=True, stop=True)
                if name == "mv":
                    for a in range(2):
                        t = 2 * i + a
                        ins = mm(o[:, a * 256:(a + 1) * 256], praw[:, 2, t * P:(t + 1) * P],
                                 wukv[:, :].rearrange("p (h a c) -> p h a c", h=4, a=2)[:, :, 1, :], start=True, stop=True)
                    return ins
                mm(o[0:96, 0:n], wuq[:, 0, 96 * i:96 * (i + 1)], praw[:, 0, 0:n], start=True, stop=False)
                return mm(o[0:96, 0:n], wuq[:, 1, 96 * i:96 * (i + 1)], praw[:, 1, 0:n], start=False, stop=True)

            def permute(l, r):
                g = ROPES[r]
                name, i = GROUPS[g]
                lo, hi = (64, 96) if name in ("kr", "mq") else (0, 128)
                c = C_P16 if name in ("qa", "ka") else C_P8
                pe.wait_ge(s_eva[l], NACT[g])
                if r >= 2:
                    pe.wait_ge(s_rope[l], r - 1)
                mm(bank[4 + r % 2][lo:hi, 0:SEQ], cst[lo:hi, c + lo:c + hi], dest(name, i)[lo:hi, 0:SEQ],
                   start=True, stop=True).then_inc(s_perm[l], 1)

            pe.wait_ge(s_cT, 1)
            pe.wait_ge(s_ones, 1)
            for c in range(3):
                modulation(0, c)
                modulation_columns(0, c)

            for l in range(DEPTH):
                n = TQ[l]
                nt = n // P
                pe.wait_ge(s_h1a[l], KD)
                pe.wait_ge(s_h1d[l], KD)
                part = None
                done = 0
                for g, (name, i) in enumerate(GROUPS):
                    if PART_OF.get(name) is not None and PART_OF[name] != part:
                        part = PART_OF[name]
                        w = arrived(INDEX["in", l, part])[:, 0:KD * IN_PARTS[part][1]].rearrange("p (k n) -> p k n", k=KD)
                    if g >= PROJ_BANKS:
                        old = g - PROJ_BANKS
                        if GROUPS[old][0] in BY_ACT:
                            pe.wait_ge(s_eva[l], NACT[old])
                        else:
                            pe.wait_ge(s_evd[l], NDVE[old])
                    if name == "ssq":
                        pe.wait_ge(s_psq[l], 3)
                    if (name, i) == ("mq", 0):
                        pe.wait_ge(s_wqkv[l], 48 if l == 0 else 32)
                        pe.wait_ge(s_pn[l], 3)
                    projection(l, g, w).then_inc(s_grp[l], 1)
                    while done < len(ROPES) and ROPES[done] + 2 <= g:
                        permute(l, done)
                        done += 1
                while done < len(ROPES):
                    permute(l, done)
                    done += 1

                uf = first[l]
                mods = [(0, c) for c in range(3, 8)] + [(1, c) for c in range(8)] if l == 0 else []
                last = len(GROUPS) - PROJ_BANKS
                pe.wait_ge(s_rope[l], ROPES.index(GI[("kd", 1)]) + 1)
                for v in range(len(units[l]) + 4):
                    if v < len(units[l]):
                        mixer, h, qt, k0 = units[l][v]
                        q = slice(qt * P, (qt + 1) * P)
                        for u in range(uf[v], uf[v + 1]):
                            if u >= 3:
                                pe.wait_ge(s_exp[l], u - 2)
                            else:
                                pe.wait_ge(s_evd[l], NDVE[last + (u - last) % PROJ_BANKS])
                            if mixer == "a":
                                lo, k = 64 * (h // 2), 64
                                qs, ks = QA[lo:lo + k, h % 2, q], KA[lo:lo + k, k0 * P:TOK]
                            elif mixer == "b":
                                qs, ks = QM[0:96, h, q], KM[0:96, h, k0 * P:TOK]
                            elif mixer == "c":
                                lo, k = 64 * (h % 2) + 32 * (u - uf[v]), 32
                                qs, ks = QDf[lo:lo + k, h // 2, q], KDf[lo:lo + k, h // 2, k0 * P:TOK]
                            else:
                                lo, k = 64 * (h % 2), 64
                                qs, ks = QN[lo:lo + k, h // 2, q], KN[lo:lo + k, h // 2, k0 * P:TOK]
                            more = mixer in "ad" and k0 == 0
                            ins = mm(bank[u % 3][:, k0 * P:TOK], qs, ks, start=True, stop=not more)
                            if more:
                                if mixer == "a":
                                    extra = cst[:, C_SWA + SEQ * qt:C_SWA + SEQ * (qt + 1)]
                                else:
                                    pe.wait_ge(s_biasm[l], 4)
                                    extra = biasm[:, h, qt, :]
                                ins = mm(bank[u % 3][:, 0:SEQ], ident, extra, start=False, stop=True)
                            ins.then_inc(s_S[l], 1)
                    if 2 <= v < len(units[l]) + 2:
                        t = v - 2
                        k0 = units[l][t][3]
                        if t == 0:
                            pe.wait_ge(s_evd[l], NDVE[-1])
                            pe.wait_ge(s_eva[l], NACT[-1])
                            pe.wait_ge(s_rope[l], len(ROPES))
                        pe.wait_ge(s_norm[l], uf[t + 1])
                        if t >= 2:
                            pe.wait_ge(s_PT[l], t - 1)
                        for kt in range(k0, 4):
                            ins = nc.tensor.transpose(bank[3 + t % 2][:, kt * P:(kt + 1) * P], Pr[:, uf[t] % 4, kt * P:(kt + 1) * P], ident)
                        ins.then_inc(s_T[l], 1)
                    if v >= 4 and v % 2 == 0:
                        p = (v - 4) // 2
                        mixer, h, qt, k0 = units[l][2 * p]
                        pe.wait_ge(s_PT[l], 2 * p + 2)
                        if p >= 2:
                            pe.wait_ge(s_att[l], p - 1)
                        for kt in range(k0, 4):
                            for i in range(2):
                                c0 = VOFF[mixer] + 64 * (h // 2 if mixer == "a" else h + i)
                                ins = mm(bank[5 + p % 2][64 * i:64 * (i + 1), 0:P], V[:, kt, c0:c0 + 64],
                                         PTs[:, (2 * p + i) % 3, kt * P:(kt + 1) * P], start=(kt == k0), stop=(kt == 3))
                        ins.then_inc(s_O[l], 1)
                    if mods and v % 4 == 3:
                        modulation(*mods[0])
                    if mods and v % 4 == 0 and v:
                        modulation_columns(*mods.pop(0))
                    step = v - (len(units[l]) - 8)
                    if step in (1, 4):
                        j = step // 4
                        pe.wait_ge(s_csq, 2 * l + j + 1)
                        if j == 0:
                            pe.wait_ge(s_modT, 16)
                        else:
                            pe.wait_ge(s_cstd, 3 * l + 1)
                        mm(bank[7][:, 0:n], cst[:, C_BLK:C_BLK + P], sqr[:, j, 0:n], start=True, stop=True).then_inc(s_css, 1)
                pe.wait_ge(s_att[l], 3 * len(units[l]) // 8)
                for m in range(KD):
                    w = arrived(INDEX["out", l, m // 4])[:, 0:KD * 512].rearrange("p (k n) -> p k n", k=KD)
                    if m >= 4:
                        pe.wait_ge(s_yg[l], m - 3)
                    for k in (0, 1, 2, 3, 4, 6, 7, 5):
                        if m == 0 and k in (4, 5):
                            pe.wait_ge(s_cn, 2 * l + k - 3)
                        if m == 0 and k == 6:
                            pe.wait_ge(s_att[l], len(units[l]) // 2)
                        ins = mm(bank[m % 4][:, 0:n], w[:, k, (m % 4) * P:(m % 4 + 1) * P], attnT[:, k, 0:n],
                                 start=(k == 0), stop=(k == 5))
                    ins.then_inc(s_y[l], 1)
                    if m >= 2:
                        mean_pe(l, 0, m - 2)
                layer_norm_pe(l, 0)
                for k in range(KD):
                    pe.wait_ge(s_h2d[l], k + 1)
                    if n > SEQ:
                        pe.wait_ge(s_h2p[l], k + 1)
                    for t in range(nt):
                        ins = mm(bank[4 + t][:, 0:36], hT[:, k, t * P:(t + 1) * P], wr[:, l, k, :], start=(k == 0), stop=(k == KD - 1))
                ins.then_inc(s_lg[l], 1)
                for q in range(2 * nt):
                    if q >= 4:
                        pe.wait_ge(s_toke[l], q - 3)
                    for a in range(4):
                        ins = nc.tensor.transpose(bank[q % 4][:, a * P:(a + 1) * P], hT[:, 4 * (q % 2) + a, (q // 2) * P:(q // 2 + 1) * P], ident)
                    ins.then_inc(s_tok[l], 1)
                pe.wait_ge(s_mask, l + 1)
                for t in range(nt):
                    ins = mm(bank[5][0:NE, 0:P], oh[2][:, t, :], ones[:, :], start=(t == 0), stop=(t == nt - 1))
                ins.then_inc(s_cnt, 1)
                keep_warm(1)
                pe.wait_ge(s_nch, l + 1)
                o = bank[6][:, 0:NE * nt].rearrange("p (t e) -> p t e", t=nt)
                mm(o, cst[:, C_UP:C_UP + P], oh[2][:, 0:nt, :], start=True, stop=False)
                for b in range(nt - 1):
                    mm(o[:, b + 1:nt, :], ones[:, :], oh[2][:, b, :].unsqueeze(1).to_broadcast([P, nt - 1 - b, NE]), start=False, stop=False)
                mm(o, nrep[0:NE, :], cst[0:NE, C_UP64:C_UP64 + NE].unsqueeze(1).to_broadcast([NE, nt, NE]), start=False, stop=True)
                mm(bank[7][:, 0:65], nrep[0:NE, :], cst[0:NE, C_UPX:C_UPX + 65], start=True, stop=True).then_inc(s_pos, 1)

                def columns(k0, k1):
                    for k in range(k0, k1):
                        for t in range(nt):
                            for i in range(3):
                                ins = mm(bank[0][:, k * CH:(k + 1) * CH], hparts[:, i, t, k * P:(k + 1) * P], pick[:, t, :],
                                         start=(t == 0 and i == 0), stop=(t == nt - 1 and i == 2))
                    return ins

                def expert(e, here, w, wd):
                    first_g = pe.value_load(tab[0:1, l, bass.ds(e + T_FIRST, 1)], min_val=0, max_val=CHUNKS[l])
                    count = pe.value_load(tab[0:1, l, bass.ds(e + T_N, 1)], min_val=1, max_val=1 + 2 * TOK // CH)
                    with pe.Fori(0, count) as j:
                        g = first_g + j
                        for s, value in here:
                            pe.wait_ge(s, value)
                        pe.wait_ge(s_xc[l], g + 1)
                        for k in range(KD):
                            for f in range(2):
                                ins = mm(bank[1][f * CH:(f + 1) * CH, 0:2 * P].rearrange("p (a f) -> p a f", a=2), xcols[:, k, :],
                                         w.rearrange("p (a k f) -> p a k f", a=2, k=KD)[:, :, k, f * P:(f + 1) * P],
                                         start=(k == 0), stop=(k == KD - 1))
                        ins.then_inc(s_hg[l], 1)
                        pe.wait_ge(s_pick[l], g + 2)
                        columns(0, 6)
                        pe.wait_ge(s_hid[l], g + 1)
                        nc.tensor.transpose(bank[2][:, 0:P], hid[:, :], ident).then_inc(s_ht[l], 1)
                        columns(6, KD).then_inc(s_xt[l], 1)
                        pe.wait_ge(s_hte[l], g + 1)
                        for f in range(2):
                            for c in range(2):
                                ins = mm(bank[3][c * CH:(c + 1) * CH, :], hidT[:, f * CH:(f + 1) * CH], wd[:, f * D + c * 512:f * D + (c + 1) * 512],
                                         start=(f == 0), stop=(f == 1))
                        ins.then_inc(s_dn[l], 1)

                pe.wait_ge(s_tab, l + 1)
                keep_warm(3 * nt // 2)
                pe.wait_ge(s_pch, split_done(l, 2 * nt - 1))
                pe.wait_ge(s_pick[l], 1)
                columns(0, KD).then_inc(s_xt[l], 1)
                keep_warm(1)

                def in_slot(e, n, r0=None):
                    slot, all_here = arrival(n)
                    here = [(w_here[slot], all_here), (g_here[slot], gate_arrival(n))]
                    if r0 is not None:
                        here = [(w_here[slot], r0 * (16 * DMAS["exp"]) + all_here), (g_here[slot], r0 * 16 + gate_arrival(n))]
                    expert(e, here, slots[:, slot, 0:4096], slots[:, slot, 4096:6144])

                for e in range(EXTRA):
                    in_slot(e, INDEX["exp", l, e])
                expert(EXTRA, [(x_here, 32 * (l + 1)), (x_down, 16 * (l + 1))], extra_in, extra_down)
                e1 = EXTRA + 1
                rounds = (NE - e1) // SLOTS
                with pe.Fori(0, rounds) as r0:
                    for a in range(SLOTS):
                        in_slot(r0 * SLOTS + (e1 + a), INDEX["exp", l, e1 + a], r0)
                for e in range(e1 + SLOTS * rounds, NE):
                    in_slot(e, INDEX["exp", l, e])
                for h in range(n // SEQ):
                    pe.wait_ge(s_cmb[l], 2 * (h + 1))
                    for m in range(KD):
                        q = KD * h + m
                        if q >= 4:
                            pe.wait_ge(s_yh[l], q - 3)
                        for a in range(2):
                            ins = nc.tensor.transpose(bank[q % 4][:, a * P:(a + 1) * P], y1[:, 2 * h + a, m * P:(m + 1) * P], ident)
                        ins.then_inc(s_yt[l], 1)
                        if h == n // SEQ - 1 and m >= 2:
                            mean_pe(l, 1, m - 2)
                layer_norm_pe(l, 1)
            pe.wait_ge(ln["x"], KD * 2 * DEPTH)
            for q in range(8):
                if q >= 2:
                    pe.wait_ge(s_oe, q - 1)
                t, j = q // 4, q % 4
                for a in range(2):
                    ins = nc.tensor.transpose(bank[q % 2][:, a * P:(a + 1) * P], xT[:, 2 * j + a, t * P:(t + 1) * P], ident)
                ins.then_inc(s_ot, 1)


def shape_constants():
    import numpy as np
    c = np.zeros((P, C_ALL), np.float32)
    p = np.arange(P)
    c[p, C_ID + p] = 1
    c[p, C_P16 + (p ^ 16)] = 1
    c[p, C_P8 + (p ^ 8)] = 1
    c[:, C_BLK:C_BLK + P] = (p[:, None] // 64 == p[None] // 64) / 64.0
    t = np.arange(SEQ)
    for width, o_cos, o_sin in ((64, C_COS64, C_SIN64), (32, C_COS32, C_SIN32)):
        r, half = width // 2, width // 4
        inv = (np.float32(10000.0) ** (-np.arange(half, dtype=np.float32) / np.float32(half))).astype(np.float32)
        d = p % width
        pos = np.where((d < r)[:, None], (t // GRID_W)[None], (t % GRID_W)[None]).astype(np.float32)
        ang = pos * inv[d % half][:, None]
        c[:, o_cos:o_cos + SEQ] = np.cos(ang)
        c[:, o_sin:o_sin + SEQ] = np.sin(ang) * np.where(d % r < half, -1.0, 1.0)[:, None]
    q = np.arange(SEQ).reshape(2, P).T[:, :, None]
    k = t[None, None, :]
    c[:, C_SWA:C_SWA + 512] = np.where(np.abs(k - q) <= 128, 0, NEG).reshape(P, 512)
    start = np.clip(q % GRID_W - 8, 0, GRID_W - 16)
    c[:, C_NA:C_NA + 512] = np.where((k % GRID_W >= start) & (k % GRID_W < start + 16), 0, NEG).reshape(P, 512)
    c[:, C_IOTA:C_IOTA + 16] = 16 - np.arange(16)
    c[:, C_UP:C_UP + P] = p[:, None] < p[None]
    e = np.arange(NE)
    c[0:NE, C_UPX:C_UPX + NE + 1] = e[:, None] < np.arange(NE + 1)[None]
    c[0:NE, C_UPX + T_N:C_UPX + T_N + NE] = np.eye(NE)
    c[0:NE, C_UP64:C_UP64 + NE] = CH * (e[:, None] < e[None])
    c[:, C_THR:C_THR + 8] = [-1] + [CH * a for a in range(1, 8)]
    c[:, C_SLOT:C_SLOT + CH] = np.arange(CH)
    return c


def kernel(**inputs):
    import numpy as np
    import concourse.bacc as bacc
    from concourse.bass_utils import run_bass_kernel_spmd

    a = {k: np.asarray(v) for k, v in inputs.items()}
    def r128(v):
        return v.reshape(DEPTH, -1, P)
    both = np.stack([np.concatenate([a["c"].reshape(KD, P), a["c_ctx"].reshape(KD, P)])] * DEPTH)
    sub = np.concatenate([a["diff_subln"], a["diff_subln"]], -1).reshape(DEPTH, 1, P)
    vecs = np.concatenate([r128(a["b_mod"]), r128(a["ln1_g"]), r128(a["ln1_b"]), r128(a["ln2_g"]), r128(a["ln2_b"]),
                           r128(a["mla_q_norm"]), r128(a["mla_kv_norm"]), sub, both, np.zeros((DEPTH, P - 100, P), np.float32)], 1)
    rows = np.concatenate([a["attn_sink"], a["lam_q1"], a["lam_k1"], a["lam_q2"], a["lam_k2"], a["b_group"], a["b_router"]], -1)
    rows = np.ascontiguousarray(np.broadcast_to(rows[:, None, :], (DEPTH, P, R_ALL)))
    w = a["w_in"]
    w_in = np.concatenate([w[:, :, 0:64], w[:, :, 128:192], w[:, :, 64:128], w[:, :, 192:]], -1)
    t = np.arange(SEQ)
    row_off = (t[None] // GRID_W) - (t[:, None] // GRID_W) + 7
    col_off = np.clip((t[None] % GRID_W) - (t[:, None] % GRID_W) + 15, 0, 30)
    bias = a["na_rpb"][:, :, row_off, col_off]
    ins = {
        "x": a["x"], "ctx": a["ctx"], "w_mod": a["w_mod"], "w_in": w_in, "w_uq": a["w_uq"], "w_ukv": a["w_ukv"],
        "w_out": a["w_out"], "w_route": np.concatenate([a["w_group"], a["w_router"]], -1),
        "w_gate": a["w_gate"], "w_up": a["w_up"], "w_down": a["w_down"],
        "vecs": vecs, "rows": rows, "bias_na": bias, "consts": shape_constants(),
    }
    nc = bacc.Bacc("TRN2", target_bir_lowering=False, num_devices=1)
    arrays, args = {}, []
    for name, v in ins.items():
        v = np.ascontiguousarray(v)
        arrays[f"in_{name}"] = v
        args.append(nc.dram_tensor(f"in_{name}", v.shape, mybir.dt.from_np(v.dtype), kind="ExternalInput").ap())
    args.append(nc.dram_tensor("out_0", (1, SEQ, D), F32, kind="ExternalOutput").ap())
    build(nc, *args)
    r = run_bass_kernel_spmd(nc, [arrays], core_ids=[0])
    return r.results[0]["out_0"]
```
